# Optimizing a Trainium2 kernel written in Bass

```python
import math
import jax, jax.numpy as jnp
from jax import lax
import numpy as np

D_MODEL = 1024
BATCH = 1
SEQ = 512
DEPTH = 1
DEC_BATCH = 1
DEC_SEQ = 512
PAST_LEN = 128

N_META = 16
D_MIX = D_MODEL
RMS_EPS = 1e-6
DA_HEADS = 4
DA_WIDTH = D_MIX // 2
DA_V_DIM = DA_WIDTH // DA_HEADS
DA_QK_DIM = DA_V_DIM // 2
ROPE_DIM = DA_QK_DIM // 4
ROPE_THETA = 500000.0
Q_BLOCK = 128
ML_WIDTH = D_MIX - DA_WIDTH
ML_HEADS = 4
ML_HEAD_DIM = ML_WIDTH // ML_HEADS
CHUNK = 64
CONV_W = 3
NEG_BIG = -1e30
OFF_DA_Q = 0
OFF_DA_K = OFF_DA_Q + DA_WIDTH
OFF_DA_V = OFF_DA_K + DA_WIDTH
OFF_ML_QK = OFF_DA_V + DA_WIDTH
OFF_ML_V = OFF_ML_QK + 2 * ML_WIDTH
OFF_ML_O = OFF_ML_V + ML_WIDTH
OFF_GATES = OFF_ML_O + ML_WIDTH
N_GATES = 4 * ML_HEADS
D_IN = OFF_GATES + N_GATES
N_EXPERTS = 16
CAP_FACTOR = 2
D_FF_EXPERT = 2816

kernel_name = "hymba_diffattn_mlstm_ec_encoder"

def _rmsnorm(x, g):
    xf = x.astype(jnp.float32)
    y = xf * lax.rsqrt(jnp.mean(xf * xf, axis=-1, keepdims=True) + RMS_EPS)
    return (y * g.astype(jnp.float32)).astype(x.dtype)

def _lambda_init(layer_idx):
    return 0.8 - 0.6 * math.exp(-0.3 * layer_idx)

def _rope_tables(L):
    pos = jnp.arange(L, dtype=jnp.float32)
    inv = ROPE_THETA ** (-jnp.arange(0, ROPE_DIM, 2, dtype=jnp.float32) / ROPE_DIM)
    ang = pos[:, None] * inv[None, :]
    return jnp.cos(ang), jnp.sin(ang)

def _partial_rope(x, cos, sin):
    half = ROPE_DIM // 2
    x1 = x[..., :half]
    x2 = x[..., half:ROPE_DIM]
    c = cos.astype(x.dtype)
    s = sin.astype(x.dtype)
    rot = jnp.concatenate([x1 * c - x2 * s, x2 * c + x1 * s], axis=-1)
    return jnp.concatenate([rot, x[..., ROPE_DIM:]], axis=-1)

def _diff_attention(q, k, v, lam):
    B, H, _, L, dq = q.shape
    nb = -(-L // Q_BLOCK)
    Lq = nb * Q_BLOCK
    qp = jnp.pad(q, ((0, 0), (0, 0), (0, 0), (0, Lq - L), (0, 0)))
    qb = jnp.moveaxis(qp.reshape(B, H, 2, nb, Q_BLOCK, dq), 3, 0)

    def block(qblk):
        s = jnp.einsum('bhjqd,bhjkd->bhjqk', qblk, k).astype(jnp.float32)
        p = jax.nn.softmax(s, axis=-1)
        a = p[:, :, 0] - lam * p[:, :, 1]
        return jnp.einsum('bhqk,bhkd->bhqd', a.astype(v.dtype), v)

    out = lax.map(block, qb)
    out = jnp.moveaxis(out, 0, 2).reshape(B, H, Lq, v.shape[-1])
    return out[:, :, :L]

def _mlstm_chunk_scan(q, k, v, log_i, log_f):
    B, H, T, dk = q.shape
    dv = v.shape[-1]
    nc = T // CHUNK

    def to_chunks(a):
        return jnp.moveaxis(a.reshape(a.shape[:2] + (nc, CHUNK) + a.shape[3:]), 2, 0)

    mask = jnp.tril(jnp.ones((CHUNK, CHUNK), dtype=bool))

    def step(carry, inp):
        C, n, m = carry
        qc, kc, vc, li, lf = inp
        b = jnp.cumsum(lf, axis=-1)
        Dm = jnp.where(mask, b[..., :, None] - b[..., None, :] + li[..., None, :], -jnp.inf)
        inter = b + m[..., None]
        m_t = jnp.maximum(jnp.max(Dm, axis=-1), inter)
        W = jnp.exp(Dm - m_t[..., None])
        g = jnp.exp(inter - m_t)
        S = jnp.einsum('bhtd,bhsd->bhts', qc, kc) * W
        num = jnp.einsum('bhts,bhsd->bhtd', S, vc) + g[..., None] * jnp.einsum('bhtd,bhde->bhte', qc, C)
        den = jnp.sum(S, axis=-1) + g * jnp.einsum('bhtd,bhd->bht', qc, n)
        h = num / jnp.maximum(jnp.abs(den), jnp.exp(-m_t))[..., None]
        bL = b[..., -1]
        a = bL[..., None] - b + li
        m_new = jnp.maximum(bL + m, jnp.max(a, axis=-1))
        wa = jnp.exp(a - m_new[..., None])
        gd = jnp.exp(bL + m - m_new)
        C_new = gd[..., None, None] * C + jnp.einsum('bhs,bhsd,bhse->bhde', wa, kc, vc)
        n_new = gd[..., None] * n + jnp.einsum('bhs,bhsd->bhd', wa, kc)
        return (C_new, n_new, m_new), h

    init = (jnp.zeros((B, H, dk, dv), jnp.float32),
            jnp.zeros((B, H, dk), jnp.float32),
            jnp.zeros((B, H), jnp.float32))
    _, hs = lax.scan(step, init, (to_chunks(q), to_chunks(k), to_chunks(v),
                                  to_chunks(log_i), to_chunks(log_f)))
    return jnp.moveaxis(hs, 0, 2).reshape(B, H, T, dv)

def _bidir_mlstm(q, k, v, i_fw, f_fw, i_bw, f_bw):
    pad = (-N_META) % CHUNK
    pw3 = ((0, 0), (0, 0), (pad, 0))
    pw4 = pw3 + ((0, 0),)
    qp, kp, vp = jnp.pad(q, pw4), jnp.pad(k, pw4), jnp.pad(v, pw4)
    li_fw = jnp.pad(i_fw, pw3, constant_values=NEG_BIG)
    lf_fw = jnp.pad(jax.nn.log_sigmoid(f_fw), pw3)
    li_bw = jnp.pad(i_bw, pw3, constant_values=NEG_BIG)
    lf_bw = jnp.pad(jax.nn.log_sigmoid(f_bw), pw3)
    flip = lambda a: jnp.flip(a, axis=2)
    h_fw = _mlstm_chunk_scan(qp, kp, vp, li_fw, lf_fw)
    h_bw = flip(_mlstm_chunk_scan(flip(qp), flip(kp), flip(vp), flip(li_bw), flip(lf_bw)))
    return (h_fw + h_bw)[:, :, pad:]

def _centred_conv(x, w):
    L = x.shape[1]
    r = CONV_W // 2
    xp = jnp.pad(x, ((0, 0), (r, r), (0, 0)))
    y = xp[:, 0:L] * w[0]
    for j in range(1, CONV_W):
        y = y + xp[:, j:j + L] * w[j]
    return y

def _expert_choice_moe(h, w_router, w_gate, w_up, w_down):
    B, L, D = h.shape
    T = B * L
    xt = h.reshape(T, D)
    aff = jax.nn.softmax((xt @ w_router).astype(jnp.float32), axis=-1)
    cap = max(1, CAP_FACTOR * T // N_EXPERTS)
    gate, idx = lax.top_k(aff.T, cap)

    def expert(args):
        ids, wg, wu, wd = args
        xg = xt[ids]
        return (jax.nn.silu(xg @ wg) * (xg @ wu)) @ wd

    ye = lax.map(expert, (idx, w_gate, w_up, w_down))
    ye = ye * gate[..., None].astype(ye.dtype)
    y = jnp.zeros((T, D), h.dtype).at[idx.reshape(-1)].add(ye.reshape(-1, D))
    return y.reshape(B, L, D)

def _layer(x, cos, sin, lam_init, g_mix, w_in, b_gates, conv_w, g_q, g_k, lam_q1, lam_k1, lam_q2, lam_k2,
           g_da_out, g_ml_out, w_out, g_ffn, w_router, w_gate, w_up, w_down):
    B, L, _ = x.shape
    h = _rmsnorm(x, g_mix)
    z = h @ w_in

    dq = z[..., OFF_DA_Q:OFF_DA_K].reshape(B, L, DA_HEADS, 2, DA_QK_DIM)
    dk = z[..., OFF_DA_K:OFF_DA_V].reshape(B, L, DA_HEADS, 2, DA_QK_DIM)
    dv = z[..., OFF_DA_V:OFF_ML_QK].reshape(B, L, DA_HEADS, DA_V_DIM)
    dq = _rmsnorm(dq, g_q).transpose(0, 2, 3, 1, 4)
    dk = _rmsnorm(dk, g_k).transpose(0, 2, 3, 1, 4)
    dq = _partial_rope(dq, cos, sin) * (DA_QK_DIM ** -0.5)
    dk = _partial_rope(dk, cos, sin)
    dv = dv.transpose(0, 2, 1, 3)
    f32 = jnp.float32
    lam = (jnp.exp(jnp.sum(lam_q1.astype(f32) * lam_k1.astype(f32)))
           - jnp.exp(jnp.sum(lam_q2.astype(f32) * lam_k2.astype(f32))) + lam_init)
    oa = _diff_attention(dq, dk, dv, lam)
    oa = _rmsnorm(oa, g_da_out) * (1.0 - lam_init)
    oa = oa.transpose(0, 2, 1, 3).reshape(B, L, DA_WIDTH)

    mqk = jax.nn.silu(_centred_conv(z[..., OFF_ML_QK:OFF_ML_V], conv_w))
    mq = mqk[..., :ML_WIDTH].reshape(B, L, ML_HEADS, ML_HEAD_DIM).transpose(0, 2, 1, 3).astype(f32)
    mk = mqk[..., ML_WIDTH:].reshape(B, L, ML_HEADS, ML_HEAD_DIM).transpose(0, 2, 1, 3).astype(f32)
    mv = z[..., OFF_ML_V:OFF_ML_O].reshape(B, L, ML_HEADS, ML_HEAD_DIM).transpose(0, 2, 1, 3).astype(f32)
    mo = z[..., OFF_ML_O:OFF_GATES]
    gates = (z[..., OFF_GATES:] + b_gates).astype(f32).reshape(B, L, 4, ML_HEADS).transpose(2, 0, 3, 1)
    hm = _bidir_mlstm(mq * (ML_HEAD_DIM ** -0.5), mk, mv, gates[0], gates[1], gates[2], gates[3])
    hm = _rmsnorm(hm, g_ml_out)
    hm = hm.transpose(0, 2, 1, 3).reshape(B, L, ML_WIDTH).astype(x.dtype) * jax.nn.sigmoid(mo)

    x = x + jnp.concatenate([oa, hm], axis=-1) @ w_out
    x = x + _expert_choice_moe(_rmsnorm(x, g_ffn), w_router, w_gate, w_up, w_down)
    return x

def _trunk(x, meta, g_mix, w_in, b_gates, conv_w, g_q, g_k, lam_q1, lam_k1, lam_q2, lam_k2,
           g_da_out, g_ml_out, w_out, g_ffn, w_router, w_gate, w_up, w_down):
    B = x.shape[0]
    m = jnp.broadcast_to(meta.astype(x.dtype)[None], (B, N_META, x.shape[-1]))
    h = jnp.concatenate([m, x], axis=1)
    cos, sin = _rope_tables(h.shape[1])
    for l in range(DEPTH):
        h = _layer(h, cos, sin, _lambda_init(l), g_mix[l], w_in[l], b_gates[l], conv_w[l], g_q[l], g_k[l],
                   lam_q1[l], lam_k1[l], lam_q2[l], lam_k2[l], g_da_out[l], g_ml_out[l], w_out[l],
                   g_ffn[l], w_router[l], w_gate[l], w_up[l], w_down[l])
    return h[:, N_META:]

def setup_inputs(seed: int = 0) -> dict:
    key = jax.random.key(seed)
    ks = jax.random.split(key, 24)
    nrm = lambda k, s: jax.random.normal(k, s, jnp.float32)
    bi = 0.1 * nrm(ks[5], (DEPTH, 2, ML_HEADS))
    bf = jnp.linspace(3.0, 6.0, ML_HEADS, dtype=jnp.float32)[None, None] + 0.1 * nrm(ks[6], (DEPTH, 2, ML_HEADS))
    b_gates = jnp.concatenate([bi[:, 0], bf[:, 0], bi[:, 1], bf[:, 1]], axis=-1)
    return {
        "x_prompt": nrm(ks[0], (BATCH, SEQ, D_MODEL)),
        "x_sample": nrm(ks[1], (DEC_BATCH, DEC_SEQ, D_MODEL)),
        "meta": nrm(ks[2], (N_META, D_MODEL)),
        "g_mix": 1.0 + 0.1 * nrm(ks[3], (DEPTH, D_MODEL)),
        "w_in": nrm(ks[4], (DEPTH, D_MODEL, D_IN)) * D_MODEL ** -0.5,
        "b_gates": b_gates,
        "conv_w": nrm(ks[7], (DEPTH, CONV_W, 2 * ML_WIDTH)) * CONV_W ** -0.5,
        "g_q": 1.0 + 0.1 * nrm(ks[8], (DEPTH, DA_QK_DIM)),
        "g_k": 1.0 + 0.1 * nrm(ks[9], (DEPTH, DA_QK_DIM)),
        "lam_q1": 0.1 * nrm(ks[10], (DEPTH, DA_QK_DIM)),
        "lam_k1": 0.1 * nrm(ks[11], (DEPTH, DA_QK_DIM)),
        "lam_q2": 0.1 * nrm(ks[12], (DEPTH, DA_QK_DIM)),
        "lam_k2": 0.1 * nrm(ks[13], (DEPTH, DA_QK_DIM)),
        "g_da_out": 1.0 + 0.1 * nrm(ks[14], (DEPTH, DA_V_DIM)),
        "g_ml_out": 1.0 + 0.1 * nrm(ks[15], (DEPTH, ML_HEAD_DIM)),
        "w_out": nrm(ks[16], (DEPTH, D_MIX, D_MODEL)) * D_MIX ** -0.5,
        "g_ffn": 1.0 + 0.1 * nrm(ks[17], (DEPTH, D_MODEL)),
        "w_router": nrm(ks[18], (DEPTH, D_MODEL, N_EXPERTS)) * D_MODEL ** -0.5,
        "w_gate": nrm(ks[19], (DEPTH, N_EXPERTS, D_MODEL, D_FF_EXPERT)) * D_MODEL ** -0.5,
        "w_up": nrm(ks[20], (DEPTH, N_EXPERTS, D_MODEL, D_FF_EXPERT)) * D_MODEL ** -0.5,
        "w_down": nrm(ks[21], (DEPTH, N_EXPERTS, D_FF_EXPERT, D_MODEL)) * D_FF_EXPERT ** -0.5,
    }

def reference(x_prompt, x_sample, meta, g_mix, w_in, b_gates, conv_w, g_q, g_k, lam_q1, lam_k1, lam_q2, lam_k2,
              g_da_out, g_ml_out, w_out, g_ffn, w_router, w_gate, w_up, w_down):
    weights = (g_mix, w_in, b_gates, conv_w, g_q, g_k, lam_q1, lam_k1, lam_q2, lam_k2,
               g_da_out, g_ml_out, w_out, g_ffn, w_router, w_gate, w_up, w_down)
    y_prompt = _trunk(x_prompt, meta, *weights)
    y_sample = _trunk(x_sample, meta, *weights)
    return (y_prompt, y_sample)


_drawn_inputs = setup_inputs


def setup_inputs(seed=0):
    import zlib

    import numpy as np

    out = dict(_drawn_inputs(seed))
    spreads = {}
    factors = {}
    for name, (base, spread) in spreads.items():
        noise = np.random.default_rng([zlib.crc32(name.encode()), seed]).standard_normal(out[name].shape)
        drawn = base * np.exp(spread * noise) if base else spread * noise
        out[name] = __import__('jax').numpy.asarray(drawn.astype(out[name].dtype))
    for name, factor in factors.items():
        out[name] = (out[name] * factor).astype(out[name].dtype)
    return out
```

```python
import math
from contextlib import ExitStack

import concourse.bass as bass
from concourse import mybir
from concourse.alu_op_type import AluOpType as ALU

F32 = mybir.dt.float32
U32 = mybir.dt.uint32
ACT = mybir.ActivationFunctionType
AX = mybir.AxisListType
P = 128

N_META = 16
SEQ = 512
G = 2
T = N_META + SEQ
TZ = N_META + G * SEQ
D = 1024
KD = D // P
HALF = D // 2
HEADS = 4
HD = HALF // HEADS
QD = HD // 2
ROPE = QD // 4
ROPE_THETA = 500000.0
EPS = 1e-6
LAM_INIT = 0.8 - 0.6 * math.exp(0.0)
NEG = -1e30
EXP_LN = "natural_log_exp_and_others"
N_EXP = 16
CAP = 2 * T // N_EXP
FF = 2816
D_IN = 3600
OFF_MQK, OFF_MV, OFF_MO, OFF_GATES = 3 * HALF, 5 * HALF, 6 * HALF, 7 * HALF

ZROWS = [N_META] + [P] * (G * SEQ // P)
ZCOL = [0] + [N_META + P * i for i in range(G * SEQ // P)]
NZ = len(ZROWS)
CROWS = [N_META] + [P] * (SEQ // P)
CCOL = [0] + [N_META + P * i for i in range(SEQ // P)]
NC5 = len(CROWS)
PT = 512 - N_META


def zc(g, c):
    return 0 if c == 0 else 1 + (SEQ // P) * g + c - 1


def mixcol(g, c):
    return N_META * g if c == 0 else 2 * N_META + SEQ * g + P * (c - 1)


A_HT = 0
A_W = A_HT + KD * G * T * 4
A_S = A_W + 2 * KD * 512 * 4
A_Q = A_S + 23744
A_V = A_Q + 2 * HEADS * TZ * 4
A_MO = A_V + NZ * HALF * 4
A_MV = A_MO + NZ * HALF * 4
A_QK = A_MV + (NZ * HEADS * (HD + 1) * 4 + 31) // 32 * 32
A_END = A_QK + 2 * HEADS * G * T * 4
SLOT = 2 * KD * 256 * 4 + 2 * D * 4
A_X = A_Q + 3 * SLOT
A_MOE = A_HT


class Map:

    def __init__(self, nc, base, at, end):
        self.nc, self.base, self.at, self.end = nc, base, at, end

    def __call__(self, name, shape, dt=F32):
        n = 4
        for s in shape[1:]:
            n *= s
        assert self.at + n <= self.end, (name, self.at + n, self.end)
        t = self.nc.alloc_sbuf_tensor_at(name, shape, dt, offset=self.base + self.at)
        self.at += (n + 31) // 32 * 32
        return t


def rope_tables(np):
    inv = ROPE_THETA ** (-np.arange(0, ROPE, 2, dtype=np.float32) / np.float32(ROPE))
    ang = np.arange(T, dtype=np.float32)[:, None] * inv.astype(np.float32)[None, :]
    cos, sin = (np.zeros((P, NC5, ROPE), np.float32) for _ in range(2))
    for c in range(NC5):
        a = ang[CCOL[c]:CCOL[c] + CROWS[c]]
        cos[:len(a), c] = np.concatenate([np.cos(a), np.cos(a)], 1)
        sin[:len(a), c] = np.concatenate([-np.sin(a), np.sin(a)], 1)
    return cos, sin


def build(nc, x_meta, x_prompt, x_sample, g_mix, w_in, b_gates, conv_w, g_q, g_k, lams, g_da, g_ml,
          w_out, g_ffn, w_router, w_gate, w_up, w_down, rope_cos, rope_sin, out, xn_rows, stages=5):
    with ExitStack() as ctx:
        base = (nc.sbuf_base + 31) // 32 * 32
        everything = Map(nc, base, 0, A_END)
        assert base + A_END <= nc.sbuf_usable_end, (base, A_END, nc.sbuf_usable_end)
        del everything
        keep = Map(nc, base, A_S, A_Q)
        ident = keep("ident", [P, P])
        causal = keep("causal", [P, 2, P])
        cos2 = keep("cos2", [P, NC5, ROPE])
        sin2 = keep("sin2", [P, NC5, ROPE])
        gq = keep("gq", [P, QD])
        gk = keep("gk", [P, QD])
        gda = keep("gda", [P, HD])
        gml = keep("gml", [P, HD])
        cols = keep("cols", [P, 32])
        lamv = keep("lamv", [P, 4, QD])
        lam = keep("lam", [P, 4])
        bgate = keep("bgate", [16, 1])
        eps = keep("eps", [P, 1])
        wgates = keep("wgates", [P, KD, 16])
        gates = keep("gates", [16, TZ])
        rows_at = keep.at
        rowt = keep("rowt", [8, 6, T])
        colt = keep("colt", [P, 4, NC5, 8])

        hT = Map(nc, base, A_HT, A_W)("hT", [P, KD, TZ])
        mixT = Map(nc, base, A_HT, A_W)("mixT", [P, KD, G * T])
        wblk = Map(nc, base, A_W, A_S)("wblk", [P, 2, KD, 512])
        wo = Map(nc, base, A_W, A_S)("wo", [P, KD, D])
        qk_map = Map(nc, base, A_Q, A_V)
        qT = qk_map("qT", [P, HEADS, TZ])
        kT = qk_map("kT", [P, HEADS, TZ])
        V = Map(nc, base, A_V, A_MO)("V", [P, NZ, HALF])
        MO = Map(nc, base, A_MO, A_MV)("MO", [P, NZ, HALF])
        MV = Map(nc, base, A_MV, A_QK)("MV", [P, NZ, HEADS, HD + 1])
        MQK = Map(nc, base, A_QK, A_END)("MQK", [P, 2 * HEADS, G, T])

        ps = ctx.enter_context(nc.psum_tensor("ps", [P, 8, 512], F32))
        psf = ps[:].rearrange("p b n -> p (b n)")

        def banks(a, rows=P):
            return psf[0:rows, 512 * a:]

        def sem(name):
            return ctx.enter_context(nc.semaphore(name))

        project(nc, locals())
        if stages >= 2:
            attention(nc, locals())
        if stages >= 3:
            mlstm(nc, locals())
        if stages >= 4:
            AFF = Map(nc, base, rows_at, A_Q)("AFF", [P, NC5, G * N_EXP])
            loaded = [sem(f"group_loaded{i}") for i in range(2 * NSLOT)]
            slots = weight_groups(nc, locals())
            project_out(nc, locals())
        if stages >= 5:
            experts(nc, locals())


def rms_rstd(nc, step, ss, rstd, n, eps):
    step(nc.scalar.activation(rstd, ss, ACT.Ln, bias=eps, scale=1.0 / n))
    return nc.scalar.activation(rstd, rstd, ACT.Exp, scale=-0.5)


def chained(eng, sem):
    count = [0]

    def step(ins):
        count[0] += 1
        ins.then_inc(sem, 1)
        eng.wait_ge(sem, count[0])

    return step


def project(nc, e):
    ident, causal, cos2, sin2, gq, gk, gda, gml, cols = (e[k] for k in "ident causal cos2 sin2 gq gk gda gml cols".split())
    lamv, lam, bgate, eps, wgates, gates = (e[k] for k in "lamv lam bgate eps wgates gates".split())
    hT, wblk, qT, kT, V, MO, MV, MQK = (e[k] for k in "hT wblk qT kT V MO MV MQK".split())
    banks, base, sem = e["banks"], e["base"], e["sem"]
    early = Map(nc, base, A_QK, A_END)
    xin = [early(f"xin{i}", [P, D]) for i in range(3)]
    xs = [early(f"xs{i}", [P, D]) for i in range(2)]
    sq = early("sq", [P, 512])
    qn = [early(f"qn{i}", [P, 512]) for i in range(3)]
    rt = early("rt", [P, 8, ROPE])
    rt2 = early("rt2", [P, 8, ROPE])
    ss = early("ss", [P, 2 * NZ])
    ss8 = early("ss8", [P, 2, 8])
    rowsin = early("rowsin", [32, P])
    conv = Map(nc, base, e["rows_at"], A_Q)
    zp = conv("zp", [P, G, T + 2])
    cy = [conv(f"cy{i}", [P, G, T]) for i in range(2)]

    x_loaded = [sem(f"x_loaded{i}") for i in range(3)]
    w_loaded = [sem(f"w_loaded{i}") for i in range(2)]
    small_loaded, spread_loaded = sem("small_loaded"), sem("spread_loaded")
    const_made = sem("const_made")
    wg_loaded = sem("wg_loaded")
    xs_ready, xT_done, hT_ready = sem("xs_ready"), sem("xT_done"), sem("hT_ready")
    cols_done, cols_ready = sem("cols_done"), sem("cols_ready")
    z_done, z_read_dve, z_read_act = sem("z_done"), sem("z_read_dve"), sem("z_read_act")
    sq_ready, ss_ready, rstd_ready = sem("sq_ready"), sem("ss_ready"), sem("rstd_ready")
    qn_ready, qkT_done, qkT_read = sem("qn_ready"), sem("qkT_done"), sem("qkT_read")
    zT_done, zp_ready, cy_ready, mqk_ready = (sem(s) for s in "zT_done zp_ready cy_ready mqk_ready".split())
    act_step, dve_step = sem("p_act_step"), sem("p_dve_step")
    lam_exp = sem("lam_exp")

    w_cols = e["w_in"].rearrange("o (k p) n -> (o p) k n", p=P)
    blocks = [0, HALF, 2 * HALF, OFF_MV, OFF_MO, OFF_MQK, OFF_MQK + HALF]
    N_TOK = 5
    xsrc = [e["x_meta"]] + [e[n][0, P * i:P * (i + 1), :] for n in ("x_prompt", "x_sample") for i in range(SEQ // P)]

    def z_wait(pe, i):
        j = i - 3
        if j < 0:
            return
        if j < 4 * NZ:
            pe.wait_ge(z_read_dve, j + 1)
        else:
            pe.wait_ge(z_read_act, j - 4 * NZ + 1)

    with nc.Block() as block:

        @block.sync
        def _(sp):
            for c in range(3):
                sp.dma_start(xin[c][0:ZROWS[c], :], xsrc[c]).then_inc(x_loaded[c], 16)
            sp.dma_start(rowsin[0:24, :], e["conv_w"].rearrange("o k (j p) -> (o k j) p", p=P)).then_inc(small_loaded, 16)
            sp.dma_start(rowsin[24:32, :], e["g_mix"].rearrange("o (j p) -> (o j) p", p=P)).then_inc(small_loaded, 16)
            for n in range(2):
                sp.dma_start(wblk[:, n], w_cols[:, :, blocks[n]:blocks[n] + 512]).then_inc(w_loaded[n], 16)
            for c in range(3, NZ):
                sp.wait_ge(xs_ready, c - 2)
                sp.dma_start(xin[c % 3][:], xsrc[c]).then_inc(x_loaded[c % 3], 16)
            sp.dma_start(wgates[:], w_cols[:, :, OFF_GATES:D_IN]).then_inc(wg_loaded, 16)
            for n in range(2, 7):
                sp.wait_ge(z_done, NZ * (n - 1))
                sp.dma_start(wblk[:, n % 2], w_cols[:, :, blocks[n]:blocks[n] + 512]).then_inc(w_loaded[n % 2], 16)

        @block.gpsimd
        def _(pool):
            nc.gpsimd.memset(ident[:], 0.0).then_inc(const_made, 1)
            nc.gpsimd.memset(causal[:], 0.0).then_inc(const_made, 1)
            nc.gpsimd.memset(eps[:], EPS).then_inc(const_made, 1)
            nc.gpsimd.memset(MV[:, :, :, HD:HD + 1], 1.0).then_inc(const_made, 1)
            pool.wait_ge(const_made, 4)
            nc.gpsimd.affine_select(out=ident[:], in_=ident[:], compare_op=ALU.not_equal, fill=1.0, base=0,
                                    pattern=[[-1, P]], channel_multiplier=1).then_inc(const_made, 1)
            nc.gpsimd.affine_select(out=causal[:, 0], in_=causal[:, 0], compare_op=ALU.is_ge, fill=NEG, base=0,
                                    pattern=[[1, P]], channel_multiplier=-1).then_inc(const_made, 1)
            nc.gpsimd.affine_select(out=causal[:, 1], in_=causal[:, 1], compare_op=ALU.is_ge, fill=NEG, base=0,
                                    pattern=[[-1, P]], channel_multiplier=1).then_inc(const_made, 1)
            for dst, src in ((gq, e["g_q"]), (gk, e["g_k"]), (gda, e["g_da"]), (gml, e["g_ml"])):
                pool.dma_start(dst[:], src.to_broadcast([P, src.shape[1]])).then_inc(spread_loaded, 16)
            for i, src in enumerate(e["lams"]):
                pool.dma_start(lamv[:, i], src.to_broadcast([P, QD])).then_inc(spread_loaded, 16)
            pool.dma_start(bgate[:], e["b_gates"].rearrange("o n -> n o")).then_inc(spread_loaded, 16)
            pool.dma_start(cos2[:], e["rope_cos"]).then_inc(spread_loaded, 16)
            pool.dma_start(sin2[:], e["rope_sin"]).then_inc(spread_loaded, 16)

        @block.tensor
        def _(pe):
            pe.wait_ge(const_made, 7)
            pe.wait_ge(small_loaded, 32)
            pe.transpose(banks(7)[:, 0:32], rowsin[:], ident[0:32, 0:32]).then_inc(cols_done, 1)

            def turn_x(c):
                pe.wait_ge(xs_ready, c + 1)
                if c >= 2:
                    pe.wait_ge(hT_ready, c - 1)
                for k in range(KD):
                    mm = pe.transpose(banks(2 * (c % 2))[:, k * P:k * P + ZROWS[c]],
                                      xs[c % 2][0:ZROWS[c], k * P:(k + 1) * P], ident[0:ZROWS[c], 0:ZROWS[c]])
                mm.then_inc(xT_done, 1)

            def turn_qk(i):
                R = ZROWS[i % NZ]
                pe.wait_ge(qn_ready, i + 1)
                if i >= 1:
                    pe.wait_ge(qkT_read, i)
                else:
                    pe.wait_ge(cols_ready, 1)
                for h in range(HEADS):
                    mm = pe.transpose(banks(7)[:, h * P:h * P + R], qn[i % 3][0:R, h * P:(h + 1) * P], ident[0:R, 0:R])
                mm.then_inc(qkT_done, 1)

            turn_x(0)
            for i in range(N_TOK * NZ):
                n, c = divmod(i, NZ)
                if n == 0 and c + 1 < NZ:
                    turn_x(c + 1)
                if n == 0:
                    pe.wait_ge(hT_ready, c + 1)
                if c == 0:
                    pe.wait_ge(w_loaded[n % 2], 16 * (n // 2 + 1))
                z_wait(pe, i)
                for k in range(KD):
                    mm = pe.matmul(banks(4 + i % 3, ZROWS[c])[:, 0:512], hT[:, k, ZCOL[c]:ZCOL[c] + ZROWS[c]],
                                   wblk[:, n % 2, k], start=(k == 0), stop=(k == KD - 1))
                mm.then_inc(z_done, 1)
                if 2 <= i < 2 * NZ + 2:
                    turn_qk(i - 2)
            pe.wait_ge(qkT_read, 2 * NZ)
            z_wait(pe, N_TOK * NZ + 2)
            pe.wait_ge(z_read_dve, 4 * NZ)
            for j in range(2 * HEADS + 1):
                n = 5 + j // 4
                if j % 4 == 0 and j < 8:
                    pe.wait_ge(w_loaded[n % 2], 16 * (n // 2 + 1))
                if j == 8:
                    pe.wait_ge(wg_loaded, 16)
                if j >= 2:
                    pe.wait_ge(zp_ready, j - 1)
                M = P if j < 8 else 16
                for k in range(KD):
                    lhs = wblk[:, n % 2, k, (j % 4) * P:(j % 4 + 1) * P] if j < 8 else wgates[:, k]
                    for at, a, b in ((PT, 0, N_META), (512, N_META, N_META + SEQ), (1024, N_META + SEQ, TZ)):
                        mm = pe.matmul(banks(3 * (j % 2), M)[:, at:at + b - a], lhs, hT[:, k, a:b],
                                       start=(k == 0), stop=(k == KD - 1))
                mm.then_inc(zT_done, 1)

        @block.scalar
        def _(act):
            step = chained(act, act_step)
            act.preload_act_table_set(EXP_LN)
            act.wait_ge(const_made, 4)
            act.wait_ge(spread_loaded, 16 * 11)

            def norm_x(c):
                R = ZROWS[c]
                act.wait_ge(x_loaded[c % 3], 16 * (c // 3 + 1))
                if c >= 2:
                    act.wait_ge(xT_done, c - 1)
                step(nc.scalar.activation(xs[c % 2][0:R, :], xin[c % 3][0:R, :], ACT.Square,
                                          accum_out=ss[0:R, c:c + 1]))
                r = ss[0:R, NZ + c:NZ + c + 1]
                step(rms_rstd(nc, step, ss[0:R, c:c + 1], r, D, eps[0:R, :]))
                nc.scalar.activation(xs[c % 2][0:R, :], xin[c % 3][0:R, :], ACT.Copy, scale=r).then_inc(xs_ready, 1)

            def square_qk(i):
                R = ZROWS[i % NZ]
                act.wait_ge(z_done, i + 1)
                if i >= 1:
                    act.wait_ge(ss_ready, i)
                nc.scalar.activation(sq[0:R, :], banks(4 + i % 3, R)[:, 0:512], ACT.Square).then_inc(sq_ready, 1)

            def rstd_qk(i):
                R = ZROWS[i % NZ]
                act.wait_ge(ss_ready, i + 1)
                s = ss8[0:R, i % 2, :]
                rms_rstd(nc, step, s, s, QD, eps[0:R, :]).then_inc(rstd_ready, 1)

            def read_qkT(i):
                n, c = divmod(i, NZ)
                R = ZROWS[c]
                act.wait_ge(qkT_done, i + 1)
                dst = (qT, kT)[n][:, :, ZCOL[c]:ZCOL[c] + R]
                src = banks(7)[:, 0:512].rearrange("p (h t) -> p h t", h=HEADS)[:, :, 0:R]
                nc.scalar.activation(dst, src, ACT.Copy).then_inc(qkT_read, 1)

            norm_x(0)
            norm_x(1)
            act.wait_ge(lam_exp, 1)
            nc.scalar.activation(lam[:, 0:2], lam[:, 0:2], ACT.Exp).then_inc(lam_exp, 1)
            for i in range(2 * NZ + 2):
                if 2 <= i + 2 < NZ:
                    norm_x(i + 2)
                if i < 2 * NZ:
                    square_qk(i)
                    rstd_qk(i)
                if i >= 2:
                    read_qkT(i - 2)
            for c in range(NZ):
                act.wait_ge(z_done, 4 * NZ + c + 1)
                nc.scalar.activation(MO[0:ZROWS[c], c], banks(4 + (4 * NZ + c) % 3, ZROWS[c])[:, 0:512], ACT.Sigmoid).then_inc(z_read_act, 1)
            for j in range(8):
                b = banks(3 * (j % 2))
                act.wait_ge(zT_done, j + 1)
                if j >= 1:
                    act.wait_ge(cy_ready, j)
                else:
                    act.wait_ge(const_made, 8)
                nc.scalar.activation(zp[:, 0, 1:T + 1], b[:, PT:PT + T], ACT.Copy)
                nc.scalar.activation(zp[:, 1, 1:N_META + 1], b[:, PT:512], ACT.Copy)
                nc.scalar.activation(zp[:, 1, N_META + 1:T + 1], b[:, 1024:1536], ACT.Copy).then_inc(zp_ready, 1)
                act.wait_ge(cy_ready, j + 1)
                nc.scalar.activation(MQK[:, j], cy[j % 2][:], ACT.Silu).then_inc(mqk_ready, 1)
            act.wait_ge(zT_done, 9)
            nc.scalar.activation(gates[:], banks(0, 16)[:, PT:PT + TZ], ACT.Identity, bias=bgate[:])

        @block.vector
        def _(dve):
            step = chained(dve, dve_step)
            dve.wait_ge(spread_loaded, 16 * 11)
            dve.wait_ge(cols_done, 1)
            nc.vector.tensor_copy(cols[:], banks(7)[:, 0:32]).then_inc(cols_ready, 1)
            nc.vector.tensor_scalar(gq[:], gq[:], QD ** -0.5, None, ALU.mult)
            nc.vector.tensor_scalar(gda[:], gda[:], 1.0 - LAM_INIT, None, ALU.mult)
            for i in range(2):
                step(nc.vector.tensor_tensor(lamv[:, 2 * i], lamv[:, 2 * i], lamv[:, 2 * i + 1], ALU.mult))
                ins = nc.vector.tensor_reduce(lam[:, i:i + 1], lamv[:, 2 * i], AX.X, ALU.add)
                step(ins) if i == 0 else ins.then_inc(lam_exp, 1)
            dve.wait_ge(lam_exp, 2)
            step(nc.vector.tensor_tensor(lam[:, 2:3], lam[:, 1:2], lam[:, 0:1], ALU.subtract))
            step(nc.vector.tensor_scalar(lam[:, 3:4], lam[:, 2:3], -LAM_INIT, None, ALU.add))
            dve.wait_ge(cols_ready, 1)
            gm = cols[:, 24:32].unsqueeze(2)

            def read_xT(c):
                R = ZROWS[c]
                dve.wait_ge(xT_done, c + 1)
                src = banks(2 * (c % 2))[:, 0:D].rearrange("p (k t) -> p k t", k=KD)[:, :, 0:R]
                nc.vector.tensor_tensor(hT[:, :, ZCOL[c]:ZCOL[c] + R], src, gm.to_broadcast([P, KD, R]),
                                        ALU.mult).then_inc(hT_ready, 1)

            def norm_qk(i):
                n, c = divmod(i, NZ)
                R = ZROWS[c]
                c5 = 0 if c == 0 else 1 + (c - 1) % 4
                g = (gq, gk)[n]
                dve.wait_ge(sq_ready, i + 1)
                if i >= 2:
                    dve.wait_ge(rstd_ready, i - 1)
                s8 = ss8[0:R, i % 2, :]
                nc.vector.tensor_reduce(s8, sq[0:R, :].rearrange("p (j d) -> p j d", d=QD), AX.X,
                                        ALU.add).then_inc(ss_ready, 1)
                q = qn[i % 3][0:R, :].rearrange("p (j d) -> p j d", d=QD)
                z = banks(4 + i % 3, R)[:, 0:512].rearrange("p (j d) -> p j d", d=QD)
                dve.wait_ge(rstd_ready, i + 1)
                if i >= 3:
                    dve.wait_ge(qkT_done, i - 2)
                ins = nc.vector.tensor_tensor(q, z, s8.unsqueeze(2).to_broadcast([R, 8, QD]), ALU.mult)
                ins.then_inc(z_read_dve, 1)
                dve.wait_ge(z_read_dve, i + 1)
                step(nc.vector.tensor_tensor(q, q, g[0:R, :].unsqueeze(1).to_broadcast([R, 8, QD]), ALU.mult))
                cc = cos2[0:R, c5, :].unsqueeze(1).to_broadcast([R, 8, ROPE])
                sn = sin2[0:R, c5, :].unsqueeze(1)
                half = ROPE // 2
                nc.vector.tensor_tensor(rt[0:R], q[:, :, 0:ROPE], cc, ALU.mult)
                nc.vector.tensor_tensor(rt2[0:R, :, 0:half], q[:, :, half:ROPE],
                                        sn[:, :, 0:half].to_broadcast([R, 8, half]), ALU.mult)
                step(nc.vector.tensor_tensor(rt2[0:R, :, half:ROPE], q[:, :, 0:half],
                                             sn[:, :, half:ROPE].to_broadcast([R, 8, half]), ALU.mult))
                nc.vector.tensor_tensor(q[:, :, 0:ROPE], rt[0:R], rt2[0:R], ALU.add).then_inc(qn_ready, 1)

            read_xT(0)
            for i in range(4 * NZ):
                n, c = divmod(i, NZ)
                if n == 0 and c + 1 < NZ:
                    read_xT(c + 1)
                if n < 2:
                    norm_qk(i)
                else:
                    R = ZROWS[c]
                    dve.wait_ge(z_done, i + 1)
                    if n == 2:
                        dst, src = V[0:R, c], banks(4 + i % 3, R)[:, 0:512]
                    else:
                        dst = MV[0:R, c, :, 0:HD]
                        src = banks(4 + i % 3, R)[:, 0:512].rearrange("p (h d) -> p h d", h=HEADS)
                    nc.vector.tensor_copy(dst, src).then_inc(z_read_dve, 1)
            dve.wait_ge(qkT_done, 2 * NZ)
            nc.vector.memset(zp[:, :, 0:1], 0.0)
            nc.vector.memset(zp[:, :, T + 1:T + 2], 0.0).then_inc(const_made, 1)
            for j in range(8):
                w = [cols[:, 8 * t + j:8 * t + j + 1] for t in range(3)]
                y = cy[j % 2]
                dve.wait_ge(zp_ready, j + 1)
                if j >= 2:
                    dve.wait_ge(mqk_ready, j - 1)
                step(nc.vector.tensor_scalar(y[:], zp[:, :, 0:T], w[0], None, ALU.mult))
                step(nc.vector.scalar_tensor_tensor(y[:], zp[:, :, 1:T + 1], w[1], y[:], ALU.mult, ALU.add))
                nc.vector.scalar_tensor_tensor(y[:], zp[:, :, 2:T + 2], w[2], y[:], ALU.mult,
                                               ALU.add).then_inc(cy_ready, 1)


def attention(nc, e):
    ident, gda, lam, gates, rowt, eps = (e[k] for k in "ident gda lam gates rowt eps".split())
    mixT, qT, kT, V = (e[k] for k in "mixT qT kT V".split())
    banks, base, sem = e["banks"], e["base"], e["sem"]
    tiles = Map(nc, base, A_W, A_S)
    prob = [[tiles(f"prob{i}{j}", [P, T]) for j in range(2)] for i in range(2)]
    diff = [tiles(f"diff{i}", [P, T]) for i in range(2)]
    diffT = [tiles(f"diffT{i}", [P, NC5, P]) for i in range(2)]
    osb = tiles("osb", [P, HALF])
    osq = tiles("osq", [P, HALF])
    on = tiles("on", [P, HALF])
    nmax = tiles("nmax", [P, 2, 2])
    lsum = tiles("lsum", [P, 2, 2])
    rcp = tiles("rcp", [P, 2, 2])
    so = tiles("so", [P, HEADS])
    gt_map = Map(nc, base, A_HT + HEADS * G * T * 4, A_W)
    gt = gt_map("gt", [8, 4, T])
    ga = gt_map("ga", [8, 2, T])
    gb = gt_map("gb", [8, 2, T])

    s_done, s_max, s_exp = sem("s_done"), sem("s_max"), sem("s_exp")
    a_ready, aT_done, aT_read = sem("a_ready"), sem("aT_done"), sem("aT_read")
    pv_done, o_read, osq_ready, so_ready, or_ready, on_ready, oT_done, oT_read = (
        sem(s) for s in "pv_done o_read osq_ready so_ready or_ready on_ready oT_done oT_read".split())
    gt_loaded, g_abs, g_exp, l_ready = sem("gt_loaded"), sem("g_abs"), sem("g_exp"), sem("l_ready")
    act_step, dve_step = sem("a_act_step"), sem("a_dve_step")
    row_ready = sem("row_ready")

    units = [(g, c, h) for g in range(G) for c in range(NC5) for h in range(HEADS)]
    N = len(units)
    LAST = N + 7

    with nc.Block() as block:

        @block.sync
        def _(sp):
            for k in range(4):
                for g in range(G):
                    src = gates[4 * k:4 * k + 4, :]
                    sp.dma_start(gt[4 * g:4 * g + 4, k, 0:N_META], src[:, 0:N_META]).then_inc(gt_loaded, 16)
                    a = N_META + SEQ * g
                    sp.dma_start(gt[4 * g:4 * g + 4, k, N_META:T], src[:, a:a + SEQ]).then_inc(gt_loaded, 16)

        @block.tensor
        def _(pe):
            def scores(i):
                g, c, h = units[i]
                R, a = CROWS[c], ZCOL[zc(g, c)]
                for j in range(2):
                    if i >= 1:
                        pe.wait_ge(s_exp, 2 * (i - 1) + j + 1)
                    for at, b, n in ((0, N_META + SEQ * g, SEQ), (SEQ, 0, N_META)):
                        mm = pe.matmul(banks(2 * j, R)[:, at:at + n], qT[QD * j:QD * j + QD, h, a:a + R],
                                       kT[QD * j:QD * j + QD, h, b:b + n], start=True, stop=True)
                    mm.then_inc(s_done, 1)

            def turn(i):
                R = CROWS[units[i][1]]
                pe.wait_ge(a_ready, i + 1)
                if i >= 1:
                    pe.wait_ge(aT_read, i)
                for k in range(NC5):
                    n = P if k < 4 else N_META
                    mm = pe.transpose(banks(4, n)[:, k * P:k * P + R], diff[i % 2][0:R, k * P:k * P + n], ident[0:R, 0:R])
                mm.then_inc(aT_done, 1)

            def values(i):
                g, c, h = units[i]
                R = CROWS[c]
                pe.wait_ge(aT_read, i + 1)
                if h == 0 and i > 0:
                    pe.wait_ge(o_read, i // 4)
                for k in range(NC5):
                    n = P if k < 4 else N_META
                    mm = pe.matmul(banks(6, R)[:, h * HD:(h + 1) * HD], diffT[i % 2][0:n, k, 0:R],
                                   V[0:n, zc(g, (k + 1) % NC5), h * HD:(h + 1) * HD], start=(k == 0), stop=(k == 4))
                mm.then_inc(pv_done, 1)

            def turn_out(t):
                R = CROWS[t % NC5]
                pe.wait_ge(on_ready, t + 1)
                if t >= 1:
                    pe.wait_ge(oT_read, t)
                for h in range(HEADS):
                    mm = pe.transpose(banks(7)[:, h * P:h * P + R], on[0:R, h * HD:(h + 1) * HD], ident[0:R, 0:R])
                mm.then_inc(oT_done, 1)

            for s in range(LAST):
                if s < N:
                    scores(s)
                if 1 <= s <= N:
                    turn(s - 1)
                if 2 <= s <= N + 1:
                    values(s - 2)
                if s >= 8 and s % 4 == 0 and (s - 8) // 4 < G * NC5:
                    turn_out((s - 8) // 4)

        @block.scalar
        def _(act):
            step = chained(act, act_step)
            act.preload_act_table_set(EXP_LN)

            def softmax(i):
                R = CROWS[units[i][1]]
                for j in range(2):
                    act.wait_ge(s_max, 2 * i + j + 1)
                    if i >= 2:
                        act.wait_ge(a_ready, i - 1)
                    nc.scalar.activation(prob[i % 2][j][0:R, :], banks(2 * j, R)[:, 0:T], ACT.Exp,
                                         bias=nmax[0:R, i % 2, j:j + 1],
                                         accum_out=lsum[0:R, i % 2, j:j + 1]).then_inc(s_exp, 1)

            def read_turned(i):
                R = CROWS[units[i][1]]
                act.wait_ge(aT_done, i + 1)
                if i >= 2:
                    act.wait_ge(pv_done, i - 1)
                src = banks(4)[:, 0:4 * P].rearrange("p (k t) -> p k t", k=4)[:, :, 0:R]
                nc.scalar.activation(diffT[i % 2][:, 0:4, 0:R], src, ACT.Copy)
                nc.scalar.activation(diffT[i % 2][0:N_META, 4, 0:R], banks(5, N_META)[:, 0:R],
                                     ACT.Copy).then_inc(aT_read, 1)

            def read_out(t):
                R = CROWS[t % NC5]
                act.wait_ge(pv_done, 4 * t + 4)
                if t >= 1:
                    act.wait_ge(on_ready, t)
                nc.scalar.activation(osb[0:R, :], banks(6, R)[:, 0:HALF], ACT.Copy).then_inc(o_read, 1)
                act.wait_ge(o_read, t + 1)
                nc.scalar.activation(osq[0:R, :], osb[0:R, :], ACT.Square).then_inc(osq_ready, 1)

            def rstd_out(t):
                R = CROWS[t % NC5]
                act.wait_ge(so_ready, t + 1)
                rms_rstd(nc, step, so[0:R, :], so[0:R, :], HD, eps[0:R, :]).then_inc(or_ready, 1)

            def store_out(t):
                R, a = CROWS[t % NC5], mixcol(*divmod(t, NC5))
                act.wait_ge(oT_done, t + 1)
                src = banks(7)[:, 0:HALF].rearrange("p (h t) -> p h t", h=HEADS)[:, :, 0:R]
                nc.scalar.activation(mixT[:, 0:HEADS, a:a + R], src, ACT.Copy).then_inc(oT_read, 1)

            for s in range(LAST + 2):
                t, r = divmod(s - 6, 4)
                if r == 0 and 0 <= t < G * NC5:
                    read_out(t)
                if r == 1 and 0 <= t < G * NC5:
                    rstd_out(t)
                if r == 3 and 0 <= t < G * NC5:
                    store_out(t)
                if s < N:
                    softmax(s)
                if 1 <= s <= N:
                    read_turned(s - 1)
                if s == 5:
                    act.wait_ge(g_abs, 1)
                    step(nc.scalar.activation(ga[:], ga[:], ACT.Exp, scale=-1.0))
                    nc.scalar.activation(ga[:], ga[:], ACT.Ln, bias=1.0).then_inc(g_exp, 1)

        @block.vector
        def _(dve):
            step = chained(dve, dve_step)
            f, li = gt[:, 1::2, :], gt[:, 0::2, :]

            def gates_magnitude():
                dve.wait_ge(gt_loaded, 16 * 16)
                step(nc.vector.tensor_scalar(ga[:], f, -1.0, None, ALU.mult))
                nc.vector.tensor_tensor(ga[:], ga[:], f, ALU.max).then_inc(g_abs, 1)
                dve.wait_ge(g_abs, 1)
                step(nc.vector.tensor_scalar(gb[:], f, 0.0, None, ALU.min))

            def gate_rows():
                dve.wait_ge(g_exp, 1)
                step(nc.vector.tensor_tensor(gb[:], gb[:], ga[:], ALU.subtract))
                step(nc.vector.memset(ga[:], 0.0))
                for d, order in ((0, slice(None)), (1, slice(None, None, -1))):
                    step(nc.vector.tensor_tensor_scan(rowt[:, d, order], gb[:, d, order], ga[:, d, order], 0.0, ALU.add, ALU.add))
                    step(nc.vector.tensor_tensor_scan(rowt[:, 4 + d, order], gb[:, d, order], li[:, d, order], 0.0, ALU.add, ALU.max))
                step(nc.vector.tensor_tensor(rowt[:, 2:4], li, rowt[:, 0:2], ALU.subtract))
                step(nc.vector.tensor_tensor(rowt[:, 0:2], rowt[:, 0:2], rowt[:, 4:6], ALU.subtract))

            def maxima(i):
                R = CROWS[units[i][1]]
                for j in range(2):
                    dve.wait_ge(s_done, 2 * i + j + 1)
                    nc.vector.tensor_reduce(nmax[0:R, i % 2, j:j + 1], banks(2 * j, R)[:, 0:T], AX.X, ALU.max,
                                            negate=True).then_inc(s_max, 1)

            def combine(i):
                R = CROWS[units[i][1]]
                dve.wait_ge(s_exp, 2 * i + 2)
                r = rcp[0:R, i % 2]
                step(nc.vector.reciprocal(r, lsum[0:R, i % 2]))
                step(nc.vector.tensor_tensor(r[:, 1:2], r[:, 1:2], lam[0:R, 3:4], ALU.mult))
                if i >= 2:
                    dve.wait_ge(aT_done, i - 1)
                p0, p1 = (prob[i % 2][j][0:R, :] for j in range(2))
                step(nc.vector.tensor_scalar(diff[i % 2][0:R, :], p0, r[:, 0:1], None, ALU.mult))
                nc.vector.scalar_tensor_tensor(diff[i % 2][0:R, :], p1, r[:, 1:2], diff[i % 2][0:R, :], ALU.mult,
                                               ALU.add).then_inc(a_ready, 1)

            def sum_out(t):
                R = CROWS[t % NC5]
                dve.wait_ge(osq_ready, t + 1)
                nc.vector.tensor_reduce(so[0:R, :], osq[0:R, :].rearrange("p (h d) -> p h d", h=HEADS), AX.X,
                                        ALU.add).then_inc(so_ready, 1)

            def norm_out(t):
                R = CROWS[t % NC5]
                dve.wait_ge(or_ready, t + 1)
                if t >= 1:
                    dve.wait_ge(oT_done, t)
                o, y = (x[0:R, :].rearrange("p (h d) -> p h d", h=HEADS) for x in (osb, on))
                step(nc.vector.tensor_tensor(y, o, so[0:R, :].unsqueeze(2).to_broadcast([R, HEADS, HD]), ALU.mult))
                nc.vector.tensor_tensor(y, y, gda[0:R, :].unsqueeze(1).to_broadcast([R, HEADS, HD]),
                                        ALU.mult).then_inc(on_ready, 1)

            for s in range(LAST):
                if s < N:
                    maxima(s)
                t, r = divmod(s - 6, 4)
                if r == 0 and 0 <= t < G * NC5:
                    sum_out(t)
                if r == 1 and 0 <= t < G * NC5:
                    norm_out(t)
                if s < N:
                    combine(s)
                if s == 4:
                    gates_magnitude()
                if s == 8:
                    gate_rows()


def mlstm(nc, e):
    ident, causal, gml, rowt, colt, eps = (e[k] for k in "ident causal gml rowt colt eps".split())
    mixT, MO, MV, MQK = (e[k] for k in "mixT MO MV MQK".split())
    banks, base, sem = e["banks"], e["base"], e["sem"]
    weights = Map(nc, base, A_Q, A_MO)
    pw = [[weights(f"pw{i}{d}", [P, NC5, T]) for d in range(2)] for i in range(2)]
    diag = [weights(f"diag{i}", [P, 2, P]) for i in range(2)]
    em = weights("em", [P, 2, NC5, 8])
    den = weights("den", [P, 8])
    sh = weights("sh", [P, 2, HEADS])
    hsq = weights("hsq", [P, HALF])
    late = Map(nc, base, A_W, A_S)
    ew = [[late(f"ew{i}{d}", [P, T]) for d in range(2)] for i in range(2)]
    spr = [late(f"spr{i}", [P, 2, T]) for i in range(2)]
    hm = late("hm", [P, NC5, HALF])
    hn = [late(f"hn{i}", [P, HALF]) for i in range(2)]

    col_done, col_ready = sem("col_done"), sem("col_ready")
    a_done, spr_ready, s_done, p_ready = sem("m_a_done"), sem("m_spr_ready"), sem("m_s_done"), sem("m_p_ready")
    diag_ready, ew_ready = sem("m_diag_ready"), sem("m_ew_ready")
    n_done, n_read = sem("m_n_done"), sem("m_n_read")
    hsq_ready, sh_ready, hr_ready, hn_ready, hT_done, hT_read = (
        sem(s) for s in "hsq_ready sh_ready hr_ready hn_ready hmT_done hmT_read".split())
    act_step, dve_step = sem("m_act_step"), sem("m_dve_step")

    units = [(g, h) for g in range(G) for h in range(HEADS)]
    N = NC5 * len(units)
    outs = [n for n in range(N) if units[n // NC5][1] == HEADS - 1]
    LAST = N + 11

    def where(n):
        u, c = divmod(n, NC5)
        return u, c, CROWS[c], CCOL[c]

    with nc.Block() as block:

        @block.tensor
        def _(pe):
            for k in range(4):
                for c in range(NC5):
                    at = (k * NC5 + c) * 8
                    mm = pe.transpose(banks(7, CROWS[c])[:, at:at + 8], rowt[:, 2 + k, CCOL[c]:CCOL[c] + CROWS[c]],
                                      ident[0:8, 0:8])
            mm.then_inc(col_done, 1)

            def spread(u):
                if u >= 1:
                    pe.wait_ge(spr_ready, u)
                for d in range(2):
                    for at, a, n in ((PT, 0, N_META), (512, N_META, SEQ)):
                        mm = pe.matmul(banks(2 * d)[:, at:at + n], ident[0:8, u:u + 1].to_broadcast([8, P]),
                                       rowt[:, d, a:a + n], start=True, stop=True)
                mm.then_inc(a_done, 1)

            def scores(n):
                u, c, R, t = where(n)
                g, h = units[u]
                if n >= 1:
                    pe.wait_ge(p_ready, n)
                for at, a, w in ((PT, 0, N_META), (512, N_META, SEQ)):
                    mm = pe.matmul(banks(4, R)[:, at:at + w], MQK[:, HEADS + h, g, t:t + R], MQK[:, h, g, a:a + w],
                                   start=True, stop=True)
                mm.then_inc(s_done, 1)

            def sums(n):
                u, c, R, t = where(n)
                g, h = units[u]
                pe.wait_ge(p_ready, NC5 * (u + 1))
                if n >= 1:
                    pe.wait_ge(n_read, n)
                for d, over in ((0, range(0, c + 1)), (1, range(c, NC5))):
                    for s in over:
                        mm = pe.matmul(banks(6, R)[:, d * (HD + 1):(d + 1) * (HD + 1)], pw[u % 2][d][0:CROWS[s], s, t:t + R],
                                       MV[0:CROWS[s], zc(g, s), h], start=(s == over[0]), stop=(s == over[-1]))
                mm.then_inc(n_done, 1)

            def turn_out(o):
                R = CROWS[o % NC5]
                pe.wait_ge(hn_ready, o + 1)
                if o >= 1:
                    pe.wait_ge(hT_read, o)
                else:
                    pe.wait_ge(col_ready, 2)
                for h in range(HEADS):
                    mm = pe.transpose(banks(7)[:, h * P:h * P + R], hn[o % 2][0:R, h * HD:(h + 1) * HD], ident[0:R, 0:R])
                mm.then_inc(hT_done, 1)

            for s in range(LAST):
                if s < N:
                    if s % NC5 == 0:
                        spread(s // NC5)
                    scores(s)
                if 0 <= s - NC5 < N:
                    sums(s - NC5)
                if s - 9 in outs:
                    turn_out(outs.index(s - 9))

        @block.scalar
        def _(act):
            step = chained(act, act_step)
            act.preload_act_table_set(EXP_LN)
            act.wait_ge(col_done, 1)
            for k, dst in ((0, colt), (2, em)):
                for c in range(NC5):
                    R = CROWS[c]
                    src = banks(7, R)[:, 0:4 * NC5 * 8].rearrange("p (k c u) -> p k c u", k=4, c=NC5)[:, k:k + 2, c]
                    ins = nc.scalar.activation(dst[0:R, 0:2, c], src, ACT.Copy if k == 0 else ACT.Exp,
                                               scale=1.0 if k == 0 else -1.0)
                ins.then_inc(col_ready, 1)
            act.wait_ge(col_ready, 2)

            def weigh(n):
                u, c, R, t = where(n)
                if c == 0:
                    act.wait_ge(a_done, u + 1)
                    if u >= 2:
                        act.wait_ge(diag_ready, NC5 * (u - 1))
                    for d in range(2):
                        ins = nc.scalar.activation(spr[u % 2][:, d], banks(2 * d)[:, PT:PT + T], ACT.Copy)
                    ins.then_inc(spr_ready, 1)
                    act.wait_ge(spr_ready, u + 1)
                a = spr[u % 2]
                if n >= 2:
                    act.wait_ge(p_ready, n - 1)
                f, b = ew[n % 2]
                if c < NC5 - 1:
                    nc.scalar.activation(f[0:R, t + R:T], a[0:R, 0, t + R:T], ACT.Exp, bias=colt[0:R, 0, c, u:u + 1])
                if c > 0:
                    nc.scalar.activation(b[0:R, 0:t], a[0:R, 1, 0:t], ACT.Exp, bias=colt[0:R, 1, c, u:u + 1])
                act.wait_ge(diag_ready, n + 1)
                for d, w in enumerate((f, b)):
                    ins = nc.scalar.activation(w[0:R, t:t + R], diag[n % 2][0:R, d, 0:R], ACT.Exp)
                ins.then_inc(ew_ready, 1)

            def square_out(o):
                R, c = CROWS[o % NC5], o % NC5
                act.wait_ge(n_read, outs[o] + 1)
                if o >= 1:
                    act.wait_ge(sh_ready, o)
                nc.scalar.activation(hsq[0:R, :], hm[0:R, c], ACT.Square).then_inc(hsq_ready, 1)

            def rstd_out(o):
                R = CROWS[o % NC5]
                act.wait_ge(sh_ready, o + 1)
                rms_rstd(nc, step, sh[0:R, o % 2], sh[0:R, o % 2], HD, eps[0:R, :]).then_inc(hr_ready, 1)

            def store_out(o):
                R, a = CROWS[o % NC5], mixcol(*divmod(o, NC5))
                act.wait_ge(hT_done, o + 1)
                src = banks(7)[:, 0:HALF].rearrange("p (h t) -> p h t", h=HEADS)[:, :, 0:R]
                nc.scalar.activation(mixT[:, HEADS:, a:a + R], src, ACT.Copy).then_inc(hT_read, 1)

            for s in range(LAST):
                if s < N:
                    weigh(s)
                if s - 7 in outs:
                    square_out(outs.index(s - 7))
                if s - 8 in outs:
                    rstd_out(outs.index(s - 8))
                if s - 10 in outs:
                    store_out(outs.index(s - 10))

        @block.vector
        def _(dve):
            step = chained(dve, dve_step)
            dve.wait_ge(col_ready, 2)

            def mask(n):
                u, c, R, t = where(n)
                dve.wait_ge(spr_ready, u + 1)
                if n >= 2:
                    dve.wait_ge(ew_ready, n - 1)
                for d in range(2):
                    ins = nc.vector.scalar_tensor_tensor(diag[n % 2][0:R, d, 0:R], spr[u % 2][0:R, d, t:t + R],
                                                         colt[0:R, d, c, u:u + 1], causal[0:R, d, 0:R], ALU.add, ALU.add)
                ins.then_inc(diag_ready, 1)

            def apply(n):
                u, c, R, t = where(n)
                dve.wait_ge(s_done, n + 1)
                dve.wait_ge(ew_ready, n + 1)
                if u >= 2:
                    dve.wait_ge(n_done, NC5 * (u - 1))
                for d, a, b in ((0, t, T), (1, 0, t + R)):
                    ins = nc.vector.scalar_tensor_tensor(pw[u % 2][d][0:R, c, a:b], banks(4, R)[:, PT + a:PT + b], HD ** -0.5,
                                                         ew[n % 2][d][0:R, a:b], ALU.mult, ALU.mult)
                ins.then_inc(p_ready, 1)

            def divide(n):
                u, c, R, t = where(n)
                h = units[u][1]
                s = banks(6, R)[:, 0:2 * (HD + 1)].rearrange("p (d w) -> p d w", d=2)
                dve.wait_ge(n_done, n + 1)
                d = den[0:R, :]
                step(nc.vector.tensor_copy(d[:, 0:2], s[:, :, HD]))
                step(nc.vector.scalar_tensor_tensor(d[:, 2:4], d[:, 0:2], -1.0, d[:, 0:2], ALU.mult, ALU.max))
                step(nc.vector.tensor_tensor(d[:, 4:6], d[:, 2:4], em[0:R, :, c, u], ALU.max))
                step(nc.vector.reciprocal(d[:, 6:8], d[:, 4:6]))
                out = hm[0:R, c, h * HD:(h + 1) * HD]
                step(nc.vector.tensor_scalar(out, s[:, 0, 0:HD], d[:, 6:7], None, ALU.mult))
                nc.vector.scalar_tensor_tensor(out, s[:, 1, 0:HD], d[:, 7:8], out, ALU.mult, ALU.add).then_inc(n_read, 1)

            def sum_out(o):
                R = CROWS[o % NC5]
                dve.wait_ge(hsq_ready, o + 1)
                if o >= 2:
                    dve.wait_ge(hr_ready, o - 1)
                nc.vector.tensor_reduce(sh[0:R, o % 2], hsq[0:R, :].rearrange("p (h d) -> p h d", h=HEADS), AX.X,
                                        ALU.add).then_inc(sh_ready, 1)

            def norm_out(o):
                g, c = divmod(o, NC5)
                R = CROWS[c]
                dve.wait_ge(hr_ready, o + 1)
                if o >= 2:
                    dve.wait_ge(hT_done, o - 1)
                y = hn[o % 2][0:R, :]
                y4 = y.rearrange("p (h d) -> p h d", h=HEADS)
                x4 = hm[0:R, c].rearrange("p (h d) -> p h d", h=HEADS)
                step(nc.vector.tensor_tensor(y4, x4, sh[0:R, o % 2].unsqueeze(2).to_broadcast([R, HEADS, HD]), ALU.mult))
                step(nc.vector.tensor_tensor(y4, y4, gml[0:R, :].unsqueeze(1).to_broadcast([R, HEADS, HD]), ALU.mult))
                nc.vector.tensor_tensor(y, y, MO[0:R, zc(g, c)], ALU.mult).then_inc(hn_ready, 1)

            for s in range(LAST):
                if s < N:
                    mask(s)
                if 0 <= s - 6 < N:
                    divide(s - 6)
                if s < N:
                    apply(s)
                if s - 7 in outs:
                    sum_out(outs.index(s - 7))
                if s - 8 in outs:
                    norm_out(outs.index(s - 8))


NSLOT = 4


def weight_groups(nc, e):
    ring = Map(nc, e["base"], A_Q, A_END)
    slots = []
    for i in range(NSLOT):
        slots.append((ring(f"wg{i}", [P, KD, 256]), ring(f"wu{i}", [P, KD, 256]), ring(f"wd{i}", [P, 2, D])))
    return slots


def load_group(eng, e, slots, loaded, expert, j, part):
    wg, wu, wd = slots[j % NSLOT]
    if "gu" in part:
        for t, w in ((wg, e["w_gate"]), (wu, e["w_up"])):
            src = w[0, bass.ds(expert, 1), :, 256 * j:256 * (j + 1)].rearrange("o (k p) f -> (o p) k f", p=P)
            eng.dma_start(t[:], src).then_inc(loaded[j % NSLOT], 16)
    if "d" in part:
        src = e["w_down"][0, bass.ds(expert, 1), 256 * j:256 * (j + 1), :].rearrange("o (c p) d -> (o p) c d", p=P)
        eng.dma_start(wd[:], src).then_inc(loaded[NSLOT + j % NSLOT], 16)


def project_out(nc, e):
    ident, eps, wo, mixT = (e[k] for k in "ident eps wo mixT".split())
    banks, base, sem, slots, loaded = e["banks"], e["base"], e["sem"], e["slots"], e["loaded"]
    AFF = e["AFF"]
    tiles = Map(nc, base, A_X, A_END)
    x = [tiles(f"xr{i}", [P, D]) for i in range(2)]
    x2 = [tiles(f"x2{i}", [P, D]) for i in range(2)]
    xn = [tiles(f"xn{i}", [P, D]) for i in range(2)]
    xnT = [tiles(f"xnT{i}", [P, KD, P]) for i in range(2)]
    junk = tiles("junk", [P, D])
    gffn = tiles("gffn", [P, D])
    wr = tiles("wr", [P, KD, N_EXP])
    sx = tiles("sx", [P, 2, 2])
    ex = tiles("ex", [P, 2, 2, N_EXP])
    mx = tiles("mx", [P, 2, 2, 4])

    chunks = [(None, 0)] + [(g, c) for g in range(G) for c in range(1, NC5)]
    rows = [2 * N_META] + [P] * (NZ - 1)
    col = [0] + [mixcol(g, c) for g, c in chunks[1:]]

    def dram_rows(i):
        if i == 0:
            return [(slice(N_META * g, N_META * (g + 1)), slice(T * g, T * g + N_META)) for g in range(G)]
        g, c = chunks[i]
        return [(slice(0, P), slice(T * g + CCOL[c], T * g + CCOL[c] + P))]

    def x_rows(i):
        if i == 0:
            return [(slice(N_META * g, N_META * (g + 1)), e["x_meta"]) for g in range(G)]
        g, c = chunks[i]
        return [(slice(0, P), e[("x_prompt", "x_sample")[g]][0, P * (c - 1):P * c, :])]

    wo_loaded = [sem(f"wo_loaded{k}") for k in range(KD)]
    x_loaded = [sem(f"xr_loaded{i}") for i in range(2)]
    gffn_loaded, wr_loaded = sem("gffn_loaded"), sem("wr_loaded")
    o_done, x2_ready, sx_ready, xs_ready, xn_ready = (sem(s) for s in "o_done x2_ready sx_ready xsc_ready xn_ready".split())
    x2_stored = [sem(f"x2_stored{i}") for i in range(2)]
    xn_stored = [sem(f"xn_stored{i}") for i in range(2)]
    t_done, t_read, r_done, r_max, r_exp, r_ready = (sem(s) for s in "xnT_done xnT_read r_done r_max r_exp r_ready".split())
    act_step, dve_step = sem("o_act_step"), sem("o_dve_step")

    def loads(i):
        return 16 * (i // 2 + 1 + (1 if i % 2 == 0 else 0))

    with nc.Block() as block:

        @block.sync
        def _(sp):
            wo_rows = e["w_out"].rearrange("o (k p) n -> (o p) k n", p=P)
            for k in range(KD):
                sp.dma_start(wo[:, k], wo_rows[:, k]).then_inc(wo_loaded[k], 16)
                if k == 0:
                    for i in range(2):
                        for r, src in x_rows(i):
                            sp.dma_start(x[i][r, :], src).then_inc(x_loaded[i], 16)
            sp.dma_start(wr[:], e["w_router"].rearrange("o (k p) n -> (o p) k n", p=P)).then_inc(wr_loaded, 16)
            for j in range(3):
                load_group(sp, e, slots, loaded, 0, j, "gu d")
            for i in range(NZ):
                sp.wait_ge(x2_ready, i + 1)
                for r, d in dram_rows(i):
                    sp.dma_start(e["out"][d, :], x2[i % 2][r, :]).then_inc(x2_stored[i % 2], 16)
                if i + 2 < NZ:
                    for r, src in x_rows(i + 2):
                        sp.dma_start(x[i % 2][r, :], src).then_inc(x_loaded[i % 2], 16)
                sp.wait_ge(xn_ready, i + 1)
                for r, d in dram_rows(i):
                    sp.dma_start(e["xn_rows"][d, :], xn[i % 2][r, :]).then_inc(xn_stored[i % 2], 16)
            for i in range(2):
                last = NZ - 1 - (NZ - 1 - i) % 2
                sp.wait_ge(x2_stored[i], loads(last))
                sp.wait_ge(xn_stored[i], loads(last))

        @block.gpsimd
        def _(pool):
            pool.dma_start(gffn[:], e["g_ffn"].to_broadcast([P, D])).then_inc(gffn_loaded, 16)

        @block.tensor
        def _(pe):
            def product(i):
                R = rows[i]
                if i >= 2:
                    pe.wait_ge(x2_ready, i - 1)
                for k in range(KD):
                    if i == 0:
                        pe.wait_ge(wo_loaded[k], 16)
                    for n in range(2):
                        mm = pe.matmul(banks(2 * (i % 2) + n, R)[:, 0:512], mixT[:, k, col[i]:col[i] + R],
                                       wo[:, k, 512 * n:512 * (n + 1)], start=(k == 0), stop=(k == KD - 1))
                mm.then_inc(o_done, 1)

            def turn(i):
                R = rows[i]
                pe.wait_ge(xn_ready, i + 1)
                if i >= 1:
                    pe.wait_ge(t_read, i)
                for k in range(KD):
                    mm = pe.transpose(banks(4)[:, k * P:k * P + R], xn[i % 2][0:R, k * P:(k + 1) * P], ident[0:R, 0:R])
                mm.then_inc(t_done, 1)

            def route(i):
                pe.wait_ge(t_read, i + 1)
                if i == 0:
                    pe.wait_ge(wr_loaded, 16)
                else:
                    pe.wait_ge(r_exp, i)
                for g, a, R in ([(0, 0, N_META), (1, N_META, N_META)] if i == 0 else [(0, 0, P)]):
                    for k in range(KD):
                        mm = pe.matmul(banks(6, R)[:, N_EXP * g:N_EXP * (g + 1)], xnT[i % 2][:, k, a:a + R], wr[:, k],
                                       start=(k == 0), stop=(k == KD - 1))
                mm.then_inc(r_done, 1)

            for s in range(NZ + 3):
                if s < NZ:
                    product(s)
                if 0 <= s - 2 < NZ:
                    turn(s - 2)
                if 0 <= s - 3 < NZ:
                    route(s - 3)

        @block.scalar
        def _(act):
            step = chained(act, act_step)
            act.preload_act_table_set(EXP_LN)

            def scale(i):
                R = rows[i]
                act.wait_ge(x2_ready, i + 1)
                s = sx[0:R, i % 2]
                step(nc.scalar.activation(junk[0:R, :], x2[i % 2][0:R, :], ACT.Square, accum_out=s[:, 0:1]))
                step(rms_rstd(nc, step, s[:, 0:1], s[:, 1:2], D, eps[0:R, :]))
                if i >= 2:
                    act.wait_ge(t_done, i - 1)
                    act.wait_ge(xn_stored[i % 2], loads(i - 2))
                nc.scalar.activation(xn[i % 2][0:R, :], x2[i % 2][0:R, :], ACT.Copy, scale=s[:, 1:2]).then_inc(xs_ready, 1)

            def exp(i):
                R, n = (N_META, 2) if i == 0 else (P, 1)
                act.wait_ge(r_max, i + 1)
                for g in range(n):
                    ins = nc.scalar.activation(ex[0:R, i % 2, g], banks(6, R)[:, N_EXP * g:N_EXP * (g + 1)], ACT.Exp,
                                               bias=mx[0:R, i % 2, g, 0:1], accum_out=mx[0:R, i % 2, g, 1:2])
                ins.then_inc(r_exp, 1)

            for s in range(NZ + 4):
                if s < NZ:
                    scale(s)
                if 0 <= s - 3 < NZ:
                    exp(s - 3)

        @block.vector
        def _(dve):
            step = chained(dve, dve_step)

            def add(i):
                R = rows[i]
                dve.wait_ge(o_done, i + 1)
                dve.wait_ge(x_loaded[i % 2], loads(i))
                if i >= 2:
                    dve.wait_ge(xs_ready, i - 1)
                    dve.wait_ge(x2_stored[i % 2], loads(i - 2))
                nc.vector.tensor_tensor(x2[i % 2][0:R, :], banks(2 * (i % 2), R)[:, 0:D], x[i % 2][0:R, :],
                                        ALU.add).then_inc(x2_ready, 1)

            def weight(i):
                R = rows[i]
                dve.wait_ge(xs_ready, i + 1)
                nc.vector.tensor_tensor(xn[i % 2][0:R, :], xn[i % 2][0:R, :], gffn[0:R, :], ALU.mult).then_inc(xn_ready, 1)

            def read_turned(i):
                R = rows[i]
                dve.wait_ge(t_done, i + 1)
                if i >= 2:
                    dve.wait_ge(r_done, i - 1)
                src = banks(4)[:, 0:D].rearrange("p (k t) -> p k t", k=KD)[:, :, 0:R]
                nc.vector.tensor_copy(xnT[i % 2][:, :, 0:R], src).then_inc(t_read, 1)

            def maxima(i):
                R, n = (N_META, 2) if i == 0 else (P, 1)
                dve.wait_ge(r_done, i + 1)
                for g in range(n):
                    ins = nc.vector.tensor_reduce(mx[0:R, i % 2, g, 0:1], banks(6, R)[:, N_EXP * g:N_EXP * (g + 1)], AX.X,
                                                  ALU.max, negate=True)
                ins.then_inc(r_max, 1)

            def softmax(i):
                R, n = (N_META, 2) if i == 0 else (P, 1)
                dve.wait_ge(r_exp, i + 1)
                for g in range(n):
                    m = mx[0:R, i % 2, g]
                    to, slot = (g, 0) if i == 0 else chunks[i]
                    step(nc.vector.reciprocal(m[:, 2:3], m[:, 1:2]))
                    ins = nc.vector.tensor_scalar(AFF[0:R, slot, N_EXP * to:N_EXP * (to + 1)], ex[0:R, i % 2, g], m[:, 2:3], None,
                                                  ALU.mult)
                ins.then_inc(r_ready, 1)

            dve.wait_ge(gffn_loaded, 16)
            for s in range(NZ + 4):
                if s < NZ:
                    add(s)
                    weight(s)
                if 0 <= s - 2 < NZ:
                    read_turned(s - 2)
                if 0 <= s - 3 < NZ:
                    maxima(s - 3)
                    softmax(s - 3)


def experts(nc, e):
    ident = e["ident"]
    AFF, slots, loaded, out, xn_rows = (e[k] for k in "AFF slots loaded out xn_rows".split())
    banks, base, sem = e["banks"], e["base"], e["sem"]
    tiles = Map(nc, base, A_MOE, A_S)
    C2 = G * CAP
    RANKS = (CAP + 7) // 8 * 8
    JG = FF // 256
    PER_BANK = 3
    xg = tiles("xg", [CAP, G, D])
    xgT = tiles("xgT", [P, KD, C2])
    hid = [tiles(f"hid{i}", [P, 2, C2]) for i in range(2)]
    sil = tiles("sil", [P, 2, C2])
    yT = tiles("yT", [P, KD, C2])
    yr = tiles("yr", [CAP, G, D])
    work = [tiles(f"aff{i}", [G * N_EXP, T]) for i in range(2)]
    vals = tiles("vals", [G * N_EXP, RANKS])
    index = tiles("index", [G * N_EXP, RANKS], U32)
    indexf = tiles("indexf", [G * N_EXP, RANKS])
    gateT = tiles("gateT", [CAP, G, N_EXP])
    idxT = tiles("idxT", [CAP, G, N_EXP], U32)
    take = tiles("take", [CAP, G, 1], U32)
    give = tiles("give", [CAP, G, 1], U32)
    gate = tiles("gate", [CAP, G])

    aT_done, top_step, ranked, lists_done, lists_ready = (sem(s) for s in "affT_done top_step ranked lists_done lists_ready".split())
    take_ready, xg_loaded, xT_done, xgT_ready = (sem(s) for s in "take_ready xg_loaded xgT_done xgT_ready".split())
    gu_done, sil_ready, hid_ready, d_done = (sem(s) for s in "gu_done sil_ready hid_ready d_done".split())
    yT_ready, y_done, yr_ready = (sem(s) for s in "yT_ready yt_done yr_ready".split())
    give_free, give_ready, added = (sem(s) for s in "give_free give_ready added".split())

    def packed(first, k, rows=P):
        at = (k % PER_BANK) * C2
        return banks(first + k // PER_BANK, rows)[:, at:at + C2]

    def packed_runs(first):
        two = banks(first)[:, 0:1024].rearrange("p (b n) -> p b n", b=2)[:, :, 0:PER_BANK * C2]
        return ((slice(0, 6), two), (slice(6, 8), banks(first + 2)[:, 0:2 * C2]))

    def run_view(t, ks):
        v = t[:, ks].rearrange("p k n -> p (k n)")
        return v.rearrange("p (b n) -> p b n", b=2) if ks.start == 0 else v

    def last_user(ex, j):
        if j >= NSLOT:
            return JG * ex + j - NSLOT
        if isinstance(ex, int) and ex == 0:
            return None
        return JG * (ex - 1) + max(i for i in range(JG) if i % NSLOT == j)

    def uses(ex, j):
        return len(range(j % NSLOT, JG, NSLOT)) * ex + j // NSLOT + 1

    def per_expert(eng, body):
        body(0, True, False)
        with eng.Fori(1, N_EXP - 1) as ex:
            body(ex, False, False)
        body(N_EXP - 1, False, True)

    with nc.Block() as block:

        @block.sync
        def _(sp):
            def body(ex, first, last):
                for j in range(3 if first else 0, JG):
                    before = last_user(ex, j)
                    if before is not None:
                        sp.wait_ge(gu_done, 2 * before + 2)
                        load_group(sp, e, slots, loaded, ex, j, "gu")
                        sp.wait_ge(d_done, before + 1)
                        load_group(sp, e, slots, loaded, ex, j, "d")
                    else:
                        load_group(sp, e, slots, loaded, ex, j, "gu")
                        load_group(sp, e, slots, loaded, ex, j, "d")

            per_expert(sp, body)
            sp.wait_ge(added, 32 * N_EXP)

        @block.gpsimd
        def _(pool):
            def fetch(ex):
                pool.wait_ge(take_ready, ex + 1)
                for g in range(G):
                    nc.gpsimd.indirect_dma_start(xg[:, g, :], None, xn_rows,
                                                 bass.IndirectOffsetOnAxis(ap=take[:, g, :], axis=0)).then_inc(xg_loaded, 16)

            def add_rows(ex, first):
                if not first:
                    pool.wait_ge(added, 32 * ex)
                pool.sem_inc(give_free, 1)
                pool.wait_ge(yr_ready, 4 * ex + 4)
                for g in range(G):
                    nc.gpsimd.indirect_dma_start(out, bass.IndirectOffsetOnAxis(ap=give[:, g, :], axis=0), yr[:, g, :],
                                                 None, compute_op=ALU.add).then_inc(added, 16)

            fetch(0)
            fetch(1)
            add_rows(0, True)
            for ex in range(2, N_EXP):
                fetch(ex)
                add_rows(ex - 1, False)
            add_rows(N_EXP - 1, False)

        @block.tensor
        def _(pe):
            for c in range(NC5):
                at = PT + CCOL[c]
                mm = pe.transpose(banks(0, G * N_EXP)[:, at:at + CROWS[c]], AFF[0:CROWS[c], c], ident[0:CROWS[c], 0:CROWS[c]])
            mm.then_inc(aT_done, 1)
            pe.wait_ge(ranked, 1)
            for i, t in enumerate((vals, indexf)):
                mm = pe.transpose(banks(2, CAP)[:, 32 * i:32 * i + 32], t[:, 0:CAP], ident[0:G * N_EXP, 0:G * N_EXP])
            mm.then_inc(lists_done, 1)

            def turn_rows(ex):
                pe.wait_ge(xg_loaded, 32 * ex + 32)
                for k in range(KD):
                    for g in range(G):
                        mm = pe.transpose(packed(5, k)[:, CAP * g:CAP * (g + 1)], xg[:, g, k * P:(k + 1) * P],
                                          ident[0:CAP, 0:CAP])
                mm.then_inc(xT_done, 1)

            def up(ex, j, first):
                sl = j % NSLOT
                pe.wait_ge(loaded[sl], 32 * uses(ex, j))
                for c in range(2):
                    if not (first and j == 0):
                        pe.wait_ge(hid_ready, 2 * (JG * ex + j) + c - 1)
                    for at, w in ((0, slots[sl][0]), (C2, slots[sl][1])):
                        for k in range(KD):
                            mm = pe.matmul(banks(c)[:, at:at + C2], w[:, k, c * P:(c + 1) * P], xgT[:, k], start=(k == 0),
                                           stop=(k == KD - 1))
                    mm.then_inc(gu_done, 1)

            def down(ex, j):
                sl = j % NSLOT
                pe.wait_ge(loaded[NSLOT + sl], 16 * uses(ex, j))
                for c in range(2):
                    pe.wait_ge(hid_ready, 2 * (JG * ex + j) + c + 1)
                    for k in range(KD):
                        mm = pe.matmul(packed(2, k), slots[sl][2][:, c, k * P:(k + 1) * P], hid[j % 2][:, c],
                                       start=(j == 0 and c == 0 and k % PER_BANK == 0), stop=(j == JG - 1 and c == 1),
                                       skip_group_check=True)
                mm.then_inc(d_done, 1)

            def turn_outputs(ex, last):
                pe.wait_ge(yT_ready, ex + 1)
                if not last:
                    pe.wait_ge(xgT_ready, ex + 2)
                for i in range(4):
                    g, half = divmod(i, 2)
                    if i == 3:
                        pe.wait_ge(yr_ready, 4 * ex + 1)
                    for k in range(4):
                        mm = pe.transpose(banks(5 + i % 3, CAP)[:, k * P:(k + 1) * P], yT[:, 4 * half + k, CAP * g:CAP * (g + 1)],
                                          ident[:])
                    mm.then_inc(y_done, 1)

            def body(ex, first, last):
                pe.wait_ge(xgT_ready, ex + 1)
                for j in range(JG):
                    up(ex, j, first)
                    if j == 0 and not first:
                        turn_outputs(ex - 1, False)
                    if j >= 1:
                        down(ex, j - 1)
                if not last:
                    if not first:
                        pe.wait_ge(yr_ready, 4 * ex)
                    turn_rows(ex + 1)
                down(ex, JG - 1)

            turn_rows(0)
            per_expert(pe, body)
            turn_outputs(N_EXP - 1, True)

        @block.scalar
        def _(act):
            act.preload_act_table_set("silu_and_others")

            def group(ex, j):
                for c in range(2):
                    act.wait_ge(gu_done, 2 * (JG * ex + j) + c + 1)
                    nc.scalar.activation(sil[:, c], banks(c)[:, 0:C2], ACT.Silu).then_inc(sil_ready, 1)

            def gated_rows(ex):
                act.wait_ge(give_ready, ex + 1)
                for i in range(4):
                    g, half = divmod(i, 2)
                    act.wait_ge(y_done, 4 * ex + i + 1)
                    nc.scalar.activation(yr[:, g, 512 * half:512 * (half + 1)], banks(5 + i % 3, CAP)[:, 0:512], ACT.Copy,
                                         scale=gate[:, g:g + 1]).then_inc(yr_ready, 1)

            def body(ex, first, last):
                for j in range(JG):
                    group(ex, j)
                    if j == 0 and not first:
                        gated_rows(ex - 1)
                act.wait_ge(d_done, JG * ex + JG)
                for i, (ks, src) in enumerate(packed_runs(2)):
                    ins = nc.scalar.activation(run_view(yT, ks), src, ACT.Copy)
                ins.then_inc(yT_ready, 1)

            per_expert(act, body)
            gated_rows(N_EXP - 1)

        @block.vector
        def _(dve):
            step = chained(dve, top_step)
            dve.wait_ge(aT_done, 1)
            step(nc.vector.tensor_copy(work[0][:], banks(0, G * N_EXP)[:, PT:PT + T]))
            for r in range(RANKS // 8):
                a, b, at = work[r % 2], work[(r + 1) % 2], slice(8 * r, 8 * r + 8)
                step(nc.vector.max(vals[:, at], a[:]))
                nc.vector.max_index(index[:, at], vals[:, at], a[:])
                if r + 1 < RANKS // 8:
                    step(nc.vector.match_replace(b[:], vals[:, at], a[:], -1.0))
            step(nc.vector.engine_nop())
            nc.vector.tensor_copy(indexf[:], index[:]).then_inc(ranked, 1)
            dve.wait_ge(lists_done, 1)
            lists = banks(2, CAP)
            gates, tokens = (lists[:, a:a + 32].rearrange("p (g n) -> p g n", g=G) for a in (0, 32))
            nc.vector.tensor_copy(gateT[:], gates).then_inc(lists_ready, 1)
            for g in range(G):
                nc.vector.tensor_scalar(idxT[:, g], tokens[:, g], float(T * g), None, ALU.add).then_inc(lists_ready, 1)
            dve.wait_ge(lists_ready, 3)

            def pick(ex):
                nc.vector.tensor_copy(take[:], idxT[:, :, bass.ds(ex, 1)]).then_inc(take_ready, 1)

            def pick_out(ex):
                dve.wait_ge(give_free, ex + 1)
                nc.vector.tensor_copy(give[:], idxT[:, :, bass.ds(ex, 1)])
                nc.vector.tensor_copy(gate[:].unsqueeze(2), gateT[:, :, bass.ds(ex, 1)]).then_inc(give_ready, 1)

            def read_turned(ex):
                dve.wait_ge(xT_done, ex + 1)
                for ks, src in packed_runs(5):
                    ins = nc.vector.tensor_copy(run_view(xgT, ks), src)
                ins.then_inc(xgT_ready, 1)

            def group(ex, j):
                for c in range(2):
                    dve.wait_ge(sil_ready, 2 * (JG * ex + j) + c + 1)
                    nc.vector.tensor_tensor(hid[j % 2][:, c], sil[:, c], banks(c)[:, C2:2 * C2], ALU.mult).then_inc(hid_ready, 1)

            def body(ex, first, last):
                for j in range(JG):
                    group(ex, j)
                    if j == 0:
                        if not last:
                            dve.wait_ge(xT_done, ex + 1)
                            pick(ex + 1)
                        if not first:
                            pick_out(ex - 1)
                if not last:
                    read_turned(ex + 1)

            pick(0)
            read_turned(0)
            per_expert(dve, body)
            pick_out(N_EXP - 1)


_INS = ["x_prompt", "x_sample", "meta", "g_mix", "w_in", "b_gates", "conv_w", "g_q", "g_k", "lam_q1", "lam_k1",
        "lam_q2", "lam_k2", "g_da_out", "g_ml_out", "w_out", "g_ffn", "w_router", "w_gate", "w_up", "w_down",
        "rope_cos", "rope_sin"]


def kernel(**inputs):
    import numpy as np
    import concourse.bacc as bacc
    from concourse.bass_utils import run_bass_kernel_spmd

    inputs["rope_cos"], inputs["rope_sin"] = rope_tables(np)
    nc = bacc.Bacc("TRN2", target_bir_lowering=False, num_devices=1)
    arrays, a = {}, {}
    for name in _INS:
        arrays[f"in_{name}"] = np.ascontiguousarray(inputs[name])
        a[name] = nc.dram_tensor(f"in_{name}", arrays[f"in_{name}"].shape, F32, kind="ExternalInput").ap()
    out = nc.dram_tensor("out_rows", (G * T, D), F32, kind="ExternalOutput").ap()
    xn_rows = nc.dram_tensor("xn_rows", (G * T, D), F32, kind="Internal").ap()
    build(nc, a["meta"], a["x_prompt"], a["x_sample"], a["g_mix"], a["w_in"], a["b_gates"], a["conv_w"], a["g_q"],
          a["g_k"], [a["lam_q1"], a["lam_k1"], a["lam_q2"], a["lam_k2"]], a["g_da_out"], a["g_ml_out"], a["w_out"],
          a["g_ffn"], a["w_router"], a["w_gate"], a["w_up"], a["w_down"], a["rope_cos"], a["rope_sin"], out, xn_rows)
    rows = run_bass_kernel_spmd(nc, [arrays], core_ids=[0]).results[0]["out_rows"]
    rows = rows.reshape(G, 1, T, D)[:, :, N_META:]
    return rows[0], rows[1]
```

```python
import math
from contextlib import ExitStack

import concourse.bass as bass
from concourse import mybir
from concourse.alu_op_type import AluOpType as ALU

F32 = mybir.dt.float32
F32R = mybir.dt.float32r
BF16 = mybir.dt.bfloat16
U32 = mybir.dt.uint32
ACT = mybir.ActivationFunctionType
AX = mybir.AxisListType
P = 128

N_META = 16
SEQ = 512
G = 2
T = N_META + SEQ
TZ = N_META + G * SEQ
D = 1024
KD = D // P
HALF = D // 2
HEADS = 4
HD = HALF // HEADS
QD = HD // 2
ROPE = QD // 4
ROPE_THETA = 500000.0
EPS = 1e-6
LAM_INIT = 0.8 - 0.6 * math.exp(0.0)
NEG = -1e30
EXP_LN = "natural_log_exp_and_others"
N_EXP = 16
CAP = 2 * T // N_EXP
FF = 2816
D_IN = 3600
OFF_MQK, OFF_MV, OFF_MO, OFF_GATES = 3 * HALF, 5 * HALF, 6 * HALF, 7 * HALF

ZROWS = [N_META] + [P] * (G * SEQ // P)
ZCOL = [0] + [N_META + P * i for i in range(G * SEQ // P)]
NZ = len(ZROWS)
CROWS = [N_META] + [P] * (SEQ // P)
CCOL = [0] + [N_META + P * i for i in range(SEQ // P)]
NC5 = len(CROWS)
PT = 512 - N_META


def zc(g, c):
    return 0 if c == 0 else 1 + (SEQ // P) * g + c - 1


def mixcol(g, c):
    return N_META * g if c == 0 else 2 * N_META + SEQ * g + P * (c - 1)


A_HT = 0
A_W = A_HT + KD * G * T * 4
A_S = A_W + 2 * KD * 512 * 4
A_Q = A_S + 23744
A_V = A_Q + 2 * HEADS * TZ * 4
A_MO = A_V + NZ * HALF * 4
A_MV = A_MO + NZ * HALF * 4
A_QK = A_MV + (NZ * HEADS * (HD + 1) * 4 + 31) // 32 * 32
A_END = A_QK + 2 * HEADS * G * T * 4
SLOT = 2 * KD * 256 * 4 + 2 * D * 4
A_X = A_Q + 3 * SLOT
A_MOE = A_HT


class Map:

    def __init__(self, nc, base, at, end):
        self.nc, self.base, self.at, self.end = nc, base, at, end

    def __call__(self, name, shape, dt=F32):
        n = 4
        for s in shape[1:]:
            n *= s
        assert self.at + n <= self.end, (name, self.at + n, self.end)
        t = self.nc.alloc_sbuf_tensor_at(name, shape, dt, offset=self.base + self.at)
        self.at += (n + 31) // 32 * 32
        return t


def rope_tables(np):
    inv = ROPE_THETA ** (-np.arange(0, ROPE, 2, dtype=np.float32) / np.float32(ROPE))
    ang = np.arange(T, dtype=np.float32)[:, None] * inv.astype(np.float32)[None, :]
    cos, sin = (np.zeros((P, NC5, ROPE), np.float32) for _ in range(2))
    for c in range(NC5):
        a = ang[CCOL[c]:CCOL[c] + CROWS[c]]
        cos[:len(a), c] = np.concatenate([np.cos(a), np.cos(a)], 1)
        sin[:len(a), c] = np.concatenate([-np.sin(a), np.sin(a)], 1)
    return cos, sin


def build(nc, x_meta, x_prompt, x_sample, g_mix, w_in, b_gates, conv_w, g_q, g_k, lams, g_da, g_ml,
          w_out, g_ffn, w_router, w_gate, w_up, w_down, rope_cos, rope_sin, out, xn_rows, stages=5):
    with ExitStack() as ctx:
        base = (nc.sbuf_base + 31) // 32 * 32
        everything = Map(nc, base, 0, A_END)
        assert base + A_END <= nc.sbuf_usable_end, (base, A_END, nc.sbuf_usable_end)
        del everything
        keep = Map(nc, base, A_S, A_Q)
        ident = keep("ident", [P, P])
        causal = keep("causal", [P, 2, P])
        cos2 = keep("cos2", [P, NC5, ROPE])
        sin2 = keep("sin2", [P, NC5, ROPE])
        gq = keep("gq", [P, QD])
        gk = keep("gk", [P, QD])
        gda = keep("gda", [P, HD])
        gml = keep("gml", [P, HD])
        cols = keep("cols", [P, 32])
        lamv = keep("lamv", [P, 4, QD])
        lam = keep("lam", [P, 4])
        bgate = keep("bgate", [16, 1])
        eps = keep("eps", [P, 1])
        wgates = keep("wgates", [P, KD, 16])
        gates = keep("gates", [16, TZ])
        rows_at = keep.at
        rowt = keep("rowt", [8, 6, T])
        colt = keep("colt", [P, 4, NC5, 8])

        hT = Map(nc, base, A_HT, A_W)("hT", [P, KD, TZ])
        mixT = Map(nc, base, A_HT, A_W)("mixT", [P, KD, G * T])
        wblk = Map(nc, base, A_W, A_S)("wblk", [P, 2, KD, 512])
        wo = Map(nc, base, A_W, A_S)("wo", [P, KD, D])
        qk_map = Map(nc, base, A_Q, A_V)
        qT = qk_map("qT", [P, HEADS, TZ])
        kT = qk_map("kT", [P, HEADS, TZ])
        V = Map(nc, base, A_V, A_MO)("V", [P, NZ, HALF])
        MO = Map(nc, base, A_MO, A_MV)("MO", [P, NZ, HALF])
        MV = Map(nc, base, A_MV, A_QK)("MV", [P, NZ, HEADS, HD + 1])
        MQK = Map(nc, base, A_QK, A_END)("MQK", [P, 2 * HEADS, G, T])

        ps = ctx.enter_context(nc.psum_tensor("ps", [P, 8, 512], F32))
        psf = ps[:].rearrange("p b n -> p (b n)")

        def banks(a, rows=P):
            return psf[0:rows, 512 * a:]

        def sem(name):
            return ctx.enter_context(nc.semaphore(name))

        project(nc, locals())
        if stages >= 2:
            attention(nc, locals())
        if stages >= 3:
            mlstm(nc, locals())
        if stages >= 4:
            AFF = Map(nc, base, rows_at, A_Q)("AFF", [P, NC5, G * N_EXP])
            loaded = [sem(f"group_loaded{i}") for i in range(NGU + ND)]
            rings = weight_groups(nc, locals())
            project_out(nc, locals())
        if stages >= 5:
            experts(nc, locals())


def rms_rstd(nc, step, ss, rstd, n, eps):
    step(nc.scalar.activation(rstd, ss, ACT.Ln, bias=eps, scale=1.0 / n))
    return nc.scalar.activation(rstd, rstd, ACT.Exp, scale=-0.5)


def chained(eng, sem):
    count = [0]

    def step(ins):
        count[0] += 1
        ins.then_inc(sem, 1)
        eng.wait_ge(sem, count[0])

    return step


def project(nc, e):
    ident, causal, cos2, sin2, gq, gk, gda, gml, cols = (e[k] for k in "ident causal cos2 sin2 gq gk gda gml cols".split())
    lamv, lam, bgate, eps, wgates, gates = (e[k] for k in "lamv lam bgate eps wgates gates".split())
    hT, wblk, qT, kT, V, MO, MV, MQK = (e[k] for k in "hT wblk qT kT V MO MV MQK".split())
    banks, base, sem = e["banks"], e["base"], e["sem"]
    early = Map(nc, base, A_QK, A_END)
    xin = [early(f"xin{i}", [P, D]) for i in range(3)]
    xs = [early(f"xs{i}", [P, D]) for i in range(2)]
    sq = early("sq", [P, 512])
    qn = [early(f"qn{i}", [P, 512]) for i in range(3)]
    rt = early("rt", [P, 8, ROPE])
    rt2 = early("rt2", [P, 8, ROPE])
    ss = early("ss", [P, 2 * NZ])
    ss8 = early("ss8", [P, 2, 8])
    rowsin = early("rowsin", [32, P])
    conv = Map(nc, base, e["rows_at"], A_Q)
    zp = conv("zp", [P, G, T + 2])
    cy = [conv(f"cy{i}", [P, G, T]) for i in range(2)]

    x_loaded = [sem(f"x_loaded{i}") for i in range(3)]
    w_loaded = [sem(f"w_loaded{i}") for i in range(2)]
    small_loaded, spread_loaded = sem("small_loaded"), sem("spread_loaded")
    const_made = sem("const_made")
    wg_loaded = sem("wg_loaded")
    xs_ready, xT_done, hT_ready = sem("xs_ready"), sem("xT_done"), sem("hT_ready")
    cols_done, cols_ready = sem("cols_done"), sem("cols_ready")
    z_done, z_read_dve, z_read_act = sem("z_done"), sem("z_read_dve"), sem("z_read_act")
    sq_ready, ss_ready, rstd_ready = sem("sq_ready"), sem("ss_ready"), sem("rstd_ready")
    qn_ready, qkT_done, qkT_read = sem("qn_ready"), sem("qkT_done"), sem("qkT_read")
    zT_done, zp_ready, cy_ready, mqk_ready = (sem(s) for s in "zT_done zp_ready cy_ready mqk_ready".split())
    act_step, dve_step = sem("p_act_step"), sem("p_dve_step")
    lam_exp = sem("lam_exp")

    w_cols = e["w_in"].rearrange("o (k p) n -> (o p) k n", p=P)
    blocks = [0, HALF, 2 * HALF, OFF_MV, OFF_MO, OFF_MQK, OFF_MQK + HALF]
    N_TOK = 5
    xsrc = [e["x_meta"]] + [e[n][0, P * i:P * (i + 1), :] for n in ("x_prompt", "x_sample") for i in range(SEQ // P)]

    def z_wait(pe, i):
        j = i - 3
        if j < 0:
            return
        if j < 4 * NZ:
            pe.wait_ge(z_read_dve, j + 1)
        else:
            pe.wait_ge(z_read_act, j - 4 * NZ + 1)

    with nc.Block() as block:

        @block.sync
        def _(sp):
            for c in range(3):
                sp.dma_start(xin[c][0:ZROWS[c], :], xsrc[c]).then_inc(x_loaded[c], 16)
            sp.dma_start(rowsin[0:24, :], e["conv_w"].rearrange("o k (j p) -> (o k j) p", p=P)).then_inc(small_loaded, 16)
            sp.dma_start(rowsin[24:32, :], e["g_mix"].rearrange("o (j p) -> (o j) p", p=P)).then_inc(small_loaded, 16)
            for n in range(2):
                sp.dma_start(wblk[:, n], w_cols[:, :, blocks[n]:blocks[n] + 512]).then_inc(w_loaded[n], 16)
            for c in range(3, NZ):
                sp.wait_ge(xs_ready, c - 2)
                sp.dma_start(xin[c % 3][:], xsrc[c]).then_inc(x_loaded[c % 3], 16)
            sp.dma_start(wgates[:], w_cols[:, :, OFF_GATES:D_IN]).then_inc(wg_loaded, 16)
            for n in range(2, 7):
                sp.wait_ge(z_done, NZ * (n - 1))
                sp.dma_start(wblk[:, n % 2], w_cols[:, :, blocks[n]:blocks[n] + 512]).then_inc(w_loaded[n % 2], 16)

        @block.gpsimd
        def _(pool):
            nc.gpsimd.memset(ident[:], 0.0).then_inc(const_made, 1)
            nc.gpsimd.memset(causal[:], 0.0).then_inc(const_made, 1)
            nc.gpsimd.memset(eps[:], EPS).then_inc(const_made, 1)
            nc.gpsimd.memset(MV[:, :, :, HD:HD + 1], 1.0).then_inc(const_made, 1)
            pool.wait_ge(const_made, 4)
            nc.gpsimd.affine_select(out=ident[:], in_=ident[:], compare_op=ALU.not_equal, fill=1.0, base=0,
                                    pattern=[[-1, P]], channel_multiplier=1).then_inc(const_made, 1)
            nc.gpsimd.affine_select(out=causal[:, 0], in_=causal[:, 0], compare_op=ALU.is_ge, fill=NEG, base=0,
                                    pattern=[[1, P]], channel_multiplier=-1).then_inc(const_made, 1)
            nc.gpsimd.affine_select(out=causal[:, 1], in_=causal[:, 1], compare_op=ALU.is_ge, fill=NEG, base=0,
                                    pattern=[[-1, P]], channel_multiplier=1).then_inc(const_made, 1)
            for dst, src in ((gq, e["g_q"]), (gk, e["g_k"]), (gda, e["g_da"]), (gml, e["g_ml"])):
                pool.dma_start(dst[:], src.to_broadcast([P, src.shape[1]])).then_inc(spread_loaded, 16)
            for i, src in enumerate(e["lams"]):
                pool.dma_start(lamv[:, i], src.to_broadcast([P, QD])).then_inc(spread_loaded, 16)
            pool.dma_start(bgate[:], e["b_gates"].rearrange("o n -> n o")).then_inc(spread_loaded, 16)
            pool.dma_start(cos2[:], e["rope_cos"]).then_inc(spread_loaded, 16)
            pool.dma_start(sin2[:], e["rope_sin"]).then_inc(spread_loaded, 16)

        @block.tensor
        def _(pe):
            pe.wait_ge(const_made, 7)
            pe.wait_ge(small_loaded, 32)
            pe.transpose(banks(7)[:, 0:32], rowsin[:], ident[0:32, 0:32]).then_inc(cols_done, 1)

            def turn_x(c):
                pe.wait_ge(xs_ready, c + 1)
                if c >= 2:
                    pe.wait_ge(hT_ready, c - 1)
                for k in range(KD):
                    mm = pe.transpose(banks(2 * (c % 2))[:, k * P:k * P + ZROWS[c]],
                                      xs[c % 2][0:ZROWS[c], k * P:(k + 1) * P], ident[0:ZROWS[c], 0:ZROWS[c]])
                mm.then_inc(xT_done, 1)

            def turn_qk(i):
                R = ZROWS[i % NZ]
                pe.wait_ge(qn_ready, i + 1)
                if i >= 1:
                    pe.wait_ge(qkT_read, i)
                else:
                    pe.wait_ge(cols_ready, 1)
                for h in range(HEADS):
                    mm = pe.transpose(banks(7)[:, h * P:h * P + R], qn[i % 3][0:R, h * P:(h + 1) * P], ident[0:R, 0:R])
                mm.then_inc(qkT_done, 1)

            turn_x(0)
            for i in range(N_TOK * NZ):
                n, c = divmod(i, NZ)
                if n == 0 and c + 1 < NZ:
                    turn_x(c + 1)
                if n == 0:
                    pe.wait_ge(hT_ready, c + 1)
                if c == 0:
                    pe.wait_ge(w_loaded[n % 2], 16 * (n // 2 + 1))
                z_wait(pe, i)
                for k in range(KD):
                    mm = pe.matmul(banks(4 + i % 3, ZROWS[c])[:, 0:512], hT[:, k, ZCOL[c]:ZCOL[c] + ZROWS[c]],
                                   wblk[:, n % 2, k], start=(k == 0), stop=(k == KD - 1))
                mm.then_inc(z_done, 1)
                if 2 <= i < 2 * NZ + 2:
                    turn_qk(i - 2)
            pe.wait_ge(qkT_read, 2 * NZ)
            z_wait(pe, N_TOK * NZ + 2)
            pe.wait_ge(z_read_dve, 4 * NZ)
            for j in range(2 * HEADS + 1):
                n = 5 + j // 4
                if j % 4 == 0 and j < 8:
                    pe.wait_ge(w_loaded[n % 2], 16 * (n // 2 + 1))
                if j == 8:
                    pe.wait_ge(wg_loaded, 16)
                if j >= 2:
                    pe.wait_ge(zp_ready, j - 1)
                M = P if j < 8 else 16
                for k in range(KD):
                    lhs = wblk[:, n % 2, k, (j % 4) * P:(j % 4 + 1) * P] if j < 8 else wgates[:, k]
                    for at, a, b in ((PT, 0, N_META), (512, N_META, N_META + SEQ), (1024, N_META + SEQ, TZ)):
                        mm = pe.matmul(banks(3 * (j % 2), M)[:, at:at + b - a], lhs, hT[:, k, a:b],
                                       start=(k == 0), stop=(k == KD - 1))
                mm.then_inc(zT_done, 1)

        @block.scalar
        def _(act):
            step = chained(act, act_step)
            act.preload_act_table_set(EXP_LN)
            act.wait_ge(const_made, 4)
            act.wait_ge(spread_loaded, 16 * 11)

            def norm_x(c):
                R = ZROWS[c]
                act.wait_ge(x_loaded[c % 3], 16 * (c // 3 + 1))
                if c >= 2:
                    act.wait_ge(xT_done, c - 1)
                step(nc.scalar.activation(xs[c % 2][0:R, :], xin[c % 3][0:R, :], ACT.Square,
                                          accum_out=ss[0:R, c:c + 1]))
                r = ss[0:R, NZ + c:NZ + c + 1]
                step(rms_rstd(nc, step, ss[0:R, c:c + 1], r, D, eps[0:R, :]))
                nc.scalar.activation(xs[c % 2][0:R, :], xin[c % 3][0:R, :], ACT.Copy, scale=r).then_inc(xs_ready, 1)

            def square_qk(i):
                R = ZROWS[i % NZ]
                act.wait_ge(z_done, i + 1)
                if i >= 1:
                    act.wait_ge(ss_ready, i)
                nc.scalar.activation(sq[0:R, :], banks(4 + i % 3, R)[:, 0:512], ACT.Square).then_inc(sq_ready, 1)

            def rstd_qk(i):
                R = ZROWS[i % NZ]
                act.wait_ge(ss_ready, i + 1)
                s = ss8[0:R, i % 2, :]
                rms_rstd(nc, step, s, s, QD, eps[0:R, :]).then_inc(rstd_ready, 1)

            def read_qkT(i):
                n, c = divmod(i, NZ)
                R = ZROWS[c]
                act.wait_ge(qkT_done, i + 1)
                dst = (qT, kT)[n][:, :, ZCOL[c]:ZCOL[c] + R]
                src = banks(7)[:, 0:512].rearrange("p (h t) -> p h t", h=HEADS)[:, :, 0:R]
                nc.scalar.activation(dst, src, ACT.Copy).then_inc(qkT_read, 1)

            norm_x(0)
            norm_x(1)
            act.wait_ge(lam_exp, 1)
            nc.scalar.activation(lam[:, 0:2], lam[:, 0:2], ACT.Exp).then_inc(lam_exp, 1)
            for i in range(2 * NZ + 2):
                if 2 <= i + 2 < NZ:
                    norm_x(i + 2)
                if i < 2 * NZ:
                    square_qk(i)
                    rstd_qk(i)
                if i >= 2:
                    read_qkT(i - 2)
            for c in range(NZ):
                act.wait_ge(z_done, 4 * NZ + c + 1)
                nc.scalar.activation(MO[0:ZROWS[c], c], banks(4 + (4 * NZ + c) % 3, ZROWS[c])[:, 0:512], ACT.Sigmoid).then_inc(z_read_act, 1)
            for j in range(8):
                b = banks(3 * (j % 2))
                act.wait_ge(zT_done, j + 1)
                if j >= 1:
                    act.wait_ge(cy_ready, j)
                else:
                    act.wait_ge(const_made, 8)
                nc.scalar.activation(zp[:, 0, 1:T + 1], b[:, PT:PT + T], ACT.Copy)
                nc.scalar.activation(zp[:, 1, 1:N_META + 1], b[:, PT:512], ACT.Copy)
                nc.scalar.activation(zp[:, 1, N_META + 1:T + 1], b[:, 1024:1536], ACT.Copy).then_inc(zp_ready, 1)
                act.wait_ge(cy_ready, j + 1)
                nc.scalar.activation(MQK[:, j], cy[j % 2][:], ACT.Silu).then_inc(mqk_ready, 1)
            act.wait_ge(zT_done, 9)
            nc.scalar.activation(gates[:], banks(0, 16)[:, PT:PT + TZ], ACT.Identity, bias=bgate[:])

        @block.vector
        def _(dve):
            step = chained(dve, dve_step)
            dve.wait_ge(spread_loaded, 16 * 11)
            dve.wait_ge(cols_done, 1)
            nc.vector.tensor_copy(cols[:], banks(7)[:, 0:32]).then_inc(cols_ready, 1)
            nc.vector.tensor_scalar(gq[:], gq[:], QD ** -0.5, None, ALU.mult)
            nc.vector.tensor_scalar(gda[:], gda[:], 1.0 - LAM_INIT, None, ALU.mult)
            for i in range(2):
                step(nc.vector.tensor_tensor(lamv[:, 2 * i], lamv[:, 2 * i], lamv[:, 2 * i + 1], ALU.mult))
                ins = nc.vector.tensor_reduce(lam[:, i:i + 1], lamv[:, 2 * i], AX.X, ALU.add)
                step(ins) if i == 0 else ins.then_inc(lam_exp, 1)
            dve.wait_ge(lam_exp, 2)
            step(nc.vector.tensor_tensor(lam[:, 2:3], lam[:, 1:2], lam[:, 0:1], ALU.subtract))
            step(nc.vector.tensor_scalar(lam[:, 3:4], lam[:, 2:3], -LAM_INIT, None, ALU.add))
            dve.wait_ge(cols_ready, 1)
            gm = cols[:, 24:32].unsqueeze(2)

            def read_xT(c):
                R = ZROWS[c]
                dve.wait_ge(xT_done, c + 1)
                src = banks(2 * (c % 2))[:, 0:D].rearrange("p (k t) -> p k t", k=KD)[:, :, 0:R]
                nc.vector.tensor_tensor(hT[:, :, ZCOL[c]:ZCOL[c] + R], src, gm.to_broadcast([P, KD, R]),
                                        ALU.mult).then_inc(hT_ready, 1)

            def norm_qk(i):
                n, c = divmod(i, NZ)
                R = ZROWS[c]
                c5 = 0 if c == 0 else 1 + (c - 1) % 4
                g = (gq, gk)[n]
                dve.wait_ge(sq_ready, i + 1)
                if i >= 2:
                    dve.wait_ge(rstd_ready, i - 1)
                s8 = ss8[0:R, i % 2, :]
                nc.vector.tensor_reduce(s8, sq[0:R, :].rearrange("p (j d) -> p j d", d=QD), AX.X,
                                        ALU.add).then_inc(ss_ready, 1)
                q = qn[i % 3][0:R, :].rearrange("p (j d) -> p j d", d=QD)
                z = banks(4 + i % 3, R)[:, 0:512].rearrange("p (j d) -> p j d", d=QD)
                dve.wait_ge(rstd_ready, i + 1)
                if i >= 3:
                    dve.wait_ge(qkT_done, i - 2)
                ins = nc.vector.tensor_tensor(q, z, s8.unsqueeze(2).to_broadcast([R, 8, QD]), ALU.mult)
                ins.then_inc(z_read_dve, 1)
                dve.wait_ge(z_read_dve, i + 1)
                step(nc.vector.tensor_tensor(q, q, g[0:R, :].unsqueeze(1).to_broadcast([R, 8, QD]), ALU.mult))
                cc = cos2[0:R, c5, :].unsqueeze(1).to_broadcast([R, 8, ROPE])
                sn = sin2[0:R, c5, :].unsqueeze(1)
                half = ROPE // 2
                nc.vector.tensor_tensor(rt[0:R], q[:, :, 0:ROPE], cc, ALU.mult)
                nc.vector.tensor_tensor(rt2[0:R, :, 0:half], q[:, :, half:ROPE],
                                        sn[:, :, 0:half].to_broadcast([R, 8, half]), ALU.mult)
                step(nc.vector.tensor_tensor(rt2[0:R, :, half:ROPE], q[:, :, 0:half],
                                             sn[:, :, half:ROPE].to_broadcast([R, 8, half]), ALU.mult))
                nc.vector.tensor_tensor(q[:, :, 0:ROPE], rt[0:R], rt2[0:R], ALU.add).then_inc(qn_ready, 1)

            read_xT(0)
            for i in range(4 * NZ):
                n, c = divmod(i, NZ)
                if n == 0 and c + 1 < NZ:
                    read_xT(c + 1)
                if n < 2:
                    norm_qk(i)
                else:
                    R = ZROWS[c]
                    dve.wait_ge(z_done, i + 1)
                    if n == 2:
                        dst, src = V[0:R, c], banks(4 + i % 3, R)[:, 0:512]
                    else:
                        dst = MV[0:R, c, :, 0:HD]
                        src = banks(4 + i % 3, R)[:, 0:512].rearrange("p (h d) -> p h d", h=HEADS)
                    nc.vector.tensor_copy(dst, src).then_inc(z_read_dve, 1)
            dve.wait_ge(qkT_done, 2 * NZ)
            nc.vector.memset(zp[:, :, 0:1], 0.0)
            nc.vector.memset(zp[:, :, T + 1:T + 2], 0.0).then_inc(const_made, 1)
            for j in range(8):
                w = [cols[:, 8 * t + j:8 * t + j + 1] for t in range(3)]
                y = cy[j % 2]
                dve.wait_ge(zp_ready, j + 1)
                if j >= 2:
                    dve.wait_ge(mqk_ready, j - 1)
                step(nc.vector.tensor_scalar(y[:], zp[:, :, 0:T], w[0], None, ALU.mult))
                step(nc.vector.scalar_tensor_tensor(y[:], zp[:, :, 1:T + 1], w[1], y[:], ALU.mult, ALU.add))
                nc.vector.scalar_tensor_tensor(y[:], zp[:, :, 2:T + 2], w[2], y[:], ALU.mult,
                                               ALU.add).then_inc(cy_ready, 1)


def attention(nc, e):
    ident, gda, lam, gates, rowt, eps = (e[k] for k in "ident gda lam gates rowt eps".split())
    mixT, qT, kT, V = (e[k] for k in "mixT qT kT V".split())
    banks, base, sem = e["banks"], e["base"], e["sem"]
    tiles = Map(nc, base, A_W, A_S)
    prob = [[tiles(f"prob{i}{j}", [P, T]) for j in range(2)] for i in range(2)]
    diff = [tiles(f"diff{i}", [P, T]) for i in range(2)]
    diffT = [tiles(f"diffT{i}", [P, NC5, P]) for i in range(2)]
    osb = tiles("osb", [P, HALF])
    osq = tiles("osq", [P, HALF])
    on = tiles("on", [P, HALF])
    nmax = tiles("nmax", [P, 2, 2])
    lsum = tiles("lsum", [P, 2, 2])
    rcp = tiles("rcp", [P, 2, 2])
    so = tiles("so", [P, HEADS])
    gt_map = Map(nc, base, A_HT + HEADS * G * T * 4, A_W)
    gt = gt_map("gt", [8, 4, T])
    ga = gt_map("ga", [8, 2, T])
    gb = gt_map("gb", [8, 2, T])

    s_done, s_max, s_exp = sem("s_done"), sem("s_max"), sem("s_exp")
    a_ready, aT_done, aT_read = sem("a_ready"), sem("aT_done"), sem("aT_read")
    pv_done, o_read, osq_ready, so_ready, or_ready, on_ready, oT_done, oT_read = (
        sem(s) for s in "pv_done o_read osq_ready so_ready or_ready on_ready oT_done oT_read".split())
    gt_loaded, g_abs, g_exp, l_ready = sem("gt_loaded"), sem("g_abs"), sem("g_exp"), sem("l_ready")
    act_step, dve_step = sem("a_act_step"), sem("a_dve_step")
    row_ready = sem("row_ready")

    units = [(g, c, h) for g in range(G) for c in range(NC5) for h in range(HEADS)]
    N = len(units)
    LAST = N + 7

    with nc.Block() as block:

        @block.sync
        def _(sp):
            for k in range(4):
                for g in range(G):
                    src = gates[4 * k:4 * k + 4, :]
                    sp.dma_start(gt[4 * g:4 * g + 4, k, 0:N_META], src[:, 0:N_META]).then_inc(gt_loaded, 16)
                    a = N_META + SEQ * g
                    sp.dma_start(gt[4 * g:4 * g + 4, k, N_META:T], src[:, a:a + SEQ]).then_inc(gt_loaded, 16)

        @block.tensor
        def _(pe):
            def scores(i):
                g, c, h = units[i]
                R, a = CROWS[c], ZCOL[zc(g, c)]
                for j in range(2):
                    if i >= 1:
                        pe.wait_ge(s_exp, 2 * (i - 1) + j + 1)
                    for at, b, n in ((0, N_META + SEQ * g, SEQ), (SEQ, 0, N_META)):
                        mm = pe.matmul(banks(2 * j, R)[:, at:at + n], qT[QD * j:QD * j + QD, h, a:a + R],
                                       kT[QD * j:QD * j + QD, h, b:b + n], start=True, stop=True)
                    mm.then_inc(s_done, 1)

            def turn(i):
                R = CROWS[units[i][1]]
                pe.wait_ge(a_ready, i + 1)
                if i >= 1:
                    pe.wait_ge(aT_read, i)
                for k in range(NC5):
                    n = P if k < 4 else N_META
                    mm = pe.transpose(banks(4, n)[:, k * P:k * P + R], diff[i % 2][0:R, k * P:k * P + n], ident[0:R, 0:R])
                mm.then_inc(aT_done, 1)

            def values(i):
                g, c, h = units[i]
                R = CROWS[c]
                pe.wait_ge(aT_read, i + 1)
                if h == 0 and i > 0:
                    pe.wait_ge(o_read, i // 4)
                for k in range(NC5):
                    n = P if k < 4 else N_META
                    mm = pe.matmul(banks(6, R)[:, h * HD:(h + 1) * HD], diffT[i % 2][0:n, k, 0:R],
                                   V[0:n, zc(g, (k + 1) % NC5), h * HD:(h + 1) * HD], start=(k == 0), stop=(k == 4))
                mm.then_inc(pv_done, 1)

            def turn_out(t):
                R = CROWS[t % NC5]
                pe.wait_ge(on_ready, t + 1)
                if t >= 1:
                    pe.wait_ge(oT_read, t)
                for h in range(HEADS):
                    mm = pe.transpose(banks(7)[:, h * P:h * P + R], on[0:R, h * HD:(h + 1) * HD], ident[0:R, 0:R])
                mm.then_inc(oT_done, 1)

            for s in range(LAST):
                if s < N:
                    scores(s)
                if 1 <= s <= N:
                    turn(s - 1)
                if 2 <= s <= N + 1:
                    values(s - 2)
                if s >= 8 and s % 4 == 0 and (s - 8) // 4 < G * NC5:
                    turn_out((s - 8) // 4)

        @block.scalar
        def _(act):
            step = chained(act, act_step)
            act.preload_act_table_set(EXP_LN)

            def softmax(i):
                R = CROWS[units[i][1]]
                for j in range(2):
                    act.wait_ge(s_max, 2 * i + j + 1)
                    if i >= 2:
                        act.wait_ge(a_ready, i - 1)
                    nc.scalar.activation(prob[i % 2][j][0:R, :], banks(2 * j, R)[:, 0:T], ACT.Exp,
                                         bias=nmax[0:R, i % 2, j:j + 1],
                                         accum_out=lsum[0:R, i % 2, j:j + 1]).then_inc(s_exp, 1)

            def read_turned(i):
                R = CROWS[units[i][1]]
                act.wait_ge(aT_done, i + 1)
                if i >= 2:
                    act.wait_ge(pv_done, i - 1)
                src = banks(4)[:, 0:4 * P].rearrange("p (k t) -> p k t", k=4)[:, :, 0:R]
                nc.scalar.activation(diffT[i % 2][:, 0:4, 0:R], src, ACT.Copy)
                nc.scalar.activation(diffT[i % 2][0:N_META, 4, 0:R], banks(5, N_META)[:, 0:R],
                                     ACT.Copy).then_inc(aT_read, 1)

            def read_out(t):
                R = CROWS[t % NC5]
                act.wait_ge(pv_done, 4 * t + 4)
                if t >= 1:
                    act.wait_ge(on_ready, t)
                nc.scalar.activation(osb[0:R, :], banks(6, R)[:, 0:HALF], ACT.Copy).then_inc(o_read, 1)
                act.wait_ge(o_read, t + 1)
                nc.scalar.activation(osq[0:R, :], osb[0:R, :], ACT.Square).then_inc(osq_ready, 1)

            def rstd_out(t):
                R = CROWS[t % NC5]
                act.wait_ge(so_ready, t + 1)
                rms_rstd(nc, step, so[0:R, :], so[0:R, :], HD, eps[0:R, :]).then_inc(or_ready, 1)

            def store_out(t):
                R, a = CROWS[t % NC5], mixcol(*divmod(t, NC5))
                act.wait_ge(oT_done, t + 1)
                src = banks(7)[:, 0:HALF].rearrange("p (h t) -> p h t", h=HEADS)[:, :, 0:R]
                nc.scalar.activation(mixT[:, 0:HEADS, a:a + R], src, ACT.Copy).then_inc(oT_read, 1)

            for s in range(LAST + 2):
                t, r = divmod(s - 6, 4)
                if r == 0 and 0 <= t < G * NC5:
                    read_out(t)
                if r == 1 and 0 <= t < G * NC5:
                    rstd_out(t)
                if r == 3 and 0 <= t < G * NC5:
                    store_out(t)
                if s < N:
                    softmax(s)
                if 1 <= s <= N:
                    read_turned(s - 1)
                if s == 5:
                    act.wait_ge(g_abs, 1)
                    step(nc.scalar.activation(ga[:], ga[:], ACT.Exp, scale=-1.0))
                    nc.scalar.activation(ga[:], ga[:], ACT.Ln, bias=1.0).then_inc(g_exp, 1)

        @block.vector
        def _(dve):
            step = chained(dve, dve_step)
            f, li = gt[:, 1::2, :], gt[:, 0::2, :]

            def gates_magnitude():
                dve.wait_ge(gt_loaded, 16 * 16)
                step(nc.vector.tensor_scalar(ga[:], f, -1.0, None, ALU.mult))
                nc.vector.tensor_tensor(ga[:], ga[:], f, ALU.max).then_inc(g_abs, 1)
                dve.wait_ge(g_abs, 1)
                step(nc.vector.tensor_scalar(gb[:], f, 0.0, None, ALU.min))

            def gate_rows():
                dve.wait_ge(g_exp, 1)
                step(nc.vector.tensor_tensor(gb[:], gb[:], ga[:], ALU.subtract))
                step(nc.vector.memset(ga[:], 0.0))
                for d, order in ((0, slice(None)), (1, slice(None, None, -1))):
                    step(nc.vector.tensor_tensor_scan(rowt[:, d, order], gb[:, d, order], ga[:, d, order], 0.0, ALU.add, ALU.add))
                    step(nc.vector.tensor_tensor_scan(rowt[:, 4 + d, order], gb[:, d, order], li[:, d, order], 0.0, ALU.add, ALU.max))
                step(nc.vector.tensor_tensor(rowt[:, 2:4], li, rowt[:, 0:2], ALU.subtract))
                step(nc.vector.tensor_tensor(rowt[:, 0:2], rowt[:, 0:2], rowt[:, 4:6], ALU.subtract))

            def maxima(i):
                R = CROWS[units[i][1]]
                for j in range(2):
                    dve.wait_ge(s_done, 2 * i + j + 1)
                    nc.vector.tensor_reduce(nmax[0:R, i % 2, j:j + 1], banks(2 * j, R)[:, 0:T], AX.X, ALU.max,
                                            negate=True).then_inc(s_max, 1)

            def combine(i):
                R = CROWS[units[i][1]]
                dve.wait_ge(s_exp, 2 * i + 2)
                r = rcp[0:R, i % 2]
                step(nc.vector.reciprocal(r, lsum[0:R, i % 2]))
                step(nc.vector.tensor_tensor(r[:, 1:2], r[:, 1:2], lam[0:R, 3:4], ALU.mult))
                if i >= 2:
                    dve.wait_ge(aT_done, i - 1)
                p0, p1 = (prob[i % 2][j][0:R, :] for j in range(2))
                step(nc.vector.tensor_scalar(diff[i % 2][0:R, :], p0, r[:, 0:1], None, ALU.mult))
                nc.vector.scalar_tensor_tensor(diff[i % 2][0:R, :], p1, r[:, 1:2], diff[i % 2][0:R, :], ALU.mult,
                                               ALU.add).then_inc(a_ready, 1)

            def sum_out(t):
                R = CROWS[t % NC5]
                dve.wait_ge(osq_ready, t + 1)
                nc.vector.tensor_reduce(so[0:R, :], osq[0:R, :].rearrange("p (h d) -> p h d", h=HEADS), AX.X,
                                        ALU.add).then_inc(so_ready, 1)

            def norm_out(t):
                R = CROWS[t % NC5]
                dve.wait_ge(or_ready, t + 1)
                if t >= 1:
                    dve.wait_ge(oT_done, t)
                o, y = (x[0:R, :].rearrange("p (h d) -> p h d", h=HEADS) for x in (osb, on))
                step(nc.vector.tensor_tensor(y, o, so[0:R, :].unsqueeze(2).to_broadcast([R, HEADS, HD]), ALU.mult))
                nc.vector.tensor_tensor(y, y, gda[0:R, :].unsqueeze(1).to_broadcast([R, HEADS, HD]),
                                        ALU.mult).then_inc(on_ready, 1)

            for s in range(LAST):
                if s < N:
                    maxima(s)
                t, r = divmod(s - 6, 4)
                if r == 0 and 0 <= t < G * NC5:
                    sum_out(t)
                if r == 1 and 0 <= t < G * NC5:
                    norm_out(t)
                if s < N:
                    combine(s)
                if s == 4:
                    gates_magnitude()
                if s == 8:
                    gate_rows()


def mlstm(nc, e):
    ident, causal, gml, rowt, colt, eps = (e[k] for k in "ident causal gml rowt colt eps".split())
    mixT, MO, MV, MQK = (e[k] for k in "mixT MO MV MQK".split())
    banks, base, sem = e["banks"], e["base"], e["sem"]
    weights = Map(nc, base, A_Q, A_MO)
    pw = [[weights(f"pw{i}{d}", [P, NC5, T]) for d in range(2)] for i in range(2)]
    diag = [weights(f"diag{i}", [P, 2, P]) for i in range(2)]
    em = weights("em", [P, 2, NC5, 8])
    den = weights("den", [P, 8])
    sh = weights("sh", [P, 2, HEADS])
    hsq = weights("hsq", [P, HALF])
    late = Map(nc, base, A_W, A_S)
    ew = [[late(f"ew{i}{d}", [P, T]) for d in range(2)] for i in range(2)]
    spr = [late(f"spr{i}", [P, 2, T]) for i in range(2)]
    hm = late("hm", [P, NC5, HALF])
    hn = [late(f"hn{i}", [P, HALF]) for i in range(2)]

    col_done, col_ready = sem("col_done"), sem("col_ready")
    a_done, spr_ready, s_done, p_ready = sem("m_a_done"), sem("m_spr_ready"), sem("m_s_done"), sem("m_p_ready")
    diag_ready, ew_ready = sem("m_diag_ready"), sem("m_ew_ready")
    n_done, n_read = sem("m_n_done"), sem("m_n_read")
    hsq_ready, sh_ready, hr_ready, hn_ready, hT_done, hT_read = (
        sem(s) for s in "hsq_ready sh_ready hr_ready hn_ready hmT_done hmT_read".split())
    act_step, dve_step = sem("m_act_step"), sem("m_dve_step")

    units = [(g, h) for g in range(G) for h in range(HEADS)]
    N = NC5 * len(units)
    outs = [n for n in range(N) if units[n // NC5][1] == HEADS - 1]
    LAST = N + 11

    def where(n):
        u, c = divmod(n, NC5)
        return u, c, CROWS[c], CCOL[c]

    with nc.Block() as block:

        @block.tensor
        def _(pe):
            for k in range(4):
                for c in range(NC5):
                    at = (k * NC5 + c) * 8
                    mm = pe.transpose(banks(7, CROWS[c])[:, at:at + 8], rowt[:, 2 + k, CCOL[c]:CCOL[c] + CROWS[c]],
                                      ident[0:8, 0:8])
            mm.then_inc(col_done, 1)

            def spread(u):
                if u >= 1:
                    pe.wait_ge(spr_ready, u)
                for d in range(2):
                    for at, a, n in ((PT, 0, N_META), (512, N_META, SEQ)):
                        mm = pe.matmul(banks(2 * d)[:, at:at + n], ident[0:8, u:u + 1].to_broadcast([8, P]),
                                       rowt[:, d, a:a + n], start=True, stop=True)
                mm.then_inc(a_done, 1)

            def scores(n):
                u, c, R, t = where(n)
                g, h = units[u]
                if n >= 1:
                    pe.wait_ge(p_ready, n)
                for at, a, w in ((PT, 0, N_META), (512, N_META, SEQ)):
                    mm = pe.matmul(banks(4, R)[:, at:at + w], MQK[:, HEADS + h, g, t:t + R], MQK[:, h, g, a:a + w],
                                   start=True, stop=True)
                mm.then_inc(s_done, 1)

            def sums(n):
                u, c, R, t = where(n)
                g, h = units[u]
                pe.wait_ge(p_ready, NC5 * (u + 1))
                if n >= 1:
                    pe.wait_ge(n_read, n)
                for d, over in ((0, range(0, c + 1)), (1, range(c, NC5))):
                    for s in over:
                        mm = pe.matmul(banks(6, R)[:, d * (HD + 1):(d + 1) * (HD + 1)], pw[u % 2][d][0:CROWS[s], s, t:t + R],
                                       MV[0:CROWS[s], zc(g, s), h], start=(s == over[0]), stop=(s == over[-1]))
                mm.then_inc(n_done, 1)

            def turn_out(o):
                R = CROWS[o % NC5]
                pe.wait_ge(hn_ready, o + 1)
                if o >= 1:
                    pe.wait_ge(hT_read, o)
                else:
                    pe.wait_ge(col_ready, 2)
                for h in range(HEADS):
                    mm = pe.transpose(banks(7)[:, h * P:h * P + R], hn[o % 2][0:R, h * HD:(h + 1) * HD], ident[0:R, 0:R])
                mm.then_inc(hT_done, 1)

            for s in range(LAST):
                if s < N:
                    if s % NC5 == 0:
                        spread(s // NC5)
                    scores(s)
                if 0 <= s - NC5 < N:
                    sums(s - NC5)
                if s - 9 in outs:
                    turn_out(outs.index(s - 9))

        @block.scalar
        def _(act):
            step = chained(act, act_step)
            act.preload_act_table_set(EXP_LN)
            act.wait_ge(col_done, 1)
            for k, dst in ((0, colt), (2, em)):
                for c in range(NC5):
                    R = CROWS[c]
                    src = banks(7, R)[:, 0:4 * NC5 * 8].rearrange("p (k c u) -> p k c u", k=4, c=NC5)[:, k:k + 2, c]
                    ins = nc.scalar.activation(dst[0:R, 0:2, c], src, ACT.Copy if k == 0 else ACT.Exp,
                                               scale=1.0 if k == 0 else -1.0)
                ins.then_inc(col_ready, 1)
            act.wait_ge(col_ready, 2)

            def weigh(n):
                u, c, R, t = where(n)
                if c == 0:
                    act.wait_ge(a_done, u + 1)
                    if u >= 2:
                        act.wait_ge(diag_ready, NC5 * (u - 1))
                    for d in range(2):
                        ins = nc.scalar.activation(spr[u % 2][:, d], banks(2 * d)[:, PT:PT + T], ACT.Copy)
                    ins.then_inc(spr_ready, 1)
                    act.wait_ge(spr_ready, u + 1)
                a = spr[u % 2]
                if n >= 2:
                    act.wait_ge(p_ready, n - 1)
                f, b = ew[n % 2]
                if c < NC5 - 1:
                    nc.scalar.activation(f[0:R, t + R:T], a[0:R, 0, t + R:T], ACT.Exp, bias=colt[0:R, 0, c, u:u + 1])
                if c > 0:
                    nc.scalar.activation(b[0:R, 0:t], a[0:R, 1, 0:t], ACT.Exp, bias=colt[0:R, 1, c, u:u + 1])
                act.wait_ge(diag_ready, n + 1)
                for d, w in enumerate((f, b)):
                    ins = nc.scalar.activation(w[0:R, t:t + R], diag[n % 2][0:R, d, 0:R], ACT.Exp)
                ins.then_inc(ew_ready, 1)

            def square_out(o):
                R, c = CROWS[o % NC5], o % NC5
                act.wait_ge(n_read, outs[o] + 1)
                if o >= 1:
                    act.wait_ge(sh_ready, o)
                nc.scalar.activation(hsq[0:R, :], hm[0:R, c], ACT.Square).then_inc(hsq_ready, 1)

            def rstd_out(o):
                R = CROWS[o % NC5]
                act.wait_ge(sh_ready, o + 1)
                rms_rstd(nc, step, sh[0:R, o % 2], sh[0:R, o % 2], HD, eps[0:R, :]).then_inc(hr_ready, 1)

            def store_out(o):
                R, a = CROWS[o % NC5], mixcol(*divmod(o, NC5))
                act.wait_ge(hT_done, o + 1)
                src = banks(7)[:, 0:HALF].rearrange("p (h t) -> p h t", h=HEADS)[:, :, 0:R]
                nc.scalar.activation(mixT[:, HEADS:, a:a + R], src, ACT.Copy).then_inc(hT_read, 1)

            for s in range(LAST):
                if s < N:
                    weigh(s)
                if s - 7 in outs:
                    square_out(outs.index(s - 7))
                if s - 8 in outs:
                    rstd_out(outs.index(s - 8))
                if s - 10 in outs:
                    store_out(outs.index(s - 10))

        @block.vector
        def _(dve):
            step = chained(dve, dve_step)
            dve.wait_ge(col_ready, 2)

            def mask(n):
                u, c, R, t = where(n)
                dve.wait_ge(spr_ready, u + 1)
                if n >= 2:
                    dve.wait_ge(ew_ready, n - 1)
                for d in range(2):
                    ins = nc.vector.scalar_tensor_tensor(diag[n % 2][0:R, d, 0:R], spr[u % 2][0:R, d, t:t + R],
                                                         colt[0:R, d, c, u:u + 1], causal[0:R, d, 0:R], ALU.add, ALU.add)
                ins.then_inc(diag_ready, 1)

            def apply(n):
                u, c, R, t = where(n)
                dve.wait_ge(s_done, n + 1)
                dve.wait_ge(ew_ready, n + 1)
                if u >= 2:
                    dve.wait_ge(n_done, NC5 * (u - 1))
                for d, a, b in ((0, t, T), (1, 0, t + R)):
                    ins = nc.vector.scalar_tensor_tensor(pw[u % 2][d][0:R, c, a:b], banks(4, R)[:, PT + a:PT + b], HD ** -0.5,
                                                         ew[n % 2][d][0:R, a:b], ALU.mult, ALU.mult)
                ins.then_inc(p_ready, 1)

            def divide(n):
                u, c, R, t = where(n)
                h = units[u][1]
                s = banks(6, R)[:, 0:2 * (HD + 1)].rearrange("p (d w) -> p d w", d=2)
                dve.wait_ge(n_done, n + 1)
                d = den[0:R, :]
                step(nc.vector.tensor_copy(d[:, 0:2], s[:, :, HD]))
                step(nc.vector.scalar_tensor_tensor(d[:, 2:4], d[:, 0:2], -1.0, d[:, 0:2], ALU.mult, ALU.max))
                step(nc.vector.tensor_tensor(d[:, 4:6], d[:, 2:4], em[0:R, :, c, u], ALU.max))
                step(nc.vector.reciprocal(d[:, 6:8], d[:, 4:6]))
                out = hm[0:R, c, h * HD:(h + 1) * HD]
                step(nc.vector.tensor_scalar(out, s[:, 0, 0:HD], d[:, 6:7], None, ALU.mult))
                nc.vector.scalar_tensor_tensor(out, s[:, 1, 0:HD], d[:, 7:8], out, ALU.mult, ALU.add).then_inc(n_read, 1)

            def sum_out(o):
                R = CROWS[o % NC5]
                dve.wait_ge(hsq_ready, o + 1)
                if o >= 2:
                    dve.wait_ge(hr_ready, o - 1)
                nc.vector.tensor_reduce(sh[0:R, o % 2], hsq[0:R, :].rearrange("p (h d) -> p h d", h=HEADS), AX.X,
                                        ALU.add).then_inc(sh_ready, 1)

            def norm_out(o):
                g, c = divmod(o, NC5)
                R = CROWS[c]
                dve.wait_ge(hr_ready, o + 1)
                if o >= 2:
                    dve.wait_ge(hT_done, o - 1)
                y = hn[o % 2][0:R, :]
                y4 = y.rearrange("p (h d) -> p h d", h=HEADS)
                x4 = hm[0:R, c].rearrange("p (h d) -> p h d", h=HEADS)
                step(nc.vector.tensor_tensor(y4, x4, sh[0:R, o % 2].unsqueeze(2).to_broadcast([R, HEADS, HD]), ALU.mult))
                step(nc.vector.tensor_tensor(y4, y4, gml[0:R, :].unsqueeze(1).to_broadcast([R, HEADS, HD]), ALU.mult))
                nc.vector.tensor_tensor(y, y, MO[0:R, zc(g, c)], ALU.mult).then_inc(hn_ready, 1)

            for s in range(LAST):
                if s < N:
                    mask(s)
                if 0 <= s - 6 < N:
                    divide(s - 6)
                if s < N:
                    apply(s)
                if s - 7 in outs:
                    sum_out(outs.index(s - 7))
                if s - 8 in outs:
                    norm_out(outs.index(s - 8))


NGU, ND = 3, 4


def weight_groups(nc, e):
    ring = Map(nc, e["base"], A_Q, A_END)
    gu = [ring(f"wgu{i}", [P, 2, KD, 256]) for i in range(NGU)]
    down = [ring(f"wd{i}", [P, 2, D]) for i in range(ND)]
    whi = [ring(f"whi{i}", [P, 2, KD, P], F32R) for i in range(2)]
    return gu, down, whi


def gu_slot(j):
    return j % NGU


def load_group(eng, e, rings, loaded, expert, j, part):
    gu, down = rings[0][gu_slot(j)], rings[1][j % ND]
    if "gu" in part:
        for i, w in enumerate((e["w_gate"], e["w_up"])):
            src = w[0, bass.ds(expert, 1), :, 256 * j:256 * (j + 1)].rearrange("o (k p) f -> (o p) k f", p=P)
            eng.dma_start(gu[:, i], src).then_inc(loaded[gu_slot(j)], 16)
    if "d" in part:
        src = e["w_down"][0, bass.ds(expert, 1), 256 * j:256 * (j + 1), :].rearrange("o (c p) d -> (o p) c d", p=P)
        eng.dma_start(down[:], src).then_inc(loaded[NGU + j % ND], 16)


def project_out(nc, e):
    ident, eps, wo, mixT = (e[k] for k in "ident eps wo mixT".split())
    banks, base, sem, rings, loaded = e["banks"], e["base"], e["sem"], e["rings"], e["loaded"]
    AFF = e["AFF"]
    tiles = Map(nc, base, A_X, A_END)
    x = [tiles(f"xr{i}", [P, D]) for i in range(2)]
    x2 = [tiles(f"x2{i}", [P, D]) for i in range(2)]
    xn = [tiles(f"xn{i}", [P, D]) for i in range(2)]
    xnT = [tiles(f"xnT{i}", [P, KD, P]) for i in range(2)]
    junk = tiles("junk", [P, D])
    gffn = tiles("gffn", [P, D])
    wr = tiles("wr", [P, KD, N_EXP])
    sx = tiles("sx", [P, 2, 2])
    ex = tiles("ex", [P, 2, 2, N_EXP])
    mx = tiles("mx", [P, 2, 2, 4])

    chunks = [(None, 0)] + [(g, c) for g in range(G) for c in range(1, NC5)]
    rows = [2 * N_META] + [P] * (NZ - 1)
    col = [0] + [mixcol(g, c) for g, c in chunks[1:]]

    def dram_rows(i):
        if i == 0:
            return [(slice(N_META * g, N_META * (g + 1)), slice(T * g, T * g + N_META)) for g in range(G)]
        g, c = chunks[i]
        return [(slice(0, P), slice(T * g + CCOL[c], T * g + CCOL[c] + P))]

    def x_rows(i):
        if i == 0:
            return [(slice(N_META * g, N_META * (g + 1)), e["x_meta"]) for g in range(G)]
        g, c = chunks[i]
        return [(slice(0, P), e[("x_prompt", "x_sample")[g]][0, P * (c - 1):P * c, :])]

    wo_loaded = [sem(f"wo_loaded{k}") for k in range(KD)]
    x_loaded = [sem(f"xr_loaded{i}") for i in range(2)]
    gffn_loaded, wr_loaded = sem("gffn_loaded"), sem("wr_loaded")
    o_done, x2_ready, sx_ready, xs_ready, xn_ready = (sem(s) for s in "o_done x2_ready sx_ready xsc_ready xn_ready".split())
    x2_stored = [sem(f"x2_stored{i}") for i in range(2)]
    xn_stored = [sem(f"xn_stored{i}") for i in range(2)]
    t_done, t_read, r_done, r_max, r_exp, r_ready = (sem(s) for s in "xnT_done xnT_read r_done r_max r_exp r_ready".split())
    act_step, dve_step = sem("o_act_step"), sem("o_dve_step")

    def loads(i):
        return 16 * (i // 2 + 1 + (1 if i % 2 == 0 else 0))

    with nc.Block() as block:

        @block.sync
        def _(sp):
            wo_rows = e["w_out"].rearrange("o (k p) n -> (o p) k n", p=P)
            for k in range(KD):
                sp.dma_start(wo[:, k], wo_rows[:, k]).then_inc(wo_loaded[k], 16)
                if k == 0:
                    for i in range(2):
                        for r, src in x_rows(i):
                            sp.dma_start(x[i][r, :], src).then_inc(x_loaded[i], 16)
            sp.dma_start(wr[:], e["w_router"].rearrange("o (k p) n -> (o p) k n", p=P)).then_inc(wr_loaded, 16)
            for j in range(3):
                load_group(sp, e, rings, loaded, 0, j, "gu d")
            for i in range(NZ):
                sp.wait_ge(x2_ready, i + 1)
                for r, d in dram_rows(i):
                    sp.dma_start(e["out"][d, :], x2[i % 2][r, :]).then_inc(x2_stored[i % 2], 16)
                if i + 2 < NZ:
                    for r, src in x_rows(i + 2):
                        sp.dma_start(x[i % 2][r, :], src).then_inc(x_loaded[i % 2], 16)
                sp.wait_ge(xn_ready, i + 1)
                for r, d in dram_rows(i):
                    sp.dma_start(e["xn_rows"][d, :], xn[i % 2][r, :]).then_inc(xn_stored[i % 2], 16)
            for i in range(2):
                last = NZ - 1 - (NZ - 1 - i) % 2
                sp.wait_ge(x2_stored[i], loads(last))
                sp.wait_ge(xn_stored[i], loads(last))

        @block.gpsimd
        def _(pool):
            pool.dma_start(gffn[:], e["g_ffn"].to_broadcast([P, D])).then_inc(gffn_loaded, 16)

        @block.tensor
        def _(pe):
            def product(i):
                R = rows[i]
                if i >= 2:
                    pe.wait_ge(x2_ready, i - 1)
                for k in range(KD):
                    if i == 0:
                        pe.wait_ge(wo_loaded[k], 16)
                    for n in range(2):
                        mm = pe.matmul(banks(2 * (i % 2) + n, R)[:, 0:512], mixT[:, k, col[i]:col[i] + R],
                                       wo[:, k, 512 * n:512 * (n + 1)], start=(k == 0), stop=(k == KD - 1))
                mm.then_inc(o_done, 1)

            def turn(i):
                R = rows[i]
                pe.wait_ge(xn_ready, i + 1)
                if i >= 1:
                    pe.wait_ge(t_read, i)
                for k in range(KD):
                    mm = pe.transpose(banks(4)[:, k * P:k * P + R], xn[i % 2][0:R, k * P:(k + 1) * P], ident[0:R, 0:R])
                mm.then_inc(t_done, 1)

            def route(i):
                pe.wait_ge(t_read, i + 1)
                if i == 0:
                    pe.wait_ge(wr_loaded, 16)
                else:
                    pe.wait_ge(r_exp, i)
                for g, a, R in ([(0, 0, N_META), (1, N_META, N_META)] if i == 0 else [(0, 0, P)]):
                    for k in range(KD):
                        mm = pe.matmul(banks(6, R)[:, N_EXP * g:N_EXP * (g + 1)], xnT[i % 2][:, k, a:a + R], wr[:, k],
                                       start=(k == 0), stop=(k == KD - 1))
                mm.then_inc(r_done, 1)

            for s in range(NZ + 3):
                if s < NZ:
                    product(s)
                if 0 <= s - 2 < NZ:
                    turn(s - 2)
                if 0 <= s - 3 < NZ:
                    route(s - 3)

        @block.scalar
        def _(act):
            step = chained(act, act_step)
            act.preload_act_table_set(EXP_LN)

            def scale(i):
                R = rows[i]
                act.wait_ge(x2_ready, i + 1)
                s = sx[0:R, i % 2]
                step(nc.scalar.activation(junk[0:R, :], x2[i % 2][0:R, :], ACT.Square, accum_out=s[:, 0:1]))
                step(rms_rstd(nc, step, s[:, 0:1], s[:, 1:2], D, eps[0:R, :]))
                if i >= 2:
                    act.wait_ge(t_done, i - 1)
                    act.wait_ge(xn_stored[i % 2], loads(i - 2))
                nc.scalar.activation(xn[i % 2][0:R, :], x2[i % 2][0:R, :], ACT.Copy, scale=s[:, 1:2]).then_inc(xs_ready, 1)

            def exp(i):
                R, n = (N_META, 2) if i == 0 else (P, 1)
                act.wait_ge(r_max, i + 1)
                for g in range(n):
                    ins = nc.scalar.activation(ex[0:R, i % 2, g], banks(6, R)[:, N_EXP * g:N_EXP * (g + 1)], ACT.Exp,
                                               bias=mx[0:R, i % 2, g, 0:1], accum_out=mx[0:R, i % 2, g, 1:2])
                ins.then_inc(r_exp, 1)

            for s in range(NZ + 4):
                if s < NZ:
                    scale(s)
                if 0 <= s - 3 < NZ:
                    exp(s - 3)

        @block.vector
        def _(dve):
            step = chained(dve, dve_step)

            def add(i):
                R = rows[i]
                dve.wait_ge(o_done, i + 1)
                dve.wait_ge(x_loaded[i % 2], loads(i))
                if i >= 2:
                    dve.wait_ge(xs_ready, i - 1)
                    dve.wait_ge(x2_stored[i % 2], loads(i - 2))
                nc.vector.tensor_tensor(x2[i % 2][0:R, :], banks(2 * (i % 2), R)[:, 0:D], x[i % 2][0:R, :],
                                        ALU.add).then_inc(x2_ready, 1)

            def weight(i):
                R = rows[i]
                dve.wait_ge(xs_ready, i + 1)
                nc.vector.tensor_tensor(xn[i % 2][0:R, :], xn[i % 2][0:R, :], gffn[0:R, :], ALU.mult).then_inc(xn_ready, 1)

            def read_turned(i):
                R = rows[i]
                dve.wait_ge(t_done, i + 1)
                if i >= 2:
                    dve.wait_ge(r_done, i - 1)
                src = banks(4)[:, 0:D].rearrange("p (k t) -> p k t", k=KD)[:, :, 0:R]
                nc.vector.tensor_copy(xnT[i % 2][:, :, 0:R], src).then_inc(t_read, 1)

            def maxima(i):
                R, n = (N_META, 2) if i == 0 else (P, 1)
                dve.wait_ge(r_done, i + 1)
                for g in range(n):
                    ins = nc.vector.tensor_reduce(mx[0:R, i % 2, g, 0:1], banks(6, R)[:, N_EXP * g:N_EXP * (g + 1)], AX.X,
                                                  ALU.max, negate=True)
                ins.then_inc(r_max, 1)

            def softmax(i):
                R, n = (N_META, 2) if i == 0 else (P, 1)
                dve.wait_ge(r_exp, i + 1)
                for g in range(n):
                    m = mx[0:R, i % 2, g]
                    to, slot = (g, 0) if i == 0 else chunks[i]
                    step(nc.vector.reciprocal(m[:, 2:3], m[:, 1:2]))
                    ins = nc.vector.tensor_scalar(AFF[0:R, slot, N_EXP * to:N_EXP * (to + 1)], ex[0:R, i % 2, g], m[:, 2:3], None,
                                                  ALU.mult)
                ins.then_inc(r_ready, 1)

            dve.wait_ge(gffn_loaded, 16)
            for s in range(NZ + 4):
                if s < NZ:
                    add(s)
                    weight(s)
                if 0 <= s - 2 < NZ:
                    read_turned(s - 2)
                if 0 <= s - 3 < NZ:
                    maxima(s - 3)
                    softmax(s - 3)


def experts(nc, e):
    ident = e["ident"]
    AFF, rings, loaded, out, xn_rows = (e[k] for k in "AFF rings loaded out xn_rows".split())
    banks, base, sem = e["banks"], e["base"], e["sem"]
    wgu, wdown, whi = rings
    tiles = Map(nc, base, A_MOE, A_S)
    C2 = G * CAP
    RANKS = (CAP + 7) // 8 * 8
    JG = FF // 256
    M = FF // P
    PER_BANK = 3
    wlo = [tiles(f"wlo{i}", [P, 2, KD, P], BF16) for i in range(2)]
    xg = tiles("xg", [CAP, G, D])
    xT = tiles("xT", [P, KD, C2])
    xx = tiles("xx", [P, KD, 2 * C2], F32R)
    xb = tiles("xb", [P, KD, C2], BF16)
    low = [tiles(f"low{i}", [P, 2, C2]) for i in range(2)]
    gu = [tiles(f"gu{i}", [P, 2, C2]) for i in range(2)]
    sil = [tiles(f"sil{i}", [P, C2]) for i in range(2)]
    hid = [tiles(f"hid{i}", [P, C2]) for i in range(2)]
    yT = tiles("yT", [P, KD, C2])
    yr = tiles("yr", [CAP, G, D])
    work = [tiles(f"aff{i}", [G * N_EXP, T]) for i in range(2)]
    vals = tiles("vals", [G * N_EXP, RANKS])
    index = tiles("index", [G * N_EXP, RANKS], U32)
    indexf = tiles("indexf", [G * N_EXP, RANKS])
    gateT = tiles("gateT", [CAP, G, N_EXP])
    idxT = tiles("idxT", [CAP, G, N_EXP], U32)
    take = tiles("take", [CAP, G, 1], U32)
    give = tiles("give", [CAP, G, 1], U32)
    gate = tiles("gate", [CAP, G])

    aT_done, top_step, ranked, lists_done, lists_ready = (sem(s) for s in "affT_done top_step ranked lists_done lists_ready".split())
    take_ready, xg_loaded, xT_done, xT_ready, xh_ready, xb_ready, xl_ready = (
        sem(s) for s in "take_ready xg_loaded xgT_done xgT_ready xh_ready xb_ready xl_ready".split())
    hi_ready, lo_ready, gu_done, low_ready, sum_ready, sil_ready, hid_ready, d_done = (
        sem(s) for s in "hi_ready lo_ready gu_done low_ready sum_ready sil_ready hid_ready d_done".split())
    yT_ready, y_done, yr_ready = (sem(s) for s in "yT_ready yt_done yr_ready".split())
    give_free, give_ready, added = (sem(s) for s in "give_free give_ready added".split())

    OUT_STEPS = {2: 0, 3: 1, 4: 2, 5: 3}
    ROW_STEPS = {10: range(0, 3), 11: range(3, 6), 12: range(6, 8)}
    TURN = 7

    def y_tile(k):
        at = (k % PER_BANK) * C2
        return banks(4 + k // PER_BANK)[:, at:at + C2]

    def last_user(slots, ex, j):
        if j >= slots:
            return JG * ex + j - slots
        if isinstance(ex, int) and ex == 0:
            return None
        return JG * (ex - 1) + max(i for i in range(JG) if i % slots == j)

    def uses(slots, ex, j):
        return len(range(j % slots, JG, slots)) * ex + j // slots + 1

    def per_expert(eng, body):
        body(0, True, False)
        with eng.Fori(1, N_EXP - 1) as ex:
            body(ex, False, False)
        body(N_EXP - 1, False, True)

    def ahead(ex, m, last):
        if m + 2 < M:
            return ex, m + 2
        return None if last else (ex + 1, m + 2 - M)

    with nc.Block() as block:

        @block.sync
        def _(sp):
            def body(ex, first, last):
                for j in range(3 if first else 0, JG):
                    before = last_user(NGU, ex, j)
                    sp.wait_ge(lo_ready, 2 * before + 2)
                    load_group(sp, e, rings, loaded, ex, j, "gu")
                    before = last_user(ND, ex, j)
                    if before is not None:
                        sp.wait_ge(d_done, 2 * before + 2)
                    load_group(sp, e, rings, loaded, ex, j, "d")

            per_expert(sp, body)
            sp.wait_ge(added, 32 * N_EXP)

        @block.gpsimd
        def _(pool):
            def fetch(ex):
                pool.wait_ge(take_ready, ex + 1)
                for g in range(G):
                    nc.gpsimd.indirect_dma_start(xg[:, g, :], None, xn_rows,
                                                 bass.IndirectOffsetOnAxis(ap=take[:, g, :], axis=0)).then_inc(xg_loaded, 16)

            def add_rows(ex, first):
                if not first:
                    pool.wait_ge(added, 32 * ex)
                pool.sem_inc(give_free, 1)
                pool.wait_ge(yr_ready, 4 * ex + 4)
                for g in range(G):
                    nc.gpsimd.indirect_dma_start(out, bass.IndirectOffsetOnAxis(ap=give[:, g, :], axis=0), yr[:, g, :],
                                                 None, compute_op=ALU.add).then_inc(added, 16)

            fetch(0)
            fetch(1)
            add_rows(0, True)
            for ex in range(2, N_EXP):
                fetch(ex)
                add_rows(ex - 1, False)
            add_rows(N_EXP - 1, False)

        @block.tensor
        def _(pe):
            for c in range(NC5):
                at = PT + CCOL[c]
                mm = pe.transpose(banks(0, G * N_EXP)[:, at:at + CROWS[c]], AFF[0:CROWS[c], c], ident[0:CROWS[c], 0:CROWS[c]])
            mm.then_inc(aT_done, 1)
            pe.wait_ge(ranked, 1)
            for i, t in enumerate((vals, indexf)):
                mm = pe.transpose(banks(2, CAP)[:, 32 * i:32 * i + 32], t[:, 0:CAP], ident[0:G * N_EXP, 0:G * N_EXP])
            mm.then_inc(lists_done, 1)

            def turn_rows(ex, part, ks):
                if part == 0:
                    pe.wait_ge(xg_loaded, 32 * ex + 32)
                elif part > 0:
                    pe.wait_ge(xT_ready, 3 * ex + part)
                for k in ks:
                    for g in range(G):
                        at = (k - ks[0]) * C2 + CAP * g
                        mm = pe.transpose(banks(TURN)[:, at:at + CAP], xg[:, g, k * P:(k + 1) * P], ident[0:CAP, 0:CAP])
                mm.then_inc(xT_done, 1)

            def up(ex, m, first):
                pe.wait_ge(lo_ready, M * ex + m + 1)
                if not (first and m < 2):
                    pe.wait_ge(sum_ready, M * ex + m - 1)
                b = 2 * (m % 2)
                for i in range(2):
                    for k in range(KD):
                        pe.matmul(banks(b + i)[:, 0:2 * C2], whi[m % 2][:, i, k], xx[:, k], start=(k == 0), stop=False,
                                  skip_group_check=True)
                for i in range(2):
                    for k in range(KD):
                        mm = pe.matmul(banks(b + i)[:, 0:C2], wlo[m % 2][:, i, k], xb[:, k], start=False, stop=(k == KD - 1),
                                       skip_group_check=True)
                mm.then_inc(gu_done, 1)

            def down(ex, m):
                j, c = divmod(m, 2)
                if c == 0:
                    pe.wait_ge(loaded[NGU + j % ND], 16 * uses(ND, ex, j))
                pe.wait_ge(hid_ready, M * ex + m + 1)
                for k in range(KD):
                    mm = pe.matmul(y_tile(k), wdown[j % ND][:, c, k * P:(k + 1) * P], hid[m % 2][:],
                                   start=(m == 0 and k % PER_BANK == 0), stop=(m == M - 1), skip_group_check=True)
                mm.then_inc(d_done, 1)

            def turn_outputs(ex, i, first_use):
                g, half = divmod(i, 2)
                if i > 0:
                    pe.wait_ge(yr_ready, 4 * ex + i)
                elif not first_use:
                    pe.wait_ge(xT_ready, 3 * ex + 6)
                for k in range(4):
                    mm = pe.transpose(banks(TURN, CAP)[:, k * P:(k + 1) * P], yT[:, 4 * half + k, CAP * g:CAP * (g + 1)], ident[:])
                mm.then_inc(y_done, 1)

            def body(ex, first, last):
                pe.wait_ge(xl_ready, ex + 1)
                pe.wait_ge(xb_ready, ex + 1)
                for m in range(M):
                    up(ex, m, first)
                    if m == 1 and not first:
                        pe.wait_ge(yT_ready, ex)
                    if m >= 1:
                        down(ex, m - 1)
                    if m in OUT_STEPS and not first:
                        turn_outputs(ex - 1, OUT_STEPS[m], False)
                    if m in ROW_STEPS and not last:
                        part = m - min(ROW_STEPS)
                        if part == 0 and not first:
                            pe.wait_ge(yr_ready, 4 * ex)
                        turn_rows(ex + 1, part, ROW_STEPS[m])
                down(ex, M - 1)

            for part, ks in enumerate(ROW_STEPS.values()):
                turn_rows(0, part, ks)
            per_expert(pe, body)
            pe.wait_ge(yT_ready, N_EXP)
            for i in range(4):
                turn_outputs(N_EXP - 1, i, True)

        @block.scalar
        def _(act):
            act.preload_act_table_set("silu_and_others")

            def split_high(ex, m):
                j, c = divmod(m, 2)
                if c == 0:
                    act.wait_ge(loaded[gu_slot(j)], 32 * uses(NGU, ex, j))
                if not (isinstance(ex, int) and ex == 0 and m < 2):
                    act.wait_ge(gu_done, M * ex + m - 1)
                nc.scalar.activation(whi[m % 2][:], wgu[gu_slot(j)][:, :, :, c * P:(c + 1) * P], ACT.Copy).then_inc(hi_ready, 1)

            def split_rows(ex, first):
                act.wait_ge(xT_ready, 3 * ex + 3)
                if not first:
                    act.wait_ge(gu_done, M * ex)
                nc.scalar.activation(xx[:, :, 0:C2], xT[:], ACT.Copy).then_inc(xh_ready, 1)
                nc.scalar.activation(xb[:], xT[:], ACT.Copy).then_inc(xb_ready, 1)

            def gated_rows(ex, i):
                if i == 0:
                    act.wait_ge(give_ready, ex + 1)
                g, half = divmod(i, 2)
                act.wait_ge(y_done, 4 * ex + i + 1)
                nc.scalar.activation(yr[:, g, 512 * half:512 * (half + 1)], banks(TURN, CAP)[:, 0:512], ACT.Copy,
                                     scale=gate[:, g:g + 1]).then_inc(yr_ready, 1)

            def body(ex, first, last):
                for m in range(M):
                    n = M * ex + m + 1
                    b = 2 * (m % 2)
                    act.wait_ge(gu_done, n)
                    src = banks(b)[:, 0:1024].rearrange("p (i n) -> p i n", i=2)
                    nc.scalar.activation(low[m % 2][:], src[:, :, C2:2 * C2], ACT.Copy).then_inc(low_ready, 1)
                    then = ahead(ex, m, last)
                    if m == M - 1:
                        act.wait_ge(sum_ready, n)
                        nc.scalar.activation(sil[m % 2][:], gu[m % 2][:, 0], ACT.Silu).then_inc(sil_ready, 1)
                        if not last:
                            split_rows(ex + 1, False)
                    if then:
                        split_high(*then)
                    if m < M - 1:
                        act.wait_ge(sum_ready, n)
                        nc.scalar.activation(sil[m % 2][:], gu[m % 2][:, 0], ACT.Silu).then_inc(sil_ready, 1)
                    if m in OUT_STEPS and not first:
                        gated_rows(ex - 1, OUT_STEPS[m])
                act.wait_ge(d_done, M * ex + M)
                two = banks(4)[:, 0:1024].rearrange("p (b n) -> p b n", b=2)[:, :, 0:PER_BANK * C2]
                nc.scalar.activation(yT[:, 0:6].rearrange("p (b k) n -> p b (k n)", b=2), two, ACT.Copy)
                nc.scalar.activation(yT[:, 6:8], banks(6)[:, 0:2 * C2].rearrange("p (k n) -> p k n", k=2),
                                     ACT.Copy).then_inc(yT_ready, 1)

            split_high(0, 0)
            split_high(0, 1)
            split_rows(0, True)
            per_expert(act, body)
            for i in range(4):
                gated_rows(N_EXP - 1, i)

        @block.vector
        def _(dve):
            step = chained(dve, top_step)

            def split_low(ex, m):
                j, c = divmod(m, 2)
                dve.wait_ge(hi_ready, M * ex + m + 1)
                nc.vector.tensor_tensor(wlo[m % 2][:], wgu[gu_slot(j)][:, :, :, c * P:(c + 1) * P], whi[m % 2][:].bitcast(F32),
                                        ALU.subtract).then_inc(lo_ready, 1)

            dve.wait_ge(aT_done, 1)
            step(nc.vector.tensor_copy(work[0][:], banks(0, G * N_EXP)[:, PT:PT + T]))
            for r in range(RANKS // 8):
                a, b, at = work[r % 2], work[(r + 1) % 2], slice(8 * r, 8 * r + 8)
                step(nc.vector.max(vals[:, at], a[:]))
                if r + 1 < RANKS // 8:
                    nc.vector.match_replace(b[:], vals[:, at], a[:], -1.0)
                step(nc.vector.max_index(index[:, at], vals[:, at], a[:]))
            nc.vector.tensor_copy(indexf[:], index[:]).then_inc(ranked, 1)
            dve.wait_ge(lists_done, 1)
            lists = banks(2, CAP)
            gates, tokens = (lists[:, a:a + 32].rearrange("p (g n) -> p g n", g=G) for a in (0, 32))
            for g in range(G):
                nc.vector.tensor_scalar(idxT[:, g], tokens[:, g], float(T * g), None, ALU.add).then_inc(lists_ready, 1)
            nc.vector.tensor_copy(gateT[:], gates).then_inc(lists_ready, 1)
            dve.wait_ge(lists_ready, 3)

            def pick(ex):
                nc.vector.tensor_copy(take[:], idxT[:, :, bass.ds(ex, 1)]).then_inc(take_ready, 1)

            def pick_out(ex):
                dve.wait_ge(give_free, ex + 1)
                nc.vector.tensor_copy(give[:], idxT[:, :, bass.ds(ex, 1)])
                nc.vector.tensor_copy(gate[:].unsqueeze(2), gateT[:, :, bass.ds(ex, 1)]).then_inc(give_ready, 1)

            def read_turned(ex, part, ks):
                dve.wait_ge(xT_done, 3 * ex + part + 1)
                if part == 0:
                    dve.wait_ge(xb_ready, ex) if not (isinstance(ex, int) and ex == 0) else None
                src = banks(TURN)[:, 0:len(ks) * C2].rearrange("p (k n) -> p k n", n=C2)
                nc.vector.tensor_copy(xT[:, ks[0]:ks[-1] + 1], src).then_inc(xT_ready, 1)

            def split_rows(ex):
                dve.wait_ge(xh_ready, ex + 1)
                nc.vector.tensor_tensor(xx[:, :, C2:2 * C2], xT[:], xx[:, :, 0:C2].bitcast(F32), ALU.subtract).then_inc(xl_ready, 1)

            def body(ex, first, last):
                for m in range(M):
                    n = M * ex + m + 1
                    b = 2 * (m % 2)
                    dve.wait_ge(low_ready, n)
                    src = banks(b)[:, 0:1024].rearrange("p (i n) -> p i n", i=2)
                    nc.vector.tensor_tensor(gu[m % 2][:], src[:, :, 0:C2], low[m % 2][:], ALU.add).then_inc(sum_ready, 1)
                    dve.wait_ge(sil_ready, n)
                    nc.vector.tensor_tensor(hid[m % 2][:], sil[m % 2][:], gu[m % 2][:, 1], ALU.mult).then_inc(hid_ready, 1)
                    if m == M - 1 and not last:
                        split_rows(ex + 1)
                    then = ahead(ex, m, last)
                    if then:
                        split_low(*then)
                    if m == 0:
                        if not last:
                            pick(ex + 1)
                        if not first:
                            pick_out(ex - 1)
                    if m in ROW_STEPS and not last:
                        read_turned(ex + 1, m - min(ROW_STEPS), ROW_STEPS[m])

            pick(0)
            split_low(0, 0)
            split_low(0, 1)
            for part, ks in enumerate(ROW_STEPS.values()):
                read_turned(0, part, ks)
            split_rows(0)
            per_expert(dve, body)
            pick_out(N_EXP - 1)


_INS = ["x_prompt", "x_sample", "meta", "g_mix", "w_in", "b_gates", "conv_w", "g_q", "g_k", "lam_q1", "lam_k1",
        "lam_q2", "lam_k2", "g_da_out", "g_ml_out", "w_out", "g_ffn", "w_router", "w_gate", "w_up", "w_down",
        "rope_cos", "rope_sin"]


def kernel(**inputs):
    import numpy as np
    import concourse.bacc as bacc
    from concourse.bass_utils import run_bass_kernel_spmd

    inputs["rope_cos"], inputs["rope_sin"] = rope_tables(np)
    nc = bacc.Bacc("TRN2", target_bir_lowering=False, num_devices=1)
    arrays, a = {}, {}
    for name in _INS:
        arrays[f"in_{name}"] = np.ascontiguousarray(inputs[name])
        a[name] = nc.dram_tensor(f"in_{name}", arrays[f"in_{name}"].shape, F32, kind="ExternalInput").ap()
    out = nc.dram_tensor("out_rows", (G * T, D), F32, kind="ExternalOutput").ap()
    xn_rows = nc.dram_tensor("xn_rows", (G * T, D), F32, kind="Internal").ap()
    build(nc, a["meta"], a["x_prompt"], a["x_sample"], a["g_mix"], a["w_in"], a["b_gates"], a["conv_w"], a["g_q"],
          a["g_k"], [a["lam_q1"], a["lam_k1"], a["lam_q2"], a["lam_k2"]], a["g_da_out"], a["g_ml_out"], a["w_out"],
          a["g_ffn"], a["w_router"], a["w_gate"], a["w_up"], a["w_down"], a["rope_cos"], a["rope_sin"], out, xn_rows)
    rows = run_bass_kernel_spmd(nc, [arrays], core_ids=[0]).results[0]["out_rows"]
    rows = rows.reshape(G, 1, T, D)[:, :, N_META:]
    return rows[0], rows[1]
```

```python
import math
from contextlib import ExitStack

import concourse.bass as bass
from concourse import mybir
from concourse.alu_op_type import AluOpType as ALU

F32 = mybir.dt.float32
F32R = mybir.dt.float32r
BF16 = mybir.dt.bfloat16
U32 = mybir.dt.uint32
ACT = mybir.ActivationFunctionType
AX = mybir.AxisListType
P = 128

N_META = 16
SEQ = 512
G = 2
T = N_META + SEQ
TZ = N_META + G * SEQ
D = 1024
KD = D // P
HALF = D // 2
HEADS = 4
HD = HALF // HEADS
QD = HD // 2
ROPE = QD // 4
ROPE_THETA = 500000.0
EPS = 1e-6
LAM_INIT = 0.8 - 0.6 * math.exp(0.0)
NEG = -1e30
EXP_LN = "natural_log_exp_and_others"
N_EXP = 16
CAP = 2 * T // N_EXP
FF = 2816
D_IN = 3600
OFF_MQK, OFF_MV, OFF_MO, OFF_GATES = 3 * HALF, 5 * HALF, 6 * HALF, 7 * HALF

ZROWS = [N_META] + [P] * (G * SEQ // P)
ZCOL = [0] + [N_META + P * i for i in range(G * SEQ // P)]
NZ = len(ZROWS)
CROWS = [N_META] + [P] * (SEQ // P)
CCOL = [0] + [N_META + P * i for i in range(SEQ // P)]
NC5 = len(CROWS)
PT = 512 - N_META
PH = 512 - T // 2
HALVES = ((PH, 0, T // 2), (512, T // 2, T))
PZ = 512 - (TZ - 512) // 2 // 16 * 16 - N_META
THIRDS = ((PZ, 0, 512 - PZ), (512, 512 - PZ, 1024 - PZ), (1024, 1024 - PZ, TZ))


def kcol(c):
    return SEQ if c == 0 else ZCOL[c] - (N_META if c <= SEQ // P else 0)


def zc(g, c):
    return 0 if c == 0 else 1 + (SEQ // P) * g + c - 1


def mixcol(g, c):
    return N_META * g if c == 0 else 2 * N_META + SEQ * g + P * (c - 1)


A_HT = 0
A_W = A_HT + KD * G * T * 4
A_S = A_W + 2 * KD * 512 * 4
A_Q = A_S + 23744
A_V = A_Q + 2 * HEADS * TZ * 4
A_MO = A_V + NZ * HALF * 4
A_MV = A_MO + NZ * HALF * 4
A_QK = A_MV + (NZ * HEADS * (HD + 1) * 4 + 31) // 32 * 32
A_END = A_QK + 2 * HEADS * G * T * 4
NW = 6
A_WO = A_Q + 2 * KD * 256 * 4
A_MOE = A_HT


class Map:

    def __init__(self, nc, base, at, end):
        self.nc, self.base, self.at, self.end = nc, base, at, end

    def __call__(self, name, shape, dt=F32):
        n = 4
        for s in shape[1:]:
            n *= s
        assert self.at + n <= self.end, (name, self.at + n, self.end)
        t = self.nc.alloc_sbuf_tensor_at(name, shape, dt, offset=self.base + self.at)
        self.at += (n + 31) // 32 * 32
        return t

    def both(self, name, shape):
        at = self.at
        whole = self(name, shape)
        self.at = at
        return whole, self(name + "_lo", shape, F32R)


def rope_tables(np):
    inv = ROPE_THETA ** (-np.arange(0, ROPE, 2, dtype=np.float32) / np.float32(ROPE))
    ang = np.arange(T, dtype=np.float32)[:, None] * inv.astype(np.float32)[None, :]
    cos, sin = (np.zeros((P, NC5, ROPE), np.float32) for _ in range(2))
    for c in range(NC5):
        a = ang[CCOL[c]:CCOL[c] + CROWS[c]]
        cos[:len(a), c] = np.concatenate([np.cos(a), np.cos(a)], 1)
        sin[:len(a), c] = np.concatenate([-np.sin(a), np.sin(a)], 1)
    return cos, sin


def build(nc, x_meta, x_prompt, x_sample, g_mix, w_in, b_gates, conv_w, g_q, g_k, lams, g_da, g_ml,
          w_out, g_ffn, w_router, w_gate, w_up, w_down, rope_cos, rope_sin, out, xn_rows, zv_rows, stages=5):
    with ExitStack() as ctx:
        base = (nc.sbuf_base + 31) // 32 * 32
        assert base + A_END <= nc.sbuf_usable_end, (base, A_END, nc.sbuf_usable_end)
        keep = Map(nc, base, A_S, A_Q)
        ident = keep("ident", [P, P])
        causal = keep("causal", [P, 2, P])
        cos2 = keep("cos2", [P, NC5, ROPE])
        sin2 = keep("sin2", [P, NC5, ROPE])
        gq = keep("gq", [P, QD])
        gk = keep("gk", [P, QD])
        gda = keep("gda", [P, HD])
        gml = keep("gml", [P, HD])
        cols = keep("cols", [P, 32])
        lamv = keep("lamv", [P, 4, QD])
        lam = keep("lam", [P, 4])
        bgate = keep("bgate", [16, 1])
        eps = keep("eps", [P, 1])
        wgates, wgates_lo = keep.both("wgates", [P, KD, 16])
        wgates_hi = keep("wgates_hi", [P, KD, 16], F32R)
        gates = keep("gates", [16, TZ])
        rows_at = keep.at
        rowt = keep("rowt", [8, 6, T])
        colt = keep("colt", [P, 4, NC5, 8])

        def sem(name):
            return ctx.enter_context(nc.semaphore(name))

        act_step, dve_step, pool_step = ((sem(f"{name}_step"), [0]) for name in ("act", "dve", "pool"))
        mv_loaded, mo_loaded = sem("mv_loaded"), sem("mo_loaded")

        h_map = Map(nc, base, A_HT, A_S)
        h_hi = h_map("h_hi", [P, KD, TZ], F32R)
        h_whole, h_lo = h_map.both("h", [P, KD, TZ])
        w_map = Map(nc, base, A_V, A_QK)
        w_hi = [w_map(f"w_hi{i}", [P, 2, 512], F32R) for i in range(NW)]
        w_whole, w_lo = zip(*[w_map.both(f"w{i}", [P, 2, 512]) for i in range(NW)])
        mixT, mix_lo = Map(nc, base, A_HT, A_W).both("mixT", [P, KD, G * T])
        qk_map = Map(nc, base, A_Q, A_V)
        qT, q_lo = qk_map.both("qT", [P, HEADS, TZ])
        kT, k_lo = qk_map.both("kT", [P, HEADS, TZ])
        high_map = Map(nc, base, A_MO, A_QK)
        q_hi = high_map("q_hi", [P, HEADS, TZ], F32R)
        k_hi = high_map("k_hi", [P, HEADS, TZ], F32R)
        V = Map(nc, base, A_V, A_MO)("V", [P, NZ, HALF])
        MO = Map(nc, base, A_MO, A_MV)("MO", [P, NZ, HALF])
        MV = Map(nc, base, A_MV, A_QK)("MV", [P, NZ, HEADS, HD + 1])
        MQK = Map(nc, base, A_QK, A_END)("MQK", [P, 2 * HEADS, G, T])

        ps = ctx.enter_context(nc.psum_tensor("ps", [P, 8, 512], F32))
        psf = ps[:].rearrange("p b n -> p (b n)")

        def banks(a, rows=P):
            return psf[0:rows, 512 * a:]

        project(nc, locals())
        if stages >= 2:
            attention(nc, locals())
        wo, wo_lo = Map(nc, base, A_QK, A_END).both("wo", [P, KD, D])
        wo_loaded = [sem(f"wo_loaded{k}") for k in range(KD)]
        if stages >= 3:
            mlstm(nc, locals())
        if stages >= 4:
            late = Map(nc, base, rows_at, A_Q)
            AFF = late("AFF", [P, NC5, G * N_EXP])
            loaded = [sem(f"group_loaded{i}") for i in range(NGU + ND)]
            rings = weight_groups(nc, locals())
            project_out(nc, locals())
        if stages >= 5:
            experts(nc, locals())


def rms_rstd(nc, step, ss, rstd, n, eps):
    step(nc.scalar.activation(rstd, ss, ACT.Ln, bias=eps, scale=1.0 / n))
    return nc.scalar.activation(rstd, rstd, ACT.Exp, scale=-0.5)


def chained(eng, steps):
    sem, count = steps

    def step(ins):
        count[0] += 1
        ins.then_inc(sem, 1)
        eng.wait_ge(sem, count[0])

    return step


def project(nc, e):
    ident, causal, cos2, sin2, gq, gk, gda, gml, cols = (e[k] for k in "ident causal cos2 sin2 gq gk gda gml cols".split())
    lamv, lam, bgate, eps, wgates, gates = (e[k] for k in "lamv lam bgate eps wgates gates".split())
    h_whole, h_hi, h_lo, w_whole, w_hi, w_lo = (e[k] for k in "h_whole h_hi h_lo w_whole w_hi w_lo".split())
    qT, kT, MQK, wgates_hi, wgates_lo = (e[k] for k in "qT kT MQK wgates_hi wgates_lo".split())
    banks, base, sem = e["banks"], e["base"], e["sem"]
    early = Map(nc, base, A_QK, A_END)
    xin = [early(f"xin{i}", [P, D]) for i in range(3)]
    xs = [early(f"xs{i}", [P, D]) for i in range(2)]
    sq = early("sq", [P, 512])
    qn = [early(f"qn{i}", [P, 512]) for i in range(3)]
    rt = early("rt", [P, 8, ROPE])
    rt2 = early("rt2", [P, 8, ROPE])
    ss = early("ss", [P, 2 * NZ])
    ss8 = early("ss8", [P, 2, 8])
    rowsin = early("rowsin", [32, P])
    conv = Map(nc, base, e["rows_at"], A_Q)
    zp = conv("zp", [P, G, T + 2])
    cy = [conv(f"cy{i}", [P, G, T]) for i in range(2)]

    x_loaded = [sem(f"x_loaded{i}") for i in range(3)]
    w_loaded = [sem(f"w_loaded{i}") for i in range(NW)]
    z_stored = [sem(f"z_stored{i}") for i in range(3)]
    w_high, w_low_dve, w_low, w_used = (sem(s) for s in "w_high w_low_dve w_low w_used".split())
    h_turned, h_high, h_low, wg_high, wg_low = (sem(s) for s in "h_turned h_high h_low wg_high wg_low".split())
    small_loaded, spread_loaded = sem("small_loaded"), sem("spread_loaded")
    const_made = sem("const_made")
    wg_loaded = sem("wg_loaded")
    xs_ready, xT_done = sem("xs_ready"), sem("xT_done")
    cols_done, cols_ready = sem("cols_done"), sem("cols_ready")
    z_done, z_read_dve, z_read_act = sem("z_done"), sem("z_read_dve"), sem("z_read_act")
    sq_ready, ss_ready, rstd_ready = sem("sq_ready"), sem("ss_ready"), sem("rstd_ready")
    qn_ready, qkT_done, qkT_read = sem("qn_ready"), sem("qkT_done"), sem("qkT_read")
    zT_done, zp_ready, cy_ready, mqk_ready = (sem(s) for s in "zT_done zp_ready cy_ready mqk_ready".split())
    act_step, dve_step = e["act_step"], e["dve_step"]
    lam_exp = sem("lam_exp")

    w_cols = e["w_in"].rearrange("o (k p) n -> (o p) k n", p=P)
    blocks = [0, HALF, 2 * HALF, OFF_MV, OFF_MO, OFF_MQK, OFF_MQK + HALF]
    N_TOK = 5
    UB = KD // 2
    UNITS = UB * len(blocks)
    N_QK = 2 * NZ

    def load_w(sp, u):
        if u >= NW:
            n, r = divmod(u - NW, UB)
            if r == UB - 1:
                sp.wait_ge(z_done, NZ * (n + 1))
            else:
                sp.wait_ge(w_used, (UB - 1) * n + r + 1)
        n, r = divmod(u, UB)
        sp.dma_start(w_whole[u % NW][:], w_cols[:, 2 * r:2 * r + 2, blocks[n]:blocks[n] + 512]).then_inc(w_loaded[u % NW], 16)

    def wait_split(pe, u):
        if u < UB:
            pe.wait_ge(w_low_dve, u + 1)
        else:
            pe.wait_ge(w_low, u - UB + 1)

    def wait_stage(eng, i):
        if i - N_QK < 3:
            eng.wait_ge(qkT_done, N_QK)
        else:
            eng.wait_ge(z_stored[i % 3], 16 * ((i - N_QK) // 3))

    def split_low(engine, w):
        return engine.tensor_tensor(w_lo[w][:], w_whole[w][:], w_hi[w][:].bitcast(F32), ALU.subtract)
    xsrc = [e["x_meta"]] + [e[n][0, P * i:P * (i + 1), :] for n in ("x_prompt", "x_sample") for i in range(SEQ // P)]

    def z_wait(pe, i):
        j = i - 3
        if j < 0:
            return
        if j < 4 * NZ:
            pe.wait_ge(z_read_dve, j + 1)
        else:
            pe.wait_ge(z_read_act, j - 4 * NZ + 1)

    with nc.Block() as block:

        @block.sync
        def _(sp):
            sp.dma_start(xin[0][0:ZROWS[0], :], xsrc[0]).then_inc(x_loaded[0], 16)
            sp.dma_start(rowsin[0:24, :], e["conv_w"].rearrange("o k (j p) -> (o k j) p", p=P)).then_inc(small_loaded, 16)
            sp.dma_start(rowsin[24:32, :], e["g_mix"].rearrange("o (j p) -> (o j) p", p=P)).then_inc(small_loaded, 16)
            sp.dma_start(xin[1][:], xsrc[1]).then_inc(x_loaded[1], 16)
            for u in range(UB):
                load_w(sp, u)
            sp.dma_start(xin[2][:], xsrc[2]).then_inc(x_loaded[2], 16)
            for c in range(3, NZ):
                sp.wait_ge(xs_ready, c - 2)
                sp.dma_start(xin[c % 3][:], xsrc[c]).then_inc(x_loaded[c % 3], 16)
                if c == 4:
                    for u in range(UB, NW):
                        load_w(sp, u)
            sp.dma_start(wgates[:], w_cols[:, :, OFF_GATES:D_IN]).then_inc(wg_loaded, 16)
            u = NW
            for n in range(N_TOK):
                for c in range(NZ):
                    if c == NZ - 1:
                        for _ in range(min(UB, UNITS - u)):
                            load_w(sp, u)
                            u += 1
                    if n >= 2:
                        sp.wait_ge(z_read_dve, NZ * n + c + 1) if n < 4 else sp.wait_ge(z_read_act, c + 1)
                        src, to = qn[(NZ * n + c) % 3][0:ZROWS[c], :], e["zv_rows"][n - 2, ZCOL[c]:ZCOL[c] + ZROWS[c], :]
                        sp.dma_start(to, src).then_inc(z_stored[(NZ * n + c) % 3], 16)
            while u < UNITS:
                load_w(sp, u)
                u += 1
            for i in range(3):
                sp.wait_ge(z_stored[i], 16 * NZ)

        @block.gpsimd
        def _(pool):
            nc.gpsimd.memset(ident[:], 0.0).then_inc(const_made, 1)
            nc.gpsimd.memset(causal[:], 0.0).then_inc(const_made, 1)
            nc.gpsimd.memset(eps[:], EPS).then_inc(const_made, 1)
            pool.wait_ge(const_made, 3)
            nc.gpsimd.affine_select(out=ident[:], in_=ident[:], compare_op=ALU.not_equal, fill=1.0, base=0,
                                    pattern=[[-1, P]], channel_multiplier=1).then_inc(const_made, 1)
            nc.gpsimd.affine_select(out=causal[:, 0], in_=causal[:, 0], compare_op=ALU.is_ge, fill=NEG, base=0,
                                    pattern=[[1, P]], channel_multiplier=-1).then_inc(const_made, 1)
            nc.gpsimd.affine_select(out=causal[:, 1], in_=causal[:, 1], compare_op=ALU.is_ge, fill=NEG, base=0,
                                    pattern=[[-1, P]], channel_multiplier=1).then_inc(const_made, 1)
            for dst, src in ((gq, e["g_q"]), (gk, e["g_k"]), (gda, e["g_da"]), (gml, e["g_ml"])):
                pool.dma_start(dst[:], src.to_broadcast([P, src.shape[1]])).then_inc(spread_loaded, 16)
            for i, src in enumerate(e["lams"]):
                pool.dma_start(lamv[:, i], src.to_broadcast([P, QD])).then_inc(spread_loaded, 16)
            pool.dma_start(bgate[:], e["b_gates"].rearrange("o n -> n o")).then_inc(spread_loaded, 16)
            pool.dma_start(cos2[:], e["rope_cos"]).then_inc(spread_loaded, 16)
            pool.dma_start(sin2[:], e["rope_sin"]).then_inc(spread_loaded, 16)

            def low_h(c):
                whole, hi, lo = (x[:, :, ZCOL[c]:ZCOL[c] + ZROWS[c]] for x in (h_whole, h_hi, h_lo))
                pool.wait_ge(h_high, c + 1)
                nc.gpsimd.tensor_tensor(lo, whole, hi.bitcast(F32), ALU.subtract).then_inc(h_low, 1)

            def low_w(u):
                pool.wait_ge(w_high, u + 1)
                split_low(nc.gpsimd, u % NW).then_inc(w_low, 1)

            for c in range(NZ):
                low_h(c)
            for u in range(UB, NW):
                low_w(u)
            pool.wait_ge(wg_high, 1)
            nc.gpsimd.tensor_tensor(wgates_lo[:], wgates[:], wgates_hi[:].bitcast(F32), ALU.subtract).then_inc(wg_low, 1)
            for u in range(NW, UNITS):
                low_w(u)

        @block.tensor
        def _(pe):
            pe.wait_ge(const_made, 6)
            pe.wait_ge(small_loaded, 32)
            pe.transpose(banks(7)[:, 0:32], rowsin[:], ident[0:32, 0:32]).then_inc(cols_done, 1)

            def turn_x(c):
                pe.wait_ge(xs_ready, c + 1)
                if c >= 2:
                    pe.wait_ge(h_turned, c - 1)
                for k in range(KD):
                    mm = pe.transpose(banks(2 * (c % 2))[:, k * P:k * P + ZROWS[c]],
                                      xs[c % 2][0:ZROWS[c], k * P:(k + 1) * P], ident[0:ZROWS[c], 0:ZROWS[c]])
                mm.then_inc(xT_done, 1)

            def turn_qk(i):
                R = ZROWS[i % NZ]
                pe.wait_ge(qn_ready, i + 1)
                if i >= 1:
                    pe.wait_ge(qkT_read, i)
                else:
                    pe.wait_ge(cols_ready, 1)
                for h in range(HEADS):
                    mm = pe.transpose(banks(7)[:, h * P:h * P + R], qn[i % 3][0:R, h * P:(h + 1) * P], ident[0:R, 0:R])
                mm.then_inc(qkT_done, 1)

            turn_x(0)
            turn_x(1)
            for i in range(N_TOK * NZ):
                n, c = divmod(i, NZ)
                if n == 0 and c + 2 < NZ:
                    turn_x(c + 2)
                if n == 0:
                    pe.wait_ge(h_low, c + 1)
                z_wait(pe, i)
                at = slice(ZCOL[c], ZCOL[c] + ZROWS[c])
                for k in range(KD):
                    u = UB * n + k // 2
                    if c == 0 and k % 2 == 0:
                        wait_split(pe, u)
                    wh, wl = w_hi[u % NW][:, k % 2], w_lo[u % NW][:, k % 2]
                    for i3, (h, w) in enumerate(((h_hi[:, k, at], wh), (h_hi[:, k, at], wl), (h_lo[:, k, at], wh))):
                        mm = pe.matmul(banks(4 + i % 3, ZROWS[c])[:, 0:512], h, w, start=(k == 0 and i3 == 0),
                                       stop=(k == KD - 1 and i3 == 2))
                    if c == NZ - 1 and k in range(1, KD - 1, 2):
                        mm.then_inc(w_used, 1)
                mm.then_inc(z_done, 1)
                if 2 <= i < 2 * NZ + 2:
                    turn_qk(i - 2)
            pe.wait_ge(qkT_read, 2 * NZ)
            z_wait(pe, N_TOK * NZ + 2)
            pe.wait_ge(z_read_dve, 4 * NZ)
            for j in range(2 * HEADS + 1):
                n = 5 + j // 4
                if j == 8:
                    pe.wait_ge(wg_low, 1)
                if j >= 2:
                    pe.wait_ge(zp_ready, j - 1)
                M = P if j < 8 else 16
                for k in range(KD):
                    if j < 8:
                        u = UB * n + k // 2
                        if j % 4 == 0 and k % 2 == 0:
                            wait_split(pe, u)
                        wh, wl = (w[u % NW][:, k % 2, (j % 4) * P:(j % 4 + 1) * P] for w in (w_hi, w_lo))
                    else:
                        wh, wl = wgates_hi[:, k], wgates_lo[:, k]
                    for i3, (w, h) in enumerate(((wh, h_hi), (wh, h_lo), (wl, h_hi))):
                        for at, a, b in THIRDS:
                            mm = pe.matmul(banks(3 * (j % 2), M)[:, at:at + b - a], w, h[:, k, a:b],
                                           start=(k == 0 and i3 == 0), stop=(k == KD - 1 and i3 == 2))
                    if j == 3 and k in range(1, KD - 1, 2):
                        mm.then_inc(w_used, 1)
                mm.then_inc(zT_done, 1)

        @block.scalar
        def _(act):
            step = chained(act, act_step)
            act.preload_act_table_set(EXP_LN)
            act.wait_ge(const_made, 3)

            def norm_x(c):
                R = ZROWS[c]
                act.wait_ge(x_loaded[c % 3], 16 * (c // 3 + 1))
                if c >= 2:
                    act.wait_ge(xT_done, c - 1)
                step(nc.scalar.activation(xs[c % 2][0:R, :], xin[c % 3][0:R, :], ACT.Square,
                                          accum_out=ss[0:R, c:c + 1]))
                r = ss[0:R, NZ + c:NZ + c + 1]
                step(rms_rstd(nc, step, ss[0:R, c:c + 1], r, D, eps[0:R, :]))
                nc.scalar.activation(xs[c % 2][0:R, :], xin[c % 3][0:R, :], ACT.Copy, scale=r).then_inc(xs_ready, 1)

            def square_qk(i):
                R = ZROWS[i % NZ]
                act.wait_ge(z_done, i + 1)
                if i >= 1:
                    act.wait_ge(ss_ready, i)
                nc.scalar.activation(sq[0:R, :], banks(4 + i % 3, R)[:, 0:512], ACT.Square).then_inc(sq_ready, 1)

            def rstd_qk(i):
                R = ZROWS[i % NZ]
                act.wait_ge(ss_ready, i + 1)
                s = ss8[0:R, i % 2, :]
                rms_rstd(nc, step, s, s, QD, eps[0:R, :]).then_inc(rstd_ready, 1)

            def read_qkT(i):
                n, c = divmod(i, NZ)
                R = ZROWS[c]
                act.wait_ge(qkT_done, i + 1)
                src = banks(7)[:, 0:512].rearrange("p (h t) -> p h t", h=HEADS)[:, :, 0:R]
                a = kcol(c) if n else ZCOL[c]
                nc.scalar.activation((qT, kT)[n][:, :, a:a + R], src, ACT.Copy).then_inc(qkT_read, 1)

            def high_h(c):
                act.wait_ge(h_turned, c + 1)
                at = slice(ZCOL[c], ZCOL[c] + ZROWS[c])
                nc.scalar.activation(h_hi[:, :, at], h_whole[:, :, at], ACT.Copy).then_inc(h_high, 1)

            def high_w(u):
                act.wait_ge(w_loaded[u % NW], 16 * (u // NW + 1))
                nc.scalar.activation(w_hi[u % NW][:], w_whole[u % NW][:], ACT.Copy).then_inc(w_high, 1)

            def high_ahead(n, c):
                u = {2: 0, 4: 1, 8: 2}.get(c)
                if u is not None and n + 1 < len(blocks):
                    high_w(UB * (n + 1) + u)

            norm_x(0)
            norm_x(1)
            high_h(0)
            for u in range(UB):
                high_w(u)
            norm_x(2)
            high_h(1)
            for i in range(2 * NZ + 2):
                n, c = divmod(i, NZ)
                if i + 3 < NZ:
                    norm_x(i + 3)
                if i + 2 < NZ:
                    high_h(i + 2)
                if i == NZ - 2:
                    act.wait_ge(wg_loaded, 16)
                    nc.scalar.activation(wgates_hi[:], wgates[:], ACT.Copy).then_inc(wg_high, 1)
                if i < 2 * NZ:
                    high_ahead(n, c)
                    square_qk(i)
                    if c == NZ - 1:
                        high_w(UB * (n + 1) + 3)
                    rstd_qk(i)
                if i >= 2:
                    read_qkT(i - 2)
            act.wait_ge(lam_exp, 1)
            nc.scalar.activation(lam[:, 0:2], lam[:, 0:2], ACT.Exp).then_inc(lam_exp, 1)
            for i in range(2 * NZ, 5 * NZ):
                n, c = divmod(i, NZ)
                high_ahead(n, c)
                if n == 4:
                    act.wait_ge(z_done, i + 1)
                    wait_stage(act, i)
                    nc.scalar.activation(qn[i % 3][0:ZROWS[c], :], banks(4 + i % 3, ZROWS[c])[:, 0:512],
                                         ACT.Sigmoid).then_inc(z_read_act, 1)
                if c == NZ - 1:
                    high_w(UB * (n + 1) + 3)
            for i in range(3):
                act.wait_ge(z_stored[i], 16 * NZ)
            for j in range(8):
                if 1 <= j <= 3:
                    high_w(UB * 6 + j - 1)
                if j == 4:
                    high_w(UB * 6 + 3)
                b = banks(3 * (j % 2))
                act.wait_ge(zT_done, j + 1)
                if j >= 1:
                    act.wait_ge(cy_ready, j)
                else:
                    act.wait_ge(const_made, 7)
                nc.scalar.activation(zp[:, 0, 1:T + 1], b[:, PZ:PZ + T], ACT.Copy)
                nc.scalar.activation(zp[:, 1, 1:N_META + 1], b[:, PZ:PZ + N_META], ACT.Copy)
                nc.scalar.activation(zp[:, 1, N_META + 1:T + 1], b[:, PZ + T:PZ + TZ], ACT.Copy).then_inc(zp_ready, 1)
                act.wait_ge(cy_ready, j + 1)
                nc.scalar.activation(MQK[:, j], cy[j % 2][:], ACT.Silu).then_inc(mqk_ready, 1)
            act.wait_ge(zT_done, 9)
            act.wait_ge(spread_loaded, 16 * 11)
            nc.scalar.activation(gates[:], banks(0, 16)[:, PZ:PZ + TZ], ACT.Identity, bias=bgate[:])

        @block.vector
        def _(dve):
            step = chained(dve, dve_step)
            dve.wait_ge(cols_done, 1)
            nc.vector.tensor_copy(cols[:], banks(7)[:, 0:32]).then_inc(cols_ready, 1)
            dve.wait_ge(cols_ready, 1)
            gm = cols[:, 24:32].unsqueeze(2)

            def read_xT(c):
                R = ZROWS[c]
                dve.wait_ge(xT_done, c + 1)
                src = banks(2 * (c % 2))[:, 0:D].rearrange("p (k t) -> p k t", k=KD)[:, :, 0:R]
                nc.vector.tensor_tensor(h_whole[:, :, ZCOL[c]:ZCOL[c] + R], src, gm.to_broadcast([P, KD, R]),
                                        ALU.mult).then_inc(h_turned, 1)

            read_xT(0)
            for u in range(UB):
                dve.wait_ge(w_high, u + 1)
                split_low(nc.vector, u).then_inc(w_low_dve, 1)
            read_xT(1)
            dve.wait_ge(spread_loaded, 16 * 11)
            nc.vector.tensor_scalar(gq[:], gq[:], QD ** -0.5, None, ALU.mult)
            nc.vector.tensor_scalar(gda[:], gda[:], 1.0 - LAM_INIT, None, ALU.mult)
            for i in range(2):
                step(nc.vector.tensor_tensor(lamv[:, 2 * i], lamv[:, 2 * i], lamv[:, 2 * i + 1], ALU.mult))
                ins = nc.vector.tensor_reduce(lam[:, i:i + 1], lamv[:, 2 * i], AX.X, ALU.add)
                step(ins) if i == 0 else ins.then_inc(lam_exp, 1)

            def norm_qk(i):
                n, c = divmod(i, NZ)
                R = ZROWS[c]
                c5 = 0 if c == 0 else 1 + (c - 1) % 4
                g = (gq, gk)[n]
                dve.wait_ge(sq_ready, i + 1)
                if i >= 2:
                    dve.wait_ge(rstd_ready, i - 1)
                s8 = ss8[0:R, i % 2, :]
                nc.vector.tensor_reduce(s8, sq[0:R, :].rearrange("p (j d) -> p j d", d=QD), AX.X,
                                        ALU.add).then_inc(ss_ready, 1)
                q = qn[i % 3][0:R, :].rearrange("p (j d) -> p j d", d=QD)
                z = banks(4 + i % 3, R)[:, 0:512].rearrange("p (j d) -> p j d", d=QD)
                dve.wait_ge(rstd_ready, i + 1)
                if i >= 3:
                    dve.wait_ge(qkT_done, i - 2)
                ins = nc.vector.tensor_tensor(q, z, s8.unsqueeze(2).to_broadcast([R, 8, QD]), ALU.mult)
                ins.then_inc(z_read_dve, 1)
                dve.wait_ge(z_read_dve, i + 1)
                step(nc.vector.tensor_tensor(q, q, g[0:R, :].unsqueeze(1).to_broadcast([R, 8, QD]), ALU.mult))
                cc = cos2[0:R, c5, :].unsqueeze(1).to_broadcast([R, 8, ROPE])
                sn = sin2[0:R, c5, :].unsqueeze(1)
                half = ROPE // 2
                nc.vector.tensor_tensor(rt[0:R], q[:, :, 0:ROPE], cc, ALU.mult)
                nc.vector.tensor_tensor(rt2[0:R, :, 0:half], q[:, :, half:ROPE],
                                        sn[:, :, 0:half].to_broadcast([R, 8, half]), ALU.mult)
                step(nc.vector.tensor_tensor(rt2[0:R, :, half:ROPE], q[:, :, 0:half],
                                             sn[:, :, half:ROPE].to_broadcast([R, 8, half]), ALU.mult))
                nc.vector.tensor_tensor(q[:, :, 0:ROPE], rt[0:R], rt2[0:R], ALU.add).then_inc(qn_ready, 1)

            for i in range(4 * NZ):
                n, c = divmod(i, NZ)
                if n == 0 and c + 2 < NZ:
                    read_xT(c + 2)
                if n < 2:
                    norm_qk(i)
                else:
                    R = ZROWS[c]
                    dve.wait_ge(z_done, i + 1)
                    wait_stage(dve, i)
                    nc.vector.tensor_copy(qn[i % 3][0:R, :], banks(4 + i % 3, R)[:, 0:512]).then_inc(z_read_dve, 1)
            dve.wait_ge(lam_exp, 2)
            step(nc.vector.tensor_tensor(lam[:, 2:3], lam[:, 1:2], lam[:, 0:1], ALU.subtract))
            step(nc.vector.tensor_scalar(lam[:, 3:4], lam[:, 2:3], -LAM_INIT, None, ALU.add))
            nc.vector.memset(zp[:, :, 0:1], 0.0)
            nc.vector.memset(zp[:, :, T + 1:T + 2], 0.0).then_inc(const_made, 1)
            for j in range(8):
                w = [cols[:, 8 * t + j:8 * t + j + 1] for t in range(3)]
                y = cy[j % 2]
                dve.wait_ge(zp_ready, j + 1)
                if j >= 2:
                    dve.wait_ge(mqk_ready, j - 1)
                step(nc.vector.tensor_scalar(y[:], zp[:, :, 0:T], w[0], None, ALU.mult))
                step(nc.vector.scalar_tensor_tensor(y[:], zp[:, :, 1:T + 1], w[1], y[:], ALU.mult, ALU.add))
                nc.vector.scalar_tensor_tensor(y[:], zp[:, :, 2:T + 2], w[2], y[:], ALU.mult,
                                               ALU.add).then_inc(cy_ready, 1)


def attention(nc, e):
    ident, gda, lam, gates, rowt, eps = (e[k] for k in "ident gda lam gates rowt eps".split())
    mixT, qT, kT, V, MO, MV, zv_rows = (e[k] for k in "mixT qT kT V MO MV zv_rows".split())
    banks, base, sem = e["banks"], e["base"], e["sem"]
    tiles = Map(nc, base, A_W, A_S)
    prob = [[tiles(f"prob{i}{j}", [P, T]) for j in range(2)] for i in range(2)]
    diff = [tiles(f"diff{i}", [P, T]) for i in range(2)]
    diffT = [tiles(f"diffT{i}", [P, NC5, P]) for i in range(2)]
    osb = tiles("osb", [P, HALF])
    osq = tiles("osq", [P, HALF])
    on = tiles("on", [P, HALF])
    nmax = tiles("nmax", [P, 2, 2])
    lsum = tiles("lsum", [P, 2, 2])
    rcp = tiles("rcp", [P, 2, 2])
    so = tiles("so", [P, HEADS])
    gt_map = Map(nc, base, A_HT + HEADS * G * T * 4, A_W)
    gt = gt_map("gt", [8, 4, T])
    ga = gt_map("ga", [8, 2, T])
    gb = gt_map("gb", [8, 2, T])

    s_done, s_max, s_exp = sem("s_done"), sem("s_max"), sem("s_exp")
    a_ready, aT_done, aT_read = sem("a_ready"), sem("aT_done"), sem("aT_read")
    pv_done, o_read, osq_ready, so_ready, or_ready, on_ready, oT_done, oT_read = (
        sem(s) for s in "pv_done o_read osq_ready so_ready or_ready on_ready oT_done oT_read".split())
    gt_loaded, g_abs, g_exp = sem("gt_loaded"), sem("g_abs"), sem("g_exp")
    act_step, dve_step, pool_step = (e[k] for k in "act_step dve_step pool_step".split())
    v_loaded = [sem(f"v_loaded{g}") for g in range(G)]
    q_lo, k_lo, q_hi, k_hi, mv_loaded, mo_loaded = (e[k] for k in "q_lo k_lo q_hi k_hi mv_loaded mo_loaded".split())
    q_high, q_low, k_high, k_low = (sem(s) for s in "q_high q_low k_high k_low".split())

    units = [(g, c, h) for g in range(G) for c in range(NC5) for h in range(HEADS)]
    N = len(units)
    LAST = N + 8

    with nc.Block() as block:

        @block.sync
        def _(sp):
            def load_rows(dst, kind, done):
                src = zv_rows[kind]
                sp.dma_start(dst[0:N_META, 0], src[0:N_META, :]).then_inc(done[0], 16)
                for g in range(G):
                    a = N_META + SEQ * g
                    sp.dma_start(dst[:, 1 + 4 * g:5 + 4 * g],
                                 src[a:a + SEQ, :].rearrange("(c p) n -> p c n", p=P)).then_inc(done[g], 16)

            load_rows(V, 0, v_loaded)
            for k in range(4):
                for g in range(G):
                    src = gates[4 * k:4 * k + 4, :]
                    sp.dma_start(gt[4 * g:4 * g + 4, k, 0:N_META], src[:, 0:N_META]).then_inc(gt_loaded, 16)
                    a = N_META + SEQ * g
                    sp.dma_start(gt[4 * g:4 * g + 4, k, N_META:T], src[:, a:a + SEQ]).then_inc(gt_loaded, 16)
            sp.wait_ge(s_done, 2 * N)
            for c in range(NZ):
                src = zv_rows[1, ZCOL[c]:ZCOL[c] + ZROWS[c], :].rearrange("p (h d) -> p h d", h=HEADS)
                sp.dma_start(MV[0:ZROWS[c], c, :, 0:HD], src).then_inc(mv_loaded, 16)
            load_rows(MO, 2, [mo_loaded] * G)

        @block.gpsimd
        def _(pool):
            step = chained(pool, pool_step)

            def norm_out(t):
                R = CROWS[t % NC5]
                pool.wait_ge(or_ready, t + 1)
                if t >= 1:
                    pool.wait_ge(oT_done, t)
                o, y = (x[0:R, :].rearrange("p (h d) -> p h d", h=HEADS) for x in (osb, on))
                step(nc.gpsimd.tensor_tensor(y, o, so[0:R, :].unsqueeze(2).to_broadcast([R, HEADS, HD]), ALU.mult))
                nc.gpsimd.tensor_tensor(y, y, gda[0:R, :].unsqueeze(1).to_broadcast([R, HEADS, HD]),
                                        ALU.mult).then_inc(on_ready, 1)

            for h in range(HEADS):
                pool.wait_ge(k_high, h + 1)
                nc.gpsimd.tensor_tensor(k_lo[:, h], kT[:, h], k_hi[:, h].bitcast(F32), ALU.subtract).then_inc(k_low, 1)
            for t in range(G * NC5):
                norm_out(t)
            pool.wait_ge(s_done, 2 * N)
            step(nc.gpsimd.memset(MV[:, :, :, HD:HD + 1], 1.0))

        @block.tensor
        def _(pe):
            def scores(i):
                g, c, h = units[i]
                R, a = CROWS[c], ZCOL[zc(g, c)]
                if i < HEADS:
                    pe.wait_ge(q_low, h + 1)
                    pe.wait_ge(k_low, h + 1)
                for j in range(2):
                    if i >= 1:
                        pe.wait_ge(s_exp, 2 * (i - 1) + j + 1)
                    for i3, (q, k) in enumerate(((q_hi, k_hi), (q_hi, k_lo), (q_lo, k_hi))):
                        for at, b, end in HALVES:
                            mm = pe.matmul(banks(2 * j, R)[:, at:at + end - b], q[QD * j:QD * j + QD, h, a:a + R],
                                           k[QD * j:QD * j + QD, h, SEQ * g + b:SEQ * g + end], start=(i3 == 0),
                                           stop=(i3 == 2))
                    mm.then_inc(s_done, 1)

            def turn(i):
                g, c, _ = units[i]
                R = CROWS[c]
                pe.wait_ge(a_ready, i + 1)
                if i >= 1:
                    pe.wait_ge(aT_read, i)
                for k in range(NC5):
                    n, b = CROWS[(k + 1) % NC5], kcol(zc(g, (k + 1) % NC5)) - SEQ * g
                    mm = pe.transpose(banks(4, n)[:, k * P:k * P + R], diff[i % 2][0:R, b:b + n], ident[0:R, 0:R])
                mm.then_inc(aT_done, 1)

            def values(i):
                g, c, h = units[i]
                R = CROWS[c]
                pe.wait_ge(aT_read, i + 1)
                if c == 0 and h == 0:
                    pe.wait_ge(v_loaded[g], 32 if g == 0 else 16)
                if h == 0 and i > 0:
                    pe.wait_ge(o_read, i // 4)
                for k in range(NC5):
                    n = P if k < 4 else N_META
                    mm = pe.matmul(banks(6, R)[:, h * HD:(h + 1) * HD], diffT[i % 2][0:n, k, 0:R],
                                   V[0:n, zc(g, (k + 1) % NC5), h * HD:(h + 1) * HD], start=(k == 0), stop=(k == 4))
                mm.then_inc(pv_done, 1)

            def turn_out(t):
                R = CROWS[t % NC5]
                pe.wait_ge(on_ready, t + 1)
                if t >= 1:
                    pe.wait_ge(oT_read, t)
                for h in range(HEADS):
                    mm = pe.transpose(banks(7)[:, h * P:h * P + R], on[0:R, h * HD:(h + 1) * HD], ident[0:R, 0:R])
                mm.then_inc(oT_done, 1)

            for s in range(LAST):
                if s < N:
                    scores(s)
                if 2 <= s <= N + 1:
                    turn(s - 2)
                if 3 <= s <= N + 2:
                    values(s - 3)
                if s >= 10 and s % 4 == 2 and (s - 10) // 4 < G * NC5:
                    turn_out((s - 10) // 4)

        @block.scalar
        def _(act):
            step = chained(act, act_step)
            act.preload_act_table_set(EXP_LN)

            def softmax(i):
                R = CROWS[units[i][1]]
                for j in range(2):
                    act.wait_ge(s_max, 2 * i + j + 1)
                    if i >= 2:
                        act.wait_ge(a_ready, i - 1)
                    nc.scalar.activation(prob[i % 2][j][0:R, :], banks(2 * j, R)[:, PH:PH + T], ACT.Exp,
                                         bias=nmax[0:R, i % 2, j:j + 1],
                                         accum_out=lsum[0:R, i % 2, j:j + 1]).then_inc(s_exp, 1)

            def read_turned(i):
                R = CROWS[units[i][1]]
                act.wait_ge(aT_done, i + 1)
                if i >= 2:
                    act.wait_ge(pv_done, i - 1)
                src = banks(4)[:, 0:4 * P].rearrange("p (k t) -> p k t", k=4)[:, :, 0:R]
                nc.scalar.activation(diffT[i % 2][:, 0:4, 0:R], src, ACT.Copy)
                nc.scalar.activation(diffT[i % 2][0:N_META, 4, 0:R], banks(5, N_META)[:, 0:R],
                                     ACT.Copy).then_inc(aT_read, 1)

            def read_out(t):
                R = CROWS[t % NC5]
                act.wait_ge(pv_done, 4 * t + 4)
                if t >= 1:
                    act.wait_ge(on_ready, t)
                nc.scalar.activation(osb[0:R, :], banks(6, R)[:, 0:HALF], ACT.Copy).then_inc(o_read, 1)
                act.wait_ge(o_read, t + 1)
                nc.scalar.activation(osq[0:R, :], osb[0:R, :], ACT.Square).then_inc(osq_ready, 1)

            def rstd_out(t):
                R = CROWS[t % NC5]
                act.wait_ge(so_ready, t + 1)
                rms_rstd(nc, step, so[0:R, :], so[0:R, :], HD, eps[0:R, :]).then_inc(or_ready, 1)

            def store_out(t):
                R, a = CROWS[t % NC5], mixcol(*divmod(t, NC5))
                act.wait_ge(oT_done, t + 1)
                src = banks(7)[:, 0:HALF].rearrange("p (h t) -> p h t", h=HEADS)[:, :, 0:R]
                nc.scalar.activation(mixT[:, 0:HEADS, a:a + R], src, ACT.Copy).then_inc(oT_read, 1)

            def high_qk(h):
                nc.scalar.activation(k_hi[:, h], kT[:, h], ACT.Copy).then_inc(k_high, 1)
                nc.scalar.activation(q_hi[:, h], qT[:, h], ACT.Copy).then_inc(q_high, 1)

            high_qk(0)
            high_qk(1)
            for s in range(LAST + 2):
                t, r = divmod(s - 7, 4)
                if r == 0 and 0 <= t - 1 < G * NC5:
                    store_out(t - 1)
                if r == 0 and 0 <= t < G * NC5:
                    read_out(t)
                if r == 1 and 0 <= t < G * NC5:
                    rstd_out(t)
                if 2 <= s + 1 < HEADS:
                    high_qk(s + 1)
                if s < N:
                    softmax(s)
                if 2 <= s <= N + 1:
                    read_turned(s - 2)
                if s == 5:
                    act.wait_ge(g_abs, 1)
                    step(nc.scalar.activation(ga[:], ga[:], ACT.Exp, scale=-1.0))
                    nc.scalar.activation(ga[:], ga[:], ACT.Ln, bias=1.0).then_inc(g_exp, 1)

        @block.vector
        def _(dve):
            step = chained(dve, dve_step)
            f, li = gt[:, 1::2, :], gt[:, 0::2, :]

            def gates_magnitude():
                dve.wait_ge(gt_loaded, 16 * 16)
                step(nc.vector.tensor_scalar(ga[:], f, -1.0, None, ALU.mult))
                nc.vector.tensor_tensor(ga[:], ga[:], f, ALU.max).then_inc(g_abs, 1)
                dve.wait_ge(g_abs, 1)
                step(nc.vector.tensor_scalar(gb[:], f, 0.0, None, ALU.min))

            def gate_rows():
                dve.wait_ge(g_exp, 1)
                step(nc.vector.tensor_tensor(gb[:], gb[:], ga[:], ALU.subtract))
                yield
                step(nc.vector.memset(ga[:], 0.0))
                yield
                for d, order in ((0, slice(None)), (1, slice(None, None, -1))):
                    step(nc.vector.tensor_tensor_scan(rowt[:, d, order], gb[:, d, order], ga[:, d, order], 0.0, ALU.add, ALU.add))
                    yield
                    step(nc.vector.tensor_tensor_scan(rowt[:, 4 + d, order], gb[:, d, order], li[:, d, order], 0.0, ALU.add, ALU.max))
                    yield
                step(nc.vector.tensor_tensor(rowt[:, 2:4], li, rowt[:, 0:2], ALU.subtract))
                yield
                step(nc.vector.tensor_tensor(rowt[:, 0:2], rowt[:, 0:2], rowt[:, 4:6], ALU.subtract))
                yield

            def maxima(i):
                R = CROWS[units[i][1]]
                for j in range(2):
                    dve.wait_ge(s_done, 2 * i + j + 1)
                    nc.vector.tensor_reduce(nmax[0:R, i % 2, j:j + 1], banks(2 * j, R)[:, PH:PH + T], AX.X, ALU.max,
                                            negate=True).then_inc(s_max, 1)

            def combine(i):
                R = CROWS[units[i][1]]
                dve.wait_ge(s_exp, 2 * i + 2)
                r = rcp[0:R, i % 2]
                step(nc.vector.reciprocal(r, lsum[0:R, i % 2]))
                step(nc.vector.tensor_tensor(r[:, 1:2], r[:, 1:2], lam[0:R, 3:4], ALU.mult))
                if i >= 2:
                    dve.wait_ge(aT_done, i - 1)
                p0, p1 = (prob[i % 2][j][0:R, :] for j in range(2))
                step(nc.vector.tensor_scalar(diff[i % 2][0:R, :], p0, r[:, 0:1], None, ALU.mult))
                nc.vector.scalar_tensor_tensor(diff[i % 2][0:R, :], p1, r[:, 1:2], diff[i % 2][0:R, :], ALU.mult,
                                               ALU.add).then_inc(a_ready, 1)

            def sum_out(t):
                R = CROWS[t % NC5]
                dve.wait_ge(osq_ready, t + 1)
                nc.vector.tensor_reduce(so[0:R, :], osq[0:R, :].rearrange("p (h d) -> p h d", h=HEADS), AX.X,
                                        ALU.add).then_inc(so_ready, 1)

            def low_q(h):
                dve.wait_ge(q_high, h + 1)
                nc.vector.tensor_tensor(q_lo[:, h], qT[:, h], q_hi[:, h].bitcast(F32), ALU.subtract).then_inc(q_low, 1)

            gate_steps = gate_rows()
            low_q(0)
            for s in range(LAST):
                if s + 1 < HEADS:
                    low_q(s + 1)
                if s < N:
                    maxima(s)
                t, r = divmod(s - 7, 4)
                if r == 0 and 0 <= t < G * NC5:
                    sum_out(t)
                if 1 <= s <= N:
                    combine(s - 1)
                if s == 4:
                    gates_magnitude()
                if 8 <= s < 16:
                    next(gate_steps)


def mlstm(nc, e):
    ident, causal, gml, rowt, colt, eps = (e[k] for k in "ident causal gml rowt colt eps".split())
    mixT, MO, MV, MQK = (e[k] for k in "mixT MO MV MQK".split())
    banks, base, sem = e["banks"], e["base"], e["sem"]
    weights = Map(nc, base, A_Q, A_MO)
    pw = [[weights(f"pw{i}{d}", [P, NC5, T]) for d in range(2)] for i in range(2)]
    diag = [weights(f"diag{i}", [P, 2, P]) for i in range(2)]
    em = weights("em", [P, 2, NC5, 8])
    den = weights("den", [P, 8])
    sh = weights("sh", [P, 2, HEADS])
    hsq = weights("hsq", [P, HALF])
    late = Map(nc, base, A_W, A_S)
    ew = [[late(f"ew{i}{d}", [P, T]) for d in range(2)] for i in range(2)]
    spr = [late(f"spr{i}", [P, 2, T]) for i in range(2)]
    hm = late("hm", [P, NC5, HALF])
    hn = [late(f"hn{i}", [P, HALF]) for i in range(2)]

    col_done, col_ready = sem("col_done"), sem("col_ready")
    a_done, spr_ready, s_done, p_ready = sem("m_a_done"), sem("m_spr_ready"), sem("m_s_done"), sem("m_p_ready")
    diag_ready, ew_ready = sem("m_diag_ready"), sem("m_ew_ready")
    n_done, n_read = sem("m_n_done"), sem("m_n_read")
    hsq_ready, sh_ready, hr_ready, hn_ready, hT_done, hT_read = (
        sem(s) for s in "hsq_ready sh_ready hr_ready hn_ready hmT_done hmT_read".split())
    act_step, dve_step, pool_step = (e[k] for k in "act_step dve_step pool_step".split())

    units = [(g, h) for g in range(G) for h in range(HEADS)]
    N = NC5 * len(units)
    outs = [n for n in range(N) if units[n // NC5][1] == HEADS - 1]
    LAST = N + 12
    SUMS = (3, 6)

    hg_ready = sem("hg_ready")

    def where(n):
        u, c = divmod(n, NC5)
        return u, c, CROWS[c], CCOL[c]

    with nc.Block() as block:

        @block.sync
        def _(sp):
            sp.wait_ge(s_done, N)
            wo_rows = e["w_out"].rearrange("o (k p) n -> (o p) k n", p=P)
            for k in range(KD):
                sp.dma_start(e["wo"][:, k], wo_rows[:, k]).then_inc(e["wo_loaded"][k], 16)

        @block.tensor
        def _(pe):
            for k in range(4):
                for c in range(NC5):
                    at = (k * NC5 + c) * 8
                    mm = pe.transpose(banks(7, CROWS[c])[:, at:at + 8], rowt[:, 2 + k, CCOL[c]:CCOL[c] + CROWS[c]],
                                      ident[0:8, 0:8])
            mm.then_inc(col_done, 1)

            def spread(u):
                if u >= 1:
                    pe.wait_ge(spr_ready, u)
                cut = 1024 - PH - T
                for d, pieces in ((0, HALVES), (1, ((PH + T, 0, cut), (1024, cut, T)))):
                    for at, a, b in pieces:
                        mm = pe.matmul(banks(0)[:, at:at + b - a], ident[0:8, u:u + 1].to_broadcast([8, P]),
                                       rowt[:, d, a:b], start=True, stop=True)
                mm.then_inc(a_done, 1)

            def scores(n):
                u, c, R, t = where(n)
                g, h = units[u]
                if n >= 1:
                    pe.wait_ge(p_ready, n)
                for at, a, b in HALVES:
                    mm = pe.matmul(banks(4, R)[:, at:at + b - a], MQK[:, HEADS + h, g, t:t + R], MQK[:, h, g, a:b],
                                   start=True, stop=True)
                mm.then_inc(s_done, 1)

            def sums(n):
                u, c, R, t = where(n)
                g, h = units[u]
                pe.wait_ge(p_ready, NC5 * (u + 1))
                if n == 0:
                    pe.wait_ge(e["mv_loaded"], 16 * NZ)
                if n >= 2:
                    pe.wait_ge(n_read, n - 1)
                for d, over in ((0, range(0, c + 1)), (1, range(c, NC5))):
                    for s in over:
                        mm = pe.matmul(banks(SUMS[n % 2], R)[:, d * (HD + 1):(d + 1) * (HD + 1)], pw[u % 2][d][0:CROWS[s], s, t:t + R],
                                       MV[0:CROWS[s], zc(g, s), h], start=(s == over[0]), stop=(s == over[-1]))
                mm.then_inc(n_done, 1)

            def turn_out(o):
                R = CROWS[o % NC5]
                pe.wait_ge(hn_ready, o + 1)
                if o >= 1:
                    pe.wait_ge(hT_read, o)
                else:
                    pe.wait_ge(col_ready, 2)
                for h in range(HEADS):
                    mm = pe.transpose(banks(7)[:, h * P:h * P + R], hn[o % 2][0:R, h * HD:(h + 1) * HD], ident[0:R, 0:R])
                mm.then_inc(hT_done, 1)

            for s in range(LAST):
                if s == 0:
                    spread(0)
                if s < N:
                    scores(s)
                if s % NC5 == 2 and s // NC5 + 1 < len(units):
                    spread(s // NC5 + 1)
                if 0 <= s - NC5 < N:
                    sums(s - NC5)
                if s - 10 in outs:
                    turn_out(outs.index(s - 10))

        @block.gpsimd
        def _(pool):
            step = chained(pool, pool_step)

            def norm_out(o):
                g, c = divmod(o, NC5)
                R = CROWS[c]
                pool.wait_ge(hr_ready, o + 1)
                if o >= 2:
                    pool.wait_ge(hT_done, o - 1)
                y = hn[o % 2][0:R, :]
                y4 = y.rearrange("p (h d) -> p h d", h=HEADS)
                x4 = hm[0:R, c].rearrange("p (h d) -> p h d", h=HEADS)
                step(nc.gpsimd.tensor_tensor(y4, x4, sh[0:R, o % 2].unsqueeze(2).to_broadcast([R, HEADS, HD]), ALU.mult))
                nc.gpsimd.tensor_tensor(y4, y4, gml[0:R, :].unsqueeze(1).to_broadcast([R, HEADS, HD]),
                                        ALU.mult).then_inc(hg_ready, 1)

            for o in range(len(outs)):
                norm_out(o)

        @block.scalar
        def _(act):
            step = chained(act, act_step)
            act.wait_ge(col_done, 1)
            for k, dst in ((0, colt), (2, em)):
                for c in range(NC5):
                    R = CROWS[c]
                    src = banks(7, R)[:, 0:4 * NC5 * 8].rearrange("p (k c u) -> p k c u", k=4, c=NC5)[:, k:k + 2, c]
                    ins = nc.scalar.activation(dst[0:R, 0:2, c], src, ACT.Copy if k == 0 else ACT.Exp,
                                               scale=1.0 if k == 0 else -1.0)
                ins.then_inc(col_ready, 1)
            act.wait_ge(col_ready, 2)

            def read_spread(u):
                act.wait_ge(a_done, u + 1)
                if u >= 2:
                    act.wait_ge(diag_ready, NC5 * (u - 1))
                for d in range(2):
                    ins = nc.scalar.activation(spr[u % 2][:, d], banks(0)[:, PH + T * d:PH + T * (d + 1)], ACT.Copy)
                ins.then_inc(spr_ready, 1)

            def weigh(n):
                u, c, R, t = where(n)
                act.wait_ge(spr_ready, u + 1)
                a = spr[u % 2]
                if n >= 2:
                    act.wait_ge(p_ready, n - 1)
                f, b = ew[n % 2]
                if c < NC5 - 1:
                    nc.scalar.activation(f[0:R, t + R:T], a[0:R, 0, t + R:T], ACT.Exp, bias=colt[0:R, 0, c, u:u + 1])
                if c > 0:
                    nc.scalar.activation(b[0:R, 0:t], a[0:R, 1, 0:t], ACT.Exp, bias=colt[0:R, 1, c, u:u + 1])
                act.wait_ge(diag_ready, n + 1)
                for d, w in enumerate((f, b)):
                    ins = nc.scalar.activation(w[0:R, t:t + R], diag[n % 2][0:R, d, 0:R], ACT.Exp)
                ins.then_inc(ew_ready, 1)

            def square_out(o):
                R, c = CROWS[o % NC5], o % NC5
                act.wait_ge(n_read, outs[o] + 1)
                if o >= 1:
                    act.wait_ge(sh_ready, o)
                nc.scalar.activation(hsq[0:R, :], hm[0:R, c], ACT.Square).then_inc(hsq_ready, 1)

            def rstd_out(o):
                R = CROWS[o % NC5]
                act.wait_ge(sh_ready, o + 1)
                rms_rstd(nc, step, sh[0:R, o % 2], sh[0:R, o % 2], HD, eps[0:R, :]).then_inc(hr_ready, 1)

            def store_out(o):
                R, a = CROWS[o % NC5], mixcol(*divmod(o, NC5))
                act.wait_ge(hT_done, o + 1)
                src = banks(7)[:, 0:HALF].rearrange("p (h t) -> p h t", h=HEADS)[:, :, 0:R]
                nc.scalar.activation(mixT[:, HEADS:, a:a + R], src, ACT.Copy).then_inc(hT_read, 1)

            for s in range(LAST):
                if s == 0:
                    read_spread(0)
                if s < N:
                    weigh(s)
                if s % NC5 == 3 and s // NC5 + 1 < len(units):
                    read_spread(s // NC5 + 1)
                if s - 7 in outs:
                    square_out(outs.index(s - 7))
                if s - 8 in outs:
                    rstd_out(outs.index(s - 8))
                if s - 11 in outs:
                    store_out(outs.index(s - 11))

        @block.vector
        def _(dve):
            step = chained(dve, dve_step)
            dve.wait_ge(col_ready, 2)

            def mask(n):
                u, c, R, t = where(n)
                dve.wait_ge(spr_ready, u + 1)
                if n >= 2:
                    dve.wait_ge(ew_ready, n - 1)
                for d in range(2):
                    ins = nc.vector.scalar_tensor_tensor(diag[n % 2][0:R, d, 0:R], spr[u % 2][0:R, d, t:t + R],
                                                         colt[0:R, d, c, u:u + 1], causal[0:R, d, 0:R], ALU.add, ALU.add)
                ins.then_inc(diag_ready, 1)

            def apply(n):
                u, c, R, t = where(n)
                dve.wait_ge(s_done, n + 1)
                dve.wait_ge(ew_ready, n + 1)
                if u >= 2:
                    dve.wait_ge(n_done, NC5 * (u - 1))
                for d, a, b in ((0, t, T), (1, 0, t + R)):
                    ins = nc.vector.scalar_tensor_tensor(pw[u % 2][d][0:R, c, a:b], banks(4, R)[:, PH + a:PH + b], HD ** -0.5,
                                                         ew[n % 2][d][0:R, a:b], ALU.mult, ALU.mult)
                ins.then_inc(p_ready, 1)

            def divide(n):
                u, c, R, t = where(n)
                h = units[u][1]
                s = banks(SUMS[n % 2], R)[:, 0:2 * (HD + 1)].rearrange("p (d w) -> p d w", d=2)
                dve.wait_ge(n_done, n + 1)
                if u == HEADS:
                    dve.wait_ge(hg_ready, c + 1)
                d = den[0:R, :]
                step(nc.vector.tensor_copy(d[:, 0:2], s[:, :, HD]))
                step(nc.vector.scalar_tensor_tensor(d[:, 2:4], d[:, 0:2], -1.0, d[:, 0:2], ALU.mult, ALU.max))
                step(nc.vector.tensor_tensor(d[:, 4:6], d[:, 2:4], em[0:R, :, c, u], ALU.max))
                step(nc.vector.reciprocal(d[:, 6:8], d[:, 4:6]))
                out = hm[0:R, c, h * HD:(h + 1) * HD]
                step(nc.vector.tensor_scalar(out, s[:, 0, 0:HD], d[:, 6:7], None, ALU.mult))
                nc.vector.scalar_tensor_tensor(out, s[:, 1, 0:HD], d[:, 7:8], out, ALU.mult, ALU.add).then_inc(n_read, 1)

            def sum_out(o):
                R = CROWS[o % NC5]
                dve.wait_ge(hsq_ready, o + 1)
                if o >= 2:
                    dve.wait_ge(hg_ready, o - 1)
                nc.vector.tensor_reduce(sh[0:R, o % 2], hsq[0:R, :].rearrange("p (h d) -> p h d", h=HEADS), AX.X,
                                        ALU.add).then_inc(sh_ready, 1)

            def gate_out(o):
                g, c = divmod(o, NC5)
                R = CROWS[c]
                dve.wait_ge(hg_ready, o + 1)
                if o == 0:
                    dve.wait_ge(e["mo_loaded"], 16 * (1 + G))
                y = hn[o % 2][0:R, :]
                nc.vector.tensor_tensor(y, y, MO[0:R, zc(g, c)], ALU.mult).then_inc(hn_ready, 1)

            mask(0)
            for s in range(LAST):
                if s + 1 < N:
                    mask(s + 1)
                if s < N:
                    apply(s)
                if 0 <= s - 6 < N:
                    divide(s - 6)
                if s - 7 in outs:
                    sum_out(outs.index(s - 7))
                if s - 9 in outs:
                    gate_out(outs.index(s - 9))




NGU, ND = 3, 4


def weight_groups(nc, e):
    ring = Map(nc, e["base"], A_Q, A_END)
    gu = [ring(f"wgu{i}", [P, 2, KD, 256]) for i in range(NGU)]
    down = [ring(f"wd{i}", [P, 2, D]) for i in range(ND)]
    whi = [ring(f"whi{i}", [P, 2, KD, P], F32R) for i in range(2)]
    return gu, down, whi


def gu_slot(j):
    return j % NGU


def load_group(eng, e, rings, loaded, expert, j, part):
    gu, down = rings[0][gu_slot(j)], rings[1][j % ND]
    if "gu" in part:
        for i, w in enumerate((e["w_gate"], e["w_up"])):
            src = w[0, bass.ds(expert, 1), :, 256 * j:256 * (j + 1)].rearrange("o (k p) f -> (o p) k f", p=P)
            eng.dma_start(gu[:, i], src).then_inc(loaded[gu_slot(j)], 16)
    if "d" in part:
        src = e["w_down"][0, bass.ds(expert, 1), 256 * j:256 * (j + 1), :].rearrange("o (c p) d -> (o p) c d", p=P)
        eng.dma_start(down[:], src).then_inc(loaded[NGU + j % ND], 16)


def project_out(nc, e):
    ident, eps, mixT, mix_lo, late = (e[k] for k in "ident eps mixT mix_lo late".split())
    banks, base, sem, rings, loaded = e["banks"], e["base"], e["sem"], e["rings"], e["loaded"]
    AFF = e["AFF"]
    tiles = Map(nc, base, A_W, A_S)
    x = [tiles(f"xr{i}", [P, D]) for i in range(2)]
    x2 = [tiles(f"x2{i}", [P, D]) for i in range(2)]
    xn = [tiles(f"xn{i}", [P, D]) for i in range(2)]
    junk = tiles("junk", [P, D])
    gffn = tiles("gffn", [P, D])
    xnT = [late(f"xnT{i}", [P, KD, P]) for i in range(2)]
    wo, wo_lo, wo_loaded = (e[k] for k in "wo wo_lo wo_loaded".split())
    parts = Map(nc, base, A_WO, A_QK)
    wo_hi = parts("wo_hi", [P, KD, D], F32R)
    mix_hi = parts("mix_hi", [P, KD, G * T], F32R)
    wr = parts("wr", [P, KD, N_EXP])
    logits = [parts(f"logits{i}", [N_EXP, P]) for i in range(2)]
    sx = parts("sx", [P, 2, 2])
    ex = parts("ex", [P, 2, 2, N_EXP])
    mx = parts("mx", [P, 2, 2, 4])

    chunks = [(None, 0)] + [(g, c) for g in range(G) for c in range(1, NC5)]
    rows = [2 * N_META] + [P] * (NZ - 1)
    col = [0] + [mixcol(g, c) for g, c in chunks[1:]]

    def dram_rows(i):
        if i == 0:
            return [(slice(N_META * g, N_META * (g + 1)), slice(T * g, T * g + N_META)) for g in range(G)]
        g, c = chunks[i]
        return [(slice(0, P), slice(T * g + CCOL[c], T * g + CCOL[c] + P))]

    def x_rows(i):
        if i == 0:
            return [(slice(N_META * g, N_META * (g + 1)), e["x_meta"]) for g in range(G)]
        g, c = chunks[i]
        return [(slice(0, P), e[("x_prompt", "x_sample")[g]][0, P * (c - 1):P * c, :])]

    x_loaded = [sem(f"xr_loaded{i}") for i in range(2)]
    wo_high, wo_low, mix_high, mix_low = (sem(s) for s in "wo_high wo_low mix_high mix_low".split())
    gffn_loaded, wr_loaded = sem("gffn_loaded"), sem("wr_loaded")
    o_done, x2_ready, xs_ready, xn_ready = (sem(s) for s in "o_done x2_ready xsc_ready xn_ready".split())
    x2_stored = [sem(f"x2_stored{i}") for i in range(2)]
    xn_stored = [sem(f"xn_stored{i}") for i in range(2)]
    rT_done, rT_read = sem("rT_done"), sem("rT_read")
    t_done, t_read, r_done, r_max, r_exp, r_ready = (sem(s) for s in "xnT_done xnT_read r_done r_max r_exp r_ready".split())
    act_step, dve_step = e["act_step"], e["dve_step"]

    def loads(i):
        return 16 * (i // 2 + 1 + (1 if i % 2 == 0 else 0))

    with nc.Block() as block:

        @block.sync
        def _(sp):
            for i in range(2):
                for r, src in x_rows(i):
                    sp.dma_start(x[i][r, :], src).then_inc(x_loaded[i], 16)
            sp.dma_start(wr[:], e["w_router"].rearrange("o (k p) n -> (o p) k n", p=P)).then_inc(wr_loaded, 16)
            load_group(sp, e, rings, loaded, 0, 0, "gu")
            for i in range(NZ):
                sp.wait_ge(x2_ready, i + 1)
                for r, d in dram_rows(i):
                    sp.dma_start(e["out"][d, :], x2[i % 2][r, :]).then_inc(x2_stored[i % 2], 16)
                if i + 2 < NZ:
                    for r, src in x_rows(i + 2):
                        sp.dma_start(x[i % 2][r, :], src).then_inc(x_loaded[i % 2], 16)
                sp.wait_ge(xn_ready, i + 1)
                for r, d in dram_rows(i):
                    sp.dma_start(e["xn_rows"][d, :], xn[i % 2][r, :]).then_inc(xn_stored[i % 2], 16)
            for j in range(3):
                load_group(sp, e, rings, loaded, 0, j, "d" if j == 0 else "gu d")
            for i in range(2):
                last = NZ - 1 - (NZ - 1 - i) % 2
                sp.wait_ge(x2_stored[i], loads(last))
                sp.wait_ge(xn_stored[i], loads(last))

        @block.gpsimd
        def _(pool):
            pool.dma_start(gffn[:], e["g_ffn"].to_broadcast([P, D])).then_inc(gffn_loaded, 16)
            for i in range(NZ):
                at = slice(col[i], col[i] + rows[i])
                pool.wait_ge(mix_high, i + 1)
                nc.gpsimd.tensor_tensor(mix_lo[:, :, at], mixT[:, :, at], mix_hi[:, :, at].bitcast(F32),
                                        ALU.subtract).then_inc(mix_low, 1)

        @block.tensor
        def _(pe):
            def product(i):
                R = rows[i]
                if i >= 2:
                    pe.wait_ge(x2_ready, i - 1)
                pe.wait_ge(mix_low, i + 1)
                for k in range(KD):
                    if i == 0:
                        pe.wait_ge(wo_low, k + 1)
                    for i3, (m, w) in enumerate(((mix_hi, wo_hi), (mix_hi, wo_lo), (mix_lo, wo_hi))):
                        for n in range(2):
                            mm = pe.matmul(banks(2 * (i % 2) + n, R)[:, 0:512], m[:, k, col[i]:col[i] + R],
                                           w[:, k, 512 * n:512 * (n + 1)], start=(k == 0 and i3 == 0),
                                           stop=(k == KD - 1 and i3 == 2))
                mm.then_inc(o_done, 1)

            def turn(i):
                R = rows[i]
                pe.wait_ge(xn_ready, i + 1)
                if i >= 1:
                    pe.wait_ge(t_read, i)
                for k in range(KD):
                    mm = pe.transpose(banks(4)[:, k * P:k * P + R], xn[i % 2][0:R, k * P:(k + 1) * P], ident[0:R, 0:R])
                mm.then_inc(t_done, 1)

            def route(i):
                pe.wait_ge(t_read, i + 1)
                if i == 0:
                    pe.wait_ge(wr_loaded, 16)
                else:
                    pe.wait_ge(rT_read, i)
                for k in range(KD):
                    mm = pe.matmul(banks(6, N_EXP)[:, 0:rows[i]], wr[:, k], xnT[i % 2][:, k, 0:rows[i]],
                                   start=(k == 0), stop=(k == KD - 1))
                mm.then_inc(rT_done, 1)

            def turn_logits(i):
                pe.wait_ge(rT_read, i + 1)
                if i >= 1:
                    pe.wait_ge(r_exp, i)
                for g, a, R in ([(0, 0, N_META), (1, N_META, N_META)] if i == 0 else [(0, 0, P)]):
                    mm = pe.transpose(banks(7, R)[:, N_EXP * g:N_EXP * (g + 1)], logits[i % 2][:, a:a + R],
                                      ident[0:N_EXP, 0:N_EXP])
                mm.then_inc(r_done, 1)

            for s in range(NZ + 3):
                if s < NZ:
                    product(s)
                if 0 <= s - 1 < NZ:
                    turn(s - 1)
                if 0 <= s - 2 < NZ:
                    route(s - 2)
                if 0 <= s - 3 < NZ:
                    turn_logits(s - 3)

        @block.scalar
        def _(act):
            step = chained(act, act_step)

            def scale(i):
                R = rows[i]
                act.wait_ge(x2_ready, i + 1)
                s = sx[0:R, i % 2]
                step(nc.scalar.activation(junk[0:R, :], x2[i % 2][0:R, :], ACT.Square, accum_out=s[:, 0:1]))
                step(rms_rstd(nc, step, s[:, 0:1], s[:, 1:2], D, eps[0:R, :]))
                if i >= 2:
                    act.wait_ge(t_done, i - 1)
                    act.wait_ge(xn_stored[i % 2], loads(i - 2))
                nc.scalar.activation(xn[i % 2][0:R, :], x2[i % 2][0:R, :], ACT.Copy, scale=s[:, 1:2]).then_inc(xs_ready, 1)

            def exp(i):
                R, n = (N_META, 2) if i == 0 else (P, 1)
                act.wait_ge(r_max, i + 1)
                for g in range(n):
                    ins = nc.scalar.activation(ex[0:R, i % 2, g], banks(7, R)[:, N_EXP * g:N_EXP * (g + 1)], ACT.Exp,
                                               bias=mx[0:R, i % 2, g, 0:1], accum_out=mx[0:R, i % 2, g, 1:2])
                ins.then_inc(r_exp, 1)

            def high_mix(i):
                at = slice(col[i], col[i] + rows[i])
                nc.scalar.activation(mix_hi[:, :, at], mixT[:, :, at], ACT.Copy).then_inc(mix_high, 1)

            high_mix(0)
            for k in range(KD):
                if k == 2:
                    high_mix(1)
                act.wait_ge(wo_loaded[k], 16)
                nc.scalar.activation(wo_hi[:, k], wo[:, k], ACT.Copy).then_inc(wo_high, 1)
            for s in range(NZ + 4):
                if s + 2 < NZ:
                    high_mix(s + 2)
                if s < NZ:
                    scale(s)
                if 0 <= s - 3 < NZ:
                    exp(s - 3)

        @block.vector
        def _(dve):
            step = chained(dve, dve_step)

            def add(i):
                R = rows[i]
                dve.wait_ge(o_done, i + 1)
                dve.wait_ge(x_loaded[i % 2], loads(i))
                if i >= 2:
                    dve.wait_ge(xs_ready, i - 1)
                    dve.wait_ge(x2_stored[i % 2], loads(i - 2))
                nc.vector.tensor_tensor(x2[i % 2][0:R, :], banks(2 * (i % 2), R)[:, 0:D], x[i % 2][0:R, :],
                                        ALU.add).then_inc(x2_ready, 1)

            def weight(i):
                R = rows[i]
                dve.wait_ge(xs_ready, i + 1)
                nc.vector.tensor_tensor(xn[i % 2][0:R, :], xn[i % 2][0:R, :], gffn[0:R, :], ALU.mult).then_inc(xn_ready, 1)

            def read_turned(i):
                R = rows[i]
                dve.wait_ge(t_done, i + 1)
                if i >= 2:
                    dve.wait_ge(rT_done, i - 1)
                src = banks(4)[:, 0:D].rearrange("p (k t) -> p k t", k=KD)[:, :, 0:R]
                nc.vector.tensor_copy(xnT[i % 2][:, :, 0:R], src).then_inc(t_read, 1)

            def read_logits(i):
                dve.wait_ge(rT_done, i + 1)
                if i >= 2:
                    dve.wait_ge(r_done, i - 1)
                nc.vector.tensor_copy(logits[i % 2][:, 0:rows[i]], banks(6, N_EXP)[:, 0:rows[i]]).then_inc(rT_read, 1)

            def maxima(i):
                R, n = (N_META, 2) if i == 0 else (P, 1)
                dve.wait_ge(r_done, i + 1)
                for g in range(n):
                    ins = nc.vector.tensor_reduce(mx[0:R, i % 2, g, 0:1], banks(7, R)[:, N_EXP * g:N_EXP * (g + 1)], AX.X,
                                                  ALU.max, negate=True)
                ins.then_inc(r_max, 1)

            def softmax(i):
                R, n = (N_META, 2) if i == 0 else (P, 1)
                dve.wait_ge(r_exp, i + 1)
                for g in range(n):
                    m = mx[0:R, i % 2, g]
                    to, slot = (g, 0) if i == 0 else chunks[i]
                    step(nc.vector.reciprocal(m[:, 2:3], m[:, 1:2]))
                    ins = nc.vector.tensor_scalar(AFF[0:R, slot, N_EXP * to:N_EXP * (to + 1)], ex[0:R, i % 2, g], m[:, 2:3], None,
                                                  ALU.mult)
                ins.then_inc(r_ready, 1)

            for k in range(KD):
                dve.wait_ge(wo_high, k + 1)
                nc.vector.tensor_tensor(wo_lo[:, k], wo[:, k], wo_hi[:, k].bitcast(F32), ALU.subtract).then_inc(wo_low, 1)
            dve.wait_ge(gffn_loaded, 16)
            for s in range(NZ + 4):
                if s < NZ:
                    add(s)
                if 0 <= s - 1 < NZ:
                    read_turned(s - 1)
                if s < NZ:
                    weight(s)
                if 0 <= s - 2 < NZ:
                    read_logits(s - 2)
                if 0 <= s - 3 < NZ:
                    maxima(s - 3)
                    softmax(s - 3)


def experts(nc, e):
    ident = e["ident"]
    AFF, rings, loaded, out, xn_rows = (e[k] for k in "AFF rings loaded out xn_rows".split())
    banks, base, sem = e["banks"], e["base"], e["sem"]
    wgu, wdown, whi = rings
    tiles = Map(nc, base, A_MOE, A_S)
    C2 = G * CAP
    RANKS = (CAP + 7) // 8 * 8
    JG = FF // 256
    M = FF // P
    PER_BANK = 3
    wlo = [tiles(f"wlo{i}", [P, 2, KD, P], BF16) for i in range(2)]
    xg = tiles("xg", [CAP, G, D])
    xT = tiles("xT", [P, KD, C2])
    xx = tiles("xx", [P, KD, 2 * C2], F32R)
    xb = tiles("xb", [P, KD, C2], BF16)
    low = [tiles(f"low{i}", [P, 2, C2]) for i in range(2)]
    gu = [tiles(f"gu{i}", [P, 2, C2]) for i in range(2)]
    sil = [tiles(f"sil{i}", [P, C2]) for i in range(2)]
    hid = [tiles(f"hid{i}", [P, C2]) for i in range(2)]
    yT = tiles("yT", [P, KD, C2])
    yr = tiles("yr", [CAP, G, D])
    work = [tiles(f"aff{i}", [G * N_EXP, T]) for i in range(2)]
    vals = tiles("vals", [G * N_EXP, RANKS])
    index = tiles("index", [G * N_EXP, RANKS], U32)
    indexf = tiles("indexf", [G * N_EXP, RANKS])
    gateT = tiles("gateT", [CAP, G, N_EXP])
    idxT = tiles("idxT", [CAP, G, N_EXP], U32)
    take = tiles("take", [CAP, G, 1], U32)
    give = tiles("give", [CAP, G, 1], U32)
    gate = tiles("gate", [CAP, G])

    aT_done, ranked, lists_done, lists_ready = (sem(s) for s in "affT_done ranked lists_done lists_ready".split())
    take_ready, xg_loaded, xT_done, xT_ready, xh_ready, xb_ready, xl_ready = (
        sem(s) for s in "take_ready xg_loaded xgT_done xgT_ready xh_ready xb_ready xl_ready".split())
    hi_ready, lo_ready, gu_done, low_ready, sum_ready, sil_ready, hid_ready, d_done = (
        sem(s) for s in "hi_ready lo_ready gu_done low_ready sum_ready sil_ready hid_ready d_done".split())
    yT_ready, y_done, yr_ready = (sem(s) for s in "yT_ready yt_done yr_ready".split())
    give_free, give_ready, added = (sem(s) for s in "give_free give_ready added".split())

    OUT_STEPS = {2: 0, 3: 1, 4: 2, 5: 3}
    ROW_STEPS = {10: range(0, 3), 11: range(3, 6), 12: range(6, 8)}
    TURN = 7
    EARLY = JG % NGU

    def y_tile(k):
        at = (k % PER_BANK) * C2
        return banks(4 + k // PER_BANK)[:, at:at + C2]

    def last_user(slots, ex, j):
        if j >= slots:
            return JG * ex + j - slots
        if isinstance(ex, int) and ex == 0:
            return None
        return JG * (ex - 1) + max(i for i in range(JG) if i % slots == j)

    def uses(slots, ex, j):
        return len(range(j % slots, JG, slots)) * ex + j // slots + 1

    def per_expert(eng, body):
        body(0, True, False)
        with eng.Fori(1, N_EXP - 1) as ex:
            body(ex, False, False)
        body(N_EXP - 1, False, True)

    def ahead(ex, m, last):
        if m + 2 < M:
            return ex, m + 2
        return None if last else (ex + 1, m + 2 - M)

    with nc.Block() as block:

        @block.sync
        def _(sp):
            def load_gu(ex, j):
                before = last_user(NGU, ex, j)
                sp.wait_ge(lo_ready, 2 * before + 2)
                load_group(sp, e, rings, loaded, ex, j, "gu")

            def body(ex, first, last):
                for j in range(3 if first else 0, JG):
                    if j != EARLY:
                        load_gu(ex, j)
                    before = last_user(ND, ex, j)
                    if before is not None:
                        sp.wait_ge(d_done, 2 * before + 2)
                    load_group(sp, e, rings, loaded, ex, j, "d")
                    if j == JG - 1 and not last:
                        load_gu(ex + 1, EARLY)

            per_expert(sp, body)
            sp.wait_ge(added, 32 * N_EXP)

        @block.gpsimd
        def _(pool):
            def fetch(ex):
                pool.wait_ge(take_ready, ex + 1)
                for g in range(G):
                    nc.gpsimd.indirect_dma_start(xg[:, g, :], None, xn_rows,
                                                 bass.IndirectOffsetOnAxis(ap=take[:, g, :], axis=0)).then_inc(xg_loaded, 16)

            def add_rows(ex, first):
                if not first:
                    pool.wait_ge(added, 32 * ex)
                pool.sem_inc(give_free, 1)
                pool.wait_ge(yr_ready, 4 * ex + 4)
                for g in range(G):
                    nc.gpsimd.indirect_dma_start(out, bass.IndirectOffsetOnAxis(ap=give[:, g, :], axis=0), yr[:, g, :],
                                                 None, compute_op=ALU.add).then_inc(added, 16)

            fetch(0)
            fetch(1)
            add_rows(0, True)
            for ex in range(2, N_EXP):
                fetch(ex)
                add_rows(ex - 1, False)
            add_rows(N_EXP - 1, False)

        @block.tensor
        def _(pe):
            for c in range(NC5):
                at = PT + CCOL[c]
                mm = pe.transpose(banks(0, G * N_EXP)[:, at:at + CROWS[c]], AFF[0:CROWS[c], c], ident[0:CROWS[c], 0:CROWS[c]])
            mm.then_inc(aT_done, 1)
            pe.wait_ge(ranked, 1)
            for i, t in enumerate((vals, indexf)):
                mm = pe.transpose(banks(2, CAP)[:, 32 * i:32 * i + 32], t[:, 0:CAP], ident[0:G * N_EXP, 0:G * N_EXP])
            mm.then_inc(lists_done, 1)

            def turn_rows(ex, part, ks):
                if part == 0:
                    pe.wait_ge(xg_loaded, 32 * ex + 32)
                elif part > 0:
                    pe.wait_ge(xT_ready, 3 * ex + part)
                for k in ks:
                    for g in range(G):
                        at = (k - ks[0]) * C2 + CAP * g
                        mm = pe.transpose(banks(TURN)[:, at:at + CAP], xg[:, g, k * P:(k + 1) * P], ident[0:CAP, 0:CAP])
                mm.then_inc(xT_done, 1)

            def up(ex, m, first):
                pe.wait_ge(lo_ready, M * ex + m + 1)
                if not (first and m < 2):
                    pe.wait_ge(sum_ready, M * ex + m - 1)
                b = 2 * (m % 2)
                for i in range(2):
                    for k in range(KD):
                        pe.matmul(banks(b + i)[:, 0:2 * C2], whi[m % 2][:, i, k], xx[:, k], start=(k == 0), stop=False,
                                  skip_group_check=True)
                for i in range(2):
                    for k in range(KD):
                        mm = pe.matmul(banks(b + i)[:, 0:C2], wlo[m % 2][:, i, k], xb[:, k], start=False, stop=(k == KD - 1),
                                       skip_group_check=True)
                mm.then_inc(gu_done, 1)

            def down(ex, m):
                j, c = divmod(m, 2)
                if c == 0:
                    pe.wait_ge(loaded[NGU + j % ND], 16 * uses(ND, ex, j))
                pe.wait_ge(hid_ready, M * ex + m + 1)
                for k in range(KD):
                    mm = pe.matmul(y_tile(k), wdown[j % ND][:, c, k * P:(k + 1) * P], hid[m % 2][:],
                                   start=(m == 0 and k % PER_BANK == 0), stop=(m == M - 1), skip_group_check=True)
                mm.then_inc(d_done, 1)

            def turn_outputs(ex, i, first_use):
                g, half = divmod(i, 2)
                if i > 0:
                    pe.wait_ge(yr_ready, 4 * ex + i)
                elif not first_use:
                    pe.wait_ge(xT_ready, 3 * ex + 6)
                for k in range(4):
                    mm = pe.transpose(banks(TURN, CAP)[:, k * P:(k + 1) * P], yT[:, 4 * half + k, CAP * g:CAP * (g + 1)], ident[:])
                mm.then_inc(y_done, 1)

            def body(ex, first, last):
                pe.wait_ge(xl_ready, ex + 1)
                pe.wait_ge(xb_ready, ex + 1)
                for m in range(M):
                    up(ex, m, first)
                    if m == 1 and not first:
                        pe.wait_ge(yT_ready, ex)
                    if m >= 1:
                        down(ex, m - 1)
                    if m in OUT_STEPS and not first:
                        turn_outputs(ex - 1, OUT_STEPS[m], False)
                    if m in ROW_STEPS and not last:
                        part = m - min(ROW_STEPS)
                        if part == 0 and not first:
                            pe.wait_ge(yr_ready, 4 * ex)
                        turn_rows(ex + 1, part, ROW_STEPS[m])
                down(ex, M - 1)

            for part, ks in enumerate(ROW_STEPS.values()):
                turn_rows(0, part, ks)
            per_expert(pe, body)
            pe.wait_ge(yT_ready, N_EXP)
            for i in range(4):
                turn_outputs(N_EXP - 1, i, True)

        @block.scalar
        def _(act):
            act.preload_act_table_set("silu_and_others")

            def split_high(ex, m):
                j, c = divmod(m, 2)
                if c == 0:
                    act.wait_ge(loaded[gu_slot(j)], 32 * uses(NGU, ex, j))
                if not (isinstance(ex, int) and ex == 0 and m < 2):
                    act.wait_ge(gu_done, M * ex + m - 1)
                nc.scalar.activation(whi[m % 2][:], wgu[gu_slot(j)][:, :, :, c * P:(c + 1) * P], ACT.Copy).then_inc(hi_ready, 1)

            def split_rows(ex, first):
                act.wait_ge(xT_ready, 3 * ex + 3)
                if not first:
                    act.wait_ge(gu_done, M * ex)
                nc.scalar.activation(xx[:, :, 0:C2], xT[:], ACT.Copy).then_inc(xh_ready, 1)
                nc.scalar.activation(xb[:], xT[:], ACT.Copy).then_inc(xb_ready, 1)

            def gated_rows(ex, i):
                if i == 0:
                    act.wait_ge(give_ready, ex + 1)
                g, half = divmod(i, 2)
                act.wait_ge(y_done, 4 * ex + i + 1)
                nc.scalar.activation(yr[:, g, 512 * half:512 * (half + 1)], banks(TURN, CAP)[:, 0:512], ACT.Copy,
                                     scale=gate[:, g:g + 1]).then_inc(yr_ready, 1)

            def body(ex, first, last):
                for m in range(M):
                    n = M * ex + m + 1
                    b = 2 * (m % 2)
                    act.wait_ge(gu_done, n)
                    src = banks(b)[:, 0:1024].rearrange("p (i n) -> p i n", i=2)
                    nc.scalar.activation(low[m % 2][:], src[:, :, C2:2 * C2], ACT.Copy).then_inc(low_ready, 1)
                    then = ahead(ex, m, last)
                    if m == M - 1:
                        act.wait_ge(sum_ready, n)
                        nc.scalar.activation(sil[m % 2][:], gu[m % 2][:, 0], ACT.Silu).then_inc(sil_ready, 1)
                        if not last:
                            split_rows(ex + 1, False)
                    if then:
                        split_high(*then)
                    if m < M - 1:
                        act.wait_ge(sum_ready, n)
                        nc.scalar.activation(sil[m % 2][:], gu[m % 2][:, 0], ACT.Silu).then_inc(sil_ready, 1)
                    if m in OUT_STEPS and not first:
                        gated_rows(ex - 1, OUT_STEPS[m])
                act.wait_ge(d_done, M * ex + M)
                two = banks(4)[:, 0:1024].rearrange("p (b n) -> p b n", b=2)[:, :, 0:PER_BANK * C2]
                nc.scalar.activation(yT[:, 0:6].rearrange("p (b k) n -> p b (k n)", b=2), two, ACT.Copy)
                nc.scalar.activation(yT[:, 6:8], banks(6)[:, 0:2 * C2].rearrange("p (k n) -> p k n", k=2),
                                     ACT.Copy).then_inc(yT_ready, 1)

            split_high(0, 0)
            split_high(0, 1)
            split_rows(0, True)
            per_expert(act, body)
            for i in range(4):
                gated_rows(N_EXP - 1, i)

        @block.vector
        def _(dve):
            step = chained(dve, e["dve_step"])

            def split_low(ex, m):
                j, c = divmod(m, 2)
                dve.wait_ge(hi_ready, M * ex + m + 1)
                nc.vector.tensor_tensor(wlo[m % 2][:], wgu[gu_slot(j)][:, :, :, c * P:(c + 1) * P], whi[m % 2][:].bitcast(F32),
                                        ALU.subtract).then_inc(lo_ready, 1)

            dve.wait_ge(aT_done, 1)
            step(nc.vector.tensor_copy(work[0][:], banks(0, G * N_EXP)[:, PT:PT + T]))
            for r in range(RANKS // 8):
                a, b, at = work[r % 2], work[(r + 1) % 2], slice(8 * r, 8 * r + 8)
                step(nc.vector.max(vals[:, at], a[:]))
                if r + 1 < RANKS // 8:
                    nc.vector.match_replace(b[:], vals[:, at], a[:], -1.0)
                step(nc.vector.max_index(index[:, at], vals[:, at], a[:]))
            nc.vector.tensor_copy(indexf[:], index[:]).then_inc(ranked, 1)
            dve.wait_ge(lists_done, 1)
            lists = banks(2, CAP)
            gates, tokens = (lists[:, a:a + 32].rearrange("p (g n) -> p g n", g=G) for a in (0, 32))
            for g in range(G):
                nc.vector.tensor_scalar(idxT[:, g], tokens[:, g], float(T * g), None, ALU.add).then_inc(lists_ready, 1)
            nc.vector.tensor_copy(gateT[:], gates).then_inc(lists_ready, 1)
            dve.wait_ge(lists_ready, 3)

            def pick(ex):
                nc.vector.tensor_copy(take[:], idxT[:, :, bass.ds(ex, 1)]).then_inc(take_ready, 1)

            def pick_out(ex):
                dve.wait_ge(give_free, ex + 1)
                nc.vector.tensor_copy(give[:], idxT[:, :, bass.ds(ex, 1)])
                nc.vector.tensor_copy(gate[:].unsqueeze(2), gateT[:, :, bass.ds(ex, 1)]).then_inc(give_ready, 1)

            def read_turned(ex, part, ks):
                dve.wait_ge(xT_done, 3 * ex + part + 1)
                if part == 0:
                    dve.wait_ge(xb_ready, ex) if not (isinstance(ex, int) and ex == 0) else None
                src = banks(TURN)[:, 0:len(ks) * C2].rearrange("p (k n) -> p k n", n=C2)
                nc.vector.tensor_copy(xT[:, ks[0]:ks[-1] + 1], src).then_inc(xT_ready, 1)

            def split_rows(ex):
                dve.wait_ge(xh_ready, ex + 1)
                nc.vector.tensor_tensor(xx[:, :, C2:2 * C2], xT[:], xx[:, :, 0:C2].bitcast(F32), ALU.subtract).then_inc(xl_ready, 1)

            def body(ex, first, last):
                for m in range(M):
                    n = M * ex + m + 1
                    b = 2 * (m % 2)
                    dve.wait_ge(low_ready, n)
                    src = banks(b)[:, 0:1024].rearrange("p (i n) -> p i n", i=2)
                    nc.vector.tensor_tensor(gu[m % 2][:], src[:, :, 0:C2], low[m % 2][:], ALU.add).then_inc(sum_ready, 1)
                    dve.wait_ge(sil_ready, n)
                    nc.vector.tensor_tensor(hid[m % 2][:], sil[m % 2][:], gu[m % 2][:, 1], ALU.mult).then_inc(hid_ready, 1)
                    if m == M - 1 and not last:
                        split_rows(ex + 1)
                    then = ahead(ex, m, last)
                    if then:
                        split_low(*then)
                    if m == 0:
                        if not last:
                            pick(ex + 1)
                        if not first:
                            pick_out(ex - 1)
                    if m in ROW_STEPS and not last:
                        read_turned(ex + 1, m - min(ROW_STEPS), ROW_STEPS[m])

            pick(0)
            split_low(0, 0)
            split_low(0, 1)
            for part, ks in enumerate(ROW_STEPS.values()):
                read_turned(0, part, ks)
            split_rows(0)
            per_expert(dve, body)
            pick_out(N_EXP - 1)


_INS = ["x_prompt", "x_sample", "meta", "g_mix", "w_in", "b_gates", "conv_w", "g_q", "g_k", "lam_q1", "lam_k1",
        "lam_q2", "lam_k2", "g_da_out", "g_ml_out", "w_out", "g_ffn", "w_router", "w_gate", "w_up", "w_down",
        "rope_cos", "rope_sin"]


def kernel(**inputs):
    import numpy as np
    import concourse.bacc as bacc
    from concourse.bass_utils import run_bass_kernel_spmd

    inputs["rope_cos"], inputs["rope_sin"] = rope_tables(np)
    nc = bacc.Bacc("TRN2", target_bir_lowering=False, num_devices=1)
    arrays, a = {}, {}
    for name in _INS:
        arrays[f"in_{name}"] = np.ascontiguousarray(inputs[name])
        a[name] = nc.dram_tensor(f"in_{name}", arrays[f"in_{name}"].shape, F32, kind="ExternalInput").ap()
    out = nc.dram_tensor("out_rows", (G * T, D), F32, kind="ExternalOutput").ap()
    xn_rows = nc.dram_tensor("xn_rows", (G * T, D), F32, kind="Internal").ap()
    zv_rows = nc.dram_tensor("zv_rows", (3, TZ, HALF), F32, kind="Internal").ap()
    build(nc, a["meta"], a["x_prompt"], a["x_sample"], a["g_mix"], a["w_in"], a["b_gates"], a["conv_w"], a["g_q"],
          a["g_k"], [a["lam_q1"], a["lam_k1"], a["lam_q2"], a["lam_k2"]], a["g_da_out"], a["g_ml_out"], a["w_out"],
          a["g_ffn"], a["w_router"], a["w_gate"], a["w_up"], a["w_down"], a["rope_cos"], a["rope_sin"], out, xn_rows, zv_rows)
    rows = run_bass_kernel_spmd(nc, [arrays], core_ids=[0]).results[0]["out_rows"]
    rows = rows.reshape(G, 1, T, D)[:, :, N_META:]
    return rows[0], rows[1]
```
